# Optimizing a Trainium2 kernel written in Bass

```python
import jax
import jax.numpy as jnp
from jax import lax
import numpy as np

D_MODEL = 1024
BATCH = 1
SEQ = 512
DEPTH = 2
DEC_BATCH = 1
DEC_SEQ = 32
PAST_LEN = 128

CHUNK = 64
Q_BLOCK = 128
HEAD_DIM = 64
ROPE_THETA = 10000.0
NORM_EPS = 1e-6
A_HEADS = 6
IDX_HEADS = 4
IDX_DIM = 64
TOPK_MAX = 256
B_HEADS = 6
FORGET_BIAS_INIT = 3.0
POOL_WINDOWS = (2, 4, 8, 16)
POOL_GROUPS = 4
POOL_GROUP_DIM = 64
POOL_WIDTH = POOL_GROUPS * POOL_GROUP_DIM
POOL_HIST = max(POOL_WINDOWS) - 1
D_FF = 2816
N_EXPERTS = 8
TOP_K_EXPERTS = 2
D_FF_EXPERT = 1408
N_DENSE = (DEPTH + 1) // 2
N_MOE = DEPTH // 2
IN_SIZES = (A_HEADS * HEAD_DIM, HEAD_DIM, HEAD_DIM, IDX_HEADS * IDX_DIM, IDX_HEADS, IDX_DIM,
            B_HEADS * HEAD_DIM, B_HEADS * HEAD_DIM, B_HEADS * HEAD_DIM, B_HEADS, POOL_WIDTH, 3 * D_MODEL)
IN_SPLITS = tuple(int(v) for v in np.cumsum(IN_SIZES)[:-1])
N_IN = int(sum(IN_SIZES))

kernel_name = 'hybrid_streaming_encoder_step'

def rms_norm(x, g):
    xf = x.astype(jnp.float32)
    y = xf * lax.rsqrt(jnp.mean(xf * xf, axis=-1, keepdims=True) + NORM_EPS)
    return (y * g.astype(jnp.float32)).astype(x.dtype)

def rope(x, pos):
    half = x.shape[-1] // 2
    inv = ROPE_THETA ** (-jnp.arange(half, dtype=jnp.float32) / half)
    ang = pos.astype(jnp.float32)[:, None] * inv[None, :]
    cos = jnp.cos(ang)[None, :, None, :]
    sin = jnp.sin(ang)[None, :, None, :]
    x1 = x[..., :half].astype(jnp.float32)
    x2 = x[..., half:].astype(jnp.float32)
    return jnp.concatenate([x1 * cos - x2 * sin, x2 * cos + x1 * sin], axis=-1).astype(x.dtype)

def sweep_queries(fn, qs, pos_q):
    n_q = pos_q.shape[0]
    if n_q <= Q_BLOCK or n_q % Q_BLOCK:
        return fn(qs, pos_q)
    nb = n_q // Q_BLOCK
    qs_b = tuple(jnp.moveaxis(a.reshape(a.shape[0], nb, Q_BLOCK, *a.shape[2:]), 1, 0) for a in qs)
    out = lax.map(lambda args: fn(args[0], args[1]), (qs_b, pos_q.reshape(nb, Q_BLOCK)))
    out = jnp.moveaxis(out, 0, 1)
    return out.reshape(out.shape[0], n_q, *out.shape[3:])

def dsa_attention(q, qi, wi, pos_q, k, v, ki, pos_k, n_sel):
    scale = HEAD_DIM ** -0.5
    ki32 = ki.astype(jnp.float32)

    def block(qs, pq):
        qb, qib, wib = qs
        rel = jax.nn.relu(jnp.einsum('bqhd,bsd->bqhs', qib.astype(jnp.float32), ki32))
        score = jnp.einsum('bqh,bqhs->bqs', wib.astype(jnp.float32), rel)
        admissible = (pos_k[None, :] // CHUNK) <= (pq[:, None] // CHUNK)
        score = jnp.where(admissible[None], score, -jnp.inf)
        top_val, top_idx = lax.top_k(score, n_sel)
        kg = jax.vmap(lambda a, i: a[i])(k, top_idx)
        vg = jax.vmap(lambda a, i: a[i])(v, top_idx)
        logits = jnp.einsum('bqhd,bqkd->bqhk', qb, kg).astype(jnp.float32) * scale
        logits = jnp.where(jnp.isfinite(top_val)[:, :, None, :], logits, -jnp.inf)
        p = jax.nn.softmax(logits, axis=-1)
        return jnp.einsum('bqhk,bqkd->bqhd', p.astype(v.dtype), vg)

    return sweep_queries(block, (q, qi, wi), pos_q)

def fox_attention(q, cum_q, pos_q, k, v, cum_k, pos_k):
    scale = HEAD_DIM ** -0.5
    cum_k_t = jnp.transpose(cum_k, (0, 2, 1))

    def block(qs, pq):
        qb, cqb = qs
        logits = jnp.einsum('bqhd,bkhd->bhqk', qb, k).astype(jnp.float32) * scale
        decay = jnp.transpose(cqb, (0, 2, 1))[..., :, None] - cum_k_t[..., None, :]
        causal = pos_k[None, :] <= pq[:, None]
        logits = jnp.where(causal[None, None], logits + decay, -jnp.inf)
        p = jax.nn.softmax(logits, axis=-1)
        return jnp.einsum('bhqk,bkhd->bqhd', p.astype(v.dtype), v)

    return sweep_queries(block, (q, cum_q), pos_q)

def pool_mixer(u, hist, start_pos, pool_w, pool_scale):
    bsz, t_new, _ = u.shape
    full = jnp.concatenate([hist, u], axis=1)
    cs = jnp.pad(jnp.cumsum(full.astype(jnp.float32), axis=1), ((0, 0), (1, 0), (0, 0)))
    pos = start_pos + jnp.arange(t_new)
    end = POOL_HIST + 1
    outs = []
    for g, w in enumerate(POOL_WINDOWS):
        sl = slice(g * POOL_GROUP_DIM, (g + 1) * POOL_GROUP_DIM)
        s = cs[:, end:end + t_new, sl] - cs[:, end - w:end - w + t_new, sl]
        cnt = jnp.minimum(pos + 1, w).astype(jnp.float32)[None, :, None]
        outs.append(s / cnt)
    pooled = jnp.concatenate(outs, axis=-1)
    z = (pooled - u.astype(jnp.float32)).astype(u.dtype)
    z = z.reshape(bsz, t_new, POOL_GROUPS, POOL_GROUP_DIM)
    z = jnp.einsum('btgc,gcd->btgd', z, pool_w).reshape(bsz, t_new, POOL_WIDTH)
    return z * pool_scale, full[:, -POOL_HIST:]

def swiglu(h, wg, wu, wd):
    return (jax.nn.silu(h @ wg) * (h @ wu)) @ wd

def moe_ffn(h, router_w, router_b, wg, wu, wd):
    bsz, t_new, d = h.shape
    tok = h.reshape(-1, d)
    logits = (tok @ router_w).astype(jnp.float32) + router_b.astype(jnp.float32)
    top_val, top_idx = lax.top_k(logits, TOP_K_EXPERTS)
    wts = jax.nn.softmax(top_val, axis=-1)
    gate = jnp.sum(jax.nn.one_hot(top_idx, N_EXPERTS, dtype=jnp.float32) * wts[..., None], axis=1)
    out = jnp.zeros_like(tok)
    for e in range(N_EXPERTS):
        out = out + gate[:, e:e + 1].astype(tok.dtype) * swiglu(tok, wg[e], wu[e], wd[e])
    return out.reshape(bsz, t_new, d)

def trunk_layer(x, c, past, lw, layer):
    f32 = jnp.float32
    bsz, t_new, _ = x.shape
    mod = jnp.einsum('bd,de->be', jax.nn.silu(c), lw['ada_w']) + lw['ada_b']
    sh1, sc1, g1, sh2, sc2, g2 = [m[:, None, :] for m in jnp.split(mod, 6, axis=-1)]
    h = rms_norm(x, lw['norm_mix_g']) * (1 + sc1) + sh1
    z = jnp.einsum('btd,dn->btn', h, lw['w_in'])
    aq, ak, av, iq, iw, ik, bq, bk, bv, bf, cu, gl = jnp.split(z, IN_SPLITS, axis=-1)
    n_past = 0 if past is None else past[0].shape[1]
    pos = n_past + jnp.arange(t_new)
    aq = rope(aq.reshape(bsz, t_new, A_HEADS, HEAD_DIM), pos)
    ak = rope(ak[:, :, None, :], pos)[:, :, 0]
    iq = rope(iq.reshape(bsz, t_new, IDX_HEADS, IDX_DIM), pos)
    ik = rope(ik[:, :, None, :], pos)[:, :, 0]
    new_a = jnp.stack([ak, av, ik], axis=2)
    bq = bq.reshape(bsz, t_new, B_HEADS, HEAD_DIM)
    new_b = jnp.stack([bk.reshape(bsz, t_new, B_HEADS, HEAD_DIM),
                       bv.reshape(bsz, t_new, B_HEADS, HEAD_DIM)], axis=2)
    new_logf = jax.nn.log_sigmoid(bf.astype(f32) + lw['b_forget'].astype(f32))
    if past is None:
        a_all, b_all, logf_all = new_a, new_b, new_logf
        hist = jnp.zeros((bsz, POOL_HIST, POOL_WIDTH), cu.dtype)
    else:
        pa, pb, pl, pc = past
        a_all = jnp.concatenate([pa.astype(new_a.dtype), new_a], axis=1)
        b_all = jnp.concatenate([pb.astype(new_b.dtype), new_b], axis=1)
        logf_all = jnp.concatenate([pl.astype(f32), new_logf], axis=1)
        hist = pc.astype(cu.dtype)
    n_keys = a_all.shape[1]
    pos_k = jnp.arange(n_keys)
    n_sel = min(TOPK_MAX, n_keys // 4)
    oa = dsa_attention(aq, iq, iw, pos, a_all[:, :, 0], a_all[:, :, 1], a_all[:, :, 2], pos_k, n_sel)
    cum_logf = jnp.cumsum(logf_all, axis=1)
    ob = fox_attention(bq, cum_logf[:, n_past:], pos, b_all[:, :, 0], b_all[:, :, 1], cum_logf, pos_k)
    oc, new_pool = pool_mixer(cu, hist, n_past, lw['pool_w'], lw['pool_scale'])
    gates = jax.nn.sigmoid(gl.astype(f32)).astype(x.dtype).reshape(bsz, t_new, 3, D_MODEL)
    merged = (gates[:, :, 0] * (oa.reshape(bsz, t_new, A_HEADS * HEAD_DIM) @ lw['w_br_a'])
              + gates[:, :, 1] * (ob.reshape(bsz, t_new, B_HEADS * HEAD_DIM) @ lw['w_br_b'])
              + gates[:, :, 2] * (oc @ lw['w_br_c']))
    x = x + g1 * (merged @ lw['w_out'])
    h = rms_norm(x, lw['norm_ffn_g']) * (1 + sc2) + sh2
    if layer % 2 == 0:
        f = swiglu(h, lw['ffn_w_gate'], lw['ffn_w_up'], lw['ffn_w_down'])
    else:
        f = moe_ffn(h, lw['moe_router_w'], lw['moe_router_b'], lw['moe_w_gate'], lw['moe_w_up'], lw['moe_w_down'])
    x = x + g2 * f
    return x, (new_a, new_b, new_logf, new_pool)

def setup_inputs(seed: int = 0) -> dict:
    key = jax.random.key(seed)
    ks = jax.random.split(key, 64)
    D = D_MODEL

    def nrm(i, shape, scale):
        return scale * jax.random.normal(ks[i], shape, jnp.float32)

    return {
        'x_prompt': nrm(0, (BATCH, SEQ, D), 1.0),
        'x_sample': nrm(1, (DEC_BATCH, DEC_SEQ, D), 1.0),
        'cache_a_kvi': nrm(2, (DEPTH, DEC_BATCH, PAST_LEN, 3, HEAD_DIM), 1.0),
        'cache_b_kv': nrm(3, (DEPTH, DEC_BATCH, PAST_LEN, 2, B_HEADS, HEAD_DIM), 1.0),
        'cache_b_logf': jax.nn.log_sigmoid(FORGET_BIAS_INIT + nrm(4, (DEPTH, DEC_BATCH, PAST_LEN, B_HEADS), 1.0)),
        'state_c_pool': nrm(5, (DEPTH, DEC_BATCH, POOL_HIST, POOL_WIDTH), 1.0),
        'c_prompt': nrm(6, (BATCH, D), 1.0),
        'c_sample': nrm(7, (DEC_BATCH, D), 1.0),
        'ada_w': nrm(8, (DEPTH, D, 6 * D), 0.3 * D ** -0.5),
        'ada_b': nrm(9, (DEPTH, 6 * D), 0.02),
        'norm_mix_g': 1.0 + nrm(10, (DEPTH, D), 0.05),
        'w_in': nrm(11, (DEPTH, D, N_IN), D ** -0.5),
        'b_forget': FORGET_BIAS_INIT + nrm(12, (DEPTH, B_HEADS), 0.1),
        'pool_w': nrm(13, (DEPTH, POOL_GROUPS, POOL_GROUP_DIM, POOL_GROUP_DIM), POOL_GROUP_DIM ** -0.5),
        'pool_scale': 1.0 + nrm(14, (DEPTH, POOL_WIDTH), 0.1),
        'w_br_a': nrm(15, (DEPTH, A_HEADS * HEAD_DIM, D), (A_HEADS * HEAD_DIM) ** -0.5),
        'w_br_b': nrm(16, (DEPTH, B_HEADS * HEAD_DIM, D), (B_HEADS * HEAD_DIM) ** -0.5),
        'w_br_c': nrm(17, (DEPTH, POOL_WIDTH, D), POOL_WIDTH ** -0.5),
        'w_out': nrm(18, (DEPTH, D, D), D ** -0.5),
        'norm_ffn_g': 1.0 + nrm(19, (DEPTH, D), 0.05),
        'ffn_w_gate': nrm(20, (N_DENSE, D, D_FF), D ** -0.5),
        'ffn_w_up': nrm(21, (N_DENSE, D, D_FF), D ** -0.5),
        'ffn_w_down': nrm(22, (N_DENSE, D_FF, D), D_FF ** -0.5),
        'moe_router_w': nrm(23, (N_MOE, D, N_EXPERTS), D ** -0.5),
        'moe_router_b': nrm(24, (N_MOE, N_EXPERTS), 0.01),
        'moe_w_gate': nrm(25, (N_MOE, N_EXPERTS, D, D_FF_EXPERT), D ** -0.5),
        'moe_w_up': nrm(26, (N_MOE, N_EXPERTS, D, D_FF_EXPERT), D ** -0.5),
        'moe_w_down': nrm(27, (N_MOE, N_EXPERTS, D_FF_EXPERT, D), D_FF_EXPERT ** -0.5),
        'final_norm_g': 1.0 + nrm(28, (D,), 0.05),
    }

def reference(x_prompt, x_sample, cache_a_kvi, cache_b_kv, cache_b_logf, state_c_pool, c_prompt, c_sample,
              ada_w, ada_b, norm_mix_g, w_in, b_forget, pool_w, pool_scale, w_br_a, w_br_b, w_br_c, w_out,
              norm_ffn_g, ffn_w_gate, ffn_w_up, ffn_w_down, moe_router_w, moe_router_b, moe_w_gate,
              moe_w_up, moe_w_down, final_norm_g):
    xp, xs = x_prompt, x_sample
    pa, pb, pl, pc = [], [], [], []
    sa, sb, sl, sc = [], [], [], []
    for layer in range(DEPTH):
        lw = dict(ada_w=ada_w[layer], ada_b=ada_b[layer], norm_mix_g=norm_mix_g[layer], w_in=w_in[layer],
                  b_forget=b_forget[layer], pool_w=pool_w[layer], pool_scale=pool_scale[layer],
                  w_br_a=w_br_a[layer], w_br_b=w_br_b[layer], w_br_c=w_br_c[layer], w_out=w_out[layer],
                  norm_ffn_g=norm_ffn_g[layer])
        j = layer // 2
        if layer % 2 == 0:
            lw.update(ffn_w_gate=ffn_w_gate[j], ffn_w_up=ffn_w_up[j], ffn_w_down=ffn_w_down[j])
        else:
            lw.update(moe_router_w=moe_router_w[j], moe_router_b=moe_router_b[j], moe_w_gate=moe_w_gate[j],
                      moe_w_up=moe_w_up[j], moe_w_down=moe_w_down[j])
        xp, (na, nb, nl, npool) = trunk_layer(xp, c_prompt, None, lw, layer)
        pa.append(na); pb.append(nb); pl.append(nl); pc.append(npool)
        past = (cache_a_kvi[layer], cache_b_kv[layer], cache_b_logf[layer], state_c_pool[layer])
        xs, (na, nb, nl, npool) = trunk_layer(xs, c_sample, past, lw, layer)
        sa.append(na); sb.append(nb); sl.append(nl); sc.append(npool)
    y_prompt = rms_norm(xp, final_norm_g)
    y_sample = rms_norm(xs, final_norm_g)
    return (y_prompt, y_sample,
            jnp.stack(pa), jnp.stack(pb), jnp.stack(pl), jnp.stack(pc),
            jnp.stack(sa), jnp.stack(sb), jnp.stack(sl), jnp.stack(sc))


_drawn_inputs = setup_inputs


def setup_inputs(seed=0):
    import zlib

    import numpy as np

    out = dict(_drawn_inputs(seed))
    spreads = {}
    factors = {'cache_b_kv': 3.071,
     'cache_b_logf': 8.0,
     'state_c_pool': 3.723,
     'pool_scale': 4.32,
     'norm_ffn_g': 3.387,
     'moe_router_b': 8.0}
    for name, (base, spread) in spreads.items():
        noise = np.random.default_rng([zlib.crc32(name.encode()), seed]).standard_normal(out[name].shape)
        drawn = base * np.exp(spread * noise) if base else spread * noise
        out[name] = jnp.asarray(drawn.astype(out[name].dtype))
    for name, factor in factors.items():
        out[name] = (out[name] * factor).astype(out[name].dtype)
    return out
```

```python
import numpy as np
import concourse.bass as bass
from concourse import mybir
from concourse.alu_op_type import AluOpType as ALU
from contextlib import ExitStack

FP = mybir.dt.float32
BF = mybir.dt.bfloat16
FR = mybir.dt.float32r
ACT = mybir.ActivationFunctionType
AX = mybir.AxisListType
ds = bass.ds

P = 128
D = 1024
KD = D // P
SEQ, DEC, PAST = 512, 32, 128
NTOK = SEQ + DEC
HALF = NTOK // 2
DEPTH = 2
TILES = SEQ // P + 1
SAMPLE = TILES - 1
HD = 64
AH = BH = 6
IH = 4
CHUNK = 64
K_PROMPT = min(256, SEQ // 4)
K_SAMPLE = min(256, (DEC + PAST) // 4)
NEXP = 8
FEXP = 1408
FLO = 6
FB = FEXP // P
EXPERTS = (2, NEXP)
NORM_EPS = 1e-6
NEG = -1e30
LOWEST = -3e38

AQ, AK, AV, IQ = 0, 384, 448, 512
IW, IK = 768, 772
BQ, BK, BV = 836, 1220, 1604
BF_, CU, GL = 1988, 1994, 2250
ZW = GL
ZB = 250
ZITER, ZBODY = 3, 3
N_IN = GL + 3 * D
PW = 256
HIST = 15

NSLOT = 4
SLOT = 2048

V_ADAB, V_NMIX, V_NFFN, V_PSC, V_FIN, V_C, V_ROWS = 0, 48, 56, 64, 66, 74, 90
M_SH1, M_SC1, M_G1, M_SH2, M_SC2, M_G2 = 0, 8, 16, 24, 32, 40

KW = [128, 256, 384, 512, PAST + DEC]
ROWS = [P, P, P, P, DEC]
MOFF = [0, 128, 384, 768, 1280]
MTOT = 1440
KEYS = SEQ + PAST + DEC
KCOL = [0, 0, 0, 0, SEQ]


def tok(t):
    return slice(t * P, t * P + ROWS[t])


def keycol(t):
    return slice(t * P, (t + 1) * P) if t < SAMPLE else slice(SEQ + PAST, KEYS)


class Ring:

    def __init__(self):
        self.n = {"begun": 0, "split": 0}
        self.fills, self.last, self.plan = [0] * NSLOT, [None] * NSLOT, {}

    def phase(self, name, iters, dmas, kind="begun"):
        n, per, after, own, before = len(dmas), [0] * NSLOT, [], [], []
        for j, m in enumerate(dmas):
            per[j % NSLOT] += m
            after.append(per[j % NSLOT])
        for j in range(min(NSLOT, n)):
            mine = [i for i in range(n) if i % NSLOT == j][-1]
            own.append(n - mine if iters > 1 else None)
            before.append(self.last[j])
        self.plan[name] = (kind, self.n[kind], list(self.fills), per, after, n, own, before)
        for s in range(NSLOT):
            self.fills[s] += iters * per[s]
        for j in range(n):
            self.last[j % NSLOT] = (kind, self.n[kind] + (iters - 1) * n + j)
        self.n[kind] += iters * n

    def ghost(self):
        self.n["begun"] += 1

    def full(self, name, it, j):
        _, _, fills, per, after, _, _, _ = self.plan[name]
        return (it * per[j % NSLOT] + (fills[j % NSLOT] + after[j])) * 16

    def value(self, kind, index):
        return index + 2 if kind == "begun" else index * 2 + 2

    def free(self, name, it, j):
        kind, first, _, _, _, n, own, before = self.plan[name]
        if j >= NSLOT:
            return [(kind, self.value(kind, it * n + (first + j - NSLOT)))]
        out = []
        if own[j] is not None and not (isinstance(it, int) and it == 0):
            out.append((kind, self.value(kind, it * n + (first - own[j]))))
        if before[j] is not None:
            out.append((before[j][0], self.value(*before[j])))
        return out


class Chain:

    def __init__(self, eng, sem):
        self.eng, self.sem, self.base, self.k = eng, sem, 0, 0

    def link(self, ins):
        self.k += 1
        ins.then_inc(self.sem, 1)
        self.eng.wait_ge(self.sem, self.base + self.k)

    def enter(self, it, start, per):
        self.total = self.base + self.k
        self.base, self.k, self.per = (it - start) * per + self.total, 0, per

    def leave(self, iters):
        assert self.k == self.per, (self.k, self.per)
        self.base, self.k = self.total + iters * self.per, 0


def encoder_step(nc, t_in, t_out):
    ring = Ring()
    for L in range(DEPTH):
        ring.phase(("ada", L), 6, [1] * 4)
        ring.phase(("z", L), ZITER, [1] * ZBODY)
        ring.phase(("gates", L), 3, [1] * 4)
        ring.phase(("branch", L), 2, [3] * 2)
        ring.phase(("out", L), 2, [1] * 2)
        ring.ghost()
        ring.phase(("ffn", L), EXPERTS[L], [2] * FB + [1] * KD, "split")

    ctx = ExitStack()
    with ctx:
        start = nc.sbuf_base
        start += -start % 64
        size = nc.sbuf_usable_end - start - 64
        ctx.enter_context(nc.sbuf_tensor("arena", [P, size // 4], FP))
        place = {"next": start}

        def sb(name, shape, dt=FP, over=None):
            n = int(np.prod(shape[1:])) * (2 if dt == BF else 4)
            n += -n % 32
            if over is None:
                at = place["next"]
                place["next"] += n
                assert place["next"] <= start + size, name
            else:
                at, room = place[over]
                assert n <= room, name
            place[name] = (at, n)
            return nc.alloc_sbuf_tensor_at(name, shape, dt, offset=at)

        def sem(name):
            return ctx.enter_context(nc.semaphore(name))

        xT = sb("xT", [P, KD, NTOK])
        hT = sb("hT", [P, KD, NTOK])
        z = sb("z", [P, TILES, ZW])
        gT = sb("gT", [P, 3 * KD, NTOK])
        slots = sb("slots", [P, NSLOT, SLOT])
        oT = sb("oT", [P, KD, NTOK])
        qk = sb("qk", [P, 1760])
        pp = sb("pp", [P, 2, 2, 512])
        amask = sb("amask", [P, MTOT], BF)
        cmask = sb("cmask", [P, P], BF)
        ident = sb("ident", [P, P])
        identb = sb("identb", [P, P], BF)
        ones = sb("ones", [P, P])
        tri = sb("tri", [P, P])
        cs = sb("cs", [P, TILES, 2, 32])
        past = sb("past", [P, 966])
        vecT = sb("vecT", [P, DEPTH, V_ROWS])
        csil = sb("csil", [P, 2, KD])
        mod = sb("mod", [P, 48, 2])
        scl = sb("scl", [P, 2, KD, 2])
        negcum = sb("negcum", [BH, KEYS])
        logf = sb("logf", [P, TILES, BH])
        lft = sb("lft", [P, 3, TILES, BH])
        bfb = sb("bfb", [P, DEPTH, BH])
        rb = sb("rb", [P, NEXP])
        rw = sb("rw", [P, KD, NEXP])
        m8 = sb("m8", [P, 8])
        stat = sb("stat", [P, 4])
        nmax = sb("nmax", [P, 12])
        rsum = sb("rsum", [P, 2, AH])
        rinv = sb("rinv", [P, 2, AH])

        hR = sb("hR", [P, 2, KD, NTOK], FR, over="z")
        hidR = sb("hidR", [P, 2, FB, NTOK], FR, over="gT")
        wR = sb("wR", [P, 2, 2, KD * P], FR, over="hT")

        xin = z[:, :, 0:D]
        vrow = gT[:, 0, 0:2 * P].rearrange("p (l n) -> p l n", l=2)
        oTf = oT[:, :, :].rearrange("p k n -> p (k n)")
        score = oTf[:, 0:1312]
        SOFF = [None, 0, 256, 640, 1152]
        rel = [oTf[:, 1312 + 512 * i:1824 + 512 * i] for i in range(2)]
        work = oTf[:, 2336:2848]
        isgt, iseq = rel
        rank = work
        iqT = qk[:, 0:2 * NTOK].rearrange("p (b n) -> p b n", b=2)
        ikT = qk[:, 2 * NTOK:2 * NTOK + KEYS]
        aqT = qk[:, 0:3 * NTOK].rearrange("p (b n) -> p b n", b=3)
        pooled = qk[0:HD, 0:512]
        poolw = qk[0:HD, 512:1024].rearrange("p (g d) -> p g d", g=4)
        hist = qk[0:HIST, 1024:1280]
        hTf = hT[:, :, :].rearrange("p k n -> p (k n)")
        bqT = hTf[:, 0:3 * NTOK].rearrange("p (b n) -> p b n", b=3)
        bkT = hTf[:, 3 * NTOK:3 * NTOK + 3 * KEYS].rearrange("p (b n) -> p b n", b=3)
        akT = hTf[:, 3 * NTOK + 3 * KEYS:3 * NTOK + 4 * KEYS]
        probs = [pp[:, 0, i, :] for i in range(2)]
        probsT = [pp[:, 1, i, :] for i in range(2)]
        poolm = pp[:, :, :, :].rearrange("p a b n -> p (a b) n")
        zf = z[:, :, :].rearrange("p t n -> p (t n)")
        sqs = [zf[:, 0:KD * NTOK].rearrange("p (k n) -> p k n", k=KD), hT]
        zq = 2 * KD * NTOK
        sg = [zf[:, zq + i * NTOK:zq + (i + 1) * NTOK] for i in range(2)]
        hidf = zf[:, zq + 2 * NTOK:zq + 3 * NTOK]
        gateT = zf[0:NEXP, zq + 3 * NTOK:zq + 4 * NTOK]
        r0 = zq + 4 * NTOK
        rt = [zf[:, r0 + 40 * i:r0 + 40 * (i + 1)].rearrange("p (t e) -> p t e", t=TILES) for i in range(8)]
        gbc = oT

        ps = ctx.enter_context(nc.psum_tensor("ps", [P, 8, 512], FP))

        def pair(i):
            return ps[:, 2 * i:2 * i + 2, 0:HALF]

        def halves(ap):
            return ap.rearrange("p (a n) -> p a n", a=2)

        slot_full = [sem(f"slot_full{s}") for s in range(NSLOT)]
        block_begun = sem("block_begun")
        w_high, w_split = sem("w_high"), sem("w_split")
        unit_done = [sem("unit_done0"), sem("unit_done1")]
        h_split = sem("h_split")
        ada_done = sem("ada_done")
        x_loaded = sem("x_loaded")
        consts_loaded = sem("consts_loaded")
        vrow_loaded = sem("vrow_loaded")
        memsets = sem("memsets")
        identb_ready = sem("identb_ready")
        xt_ready, xt_evac = sem("xt_ready"), sem("xt_evac")
        vt_ready, vt_evac = sem("vt_ready"), sem("vt_evac")
        csil_ready = sem("csil_ready")
        mod_ready = sem("mod_ready")
        sq_ready, ms_ready, v_ready, root_ready = sem("sq_ready"), sem("ms_ready"), sem("v_ready"), sem("root_ready")
        normed, h_ready = sem("normed"), sem("h_ready")
        x_upd = sem("x_upd")
        z_ready, z_evac = sem("z_ready"), sem("z_evac")
        past_loaded = sem("past_loaded")
        pool_mats_loaded = sem("pool_mats_loaded")
        poolw_zero, poolw_loaded = sem("poolw_zero"), sem("poolw_loaded")
        rope_done = sem("rope_done")
        lf_abs, lf_ln, logf_ready = sem("lf_abs"), sem("lf_ln"), sem("logf_ready")
        ti_ready, ti_evac = sem("ti_ready"), sem("ti_evac")
        is_ready, is_relu, is_acc = sem("is_ready"), sem("is_relu"), sem("is_acc")
        mask_ready = sem("mask_ready")
        g_ready, g_evac = sem("g_ready"), sem("g_evac")
        cum_ready, cum_evac = sem("cum_ready"), sem("cum_evac")
        pm_ready, pm_evac, po_ready, po_evac = sem("pm_ready"), sem("pm_evac"), sem("po_ready"), sem("po_evac")
        at_ready, at_evac_act, at_evac_dve = sem("at_ready"), sem("at_evac_act"), sem("at_evac_dve")
        s_ready, mx_ready, p_ready = sem("s_ready"), sem("mx_ready"), sem("p_ready")
        pt_ready, pt_evac, pv_done = sem("pt_ready"), sem("pt_evac"), sem("pv_done")
        o_evac, ot_ready, ot_evac = sem("o_evac"), sem("ot_ready"), sem("ot_evac")
        b_ready, b_evac, m_ready = sem("b_ready"), sem("b_evac"), sem("m_ready")
        r_ready = sem("r_ready")
        sg_ready, sgg_ready, hid_ready = sem("sg_ready"), sem("sgg_ready"), sem("hid_ready")
        rl_ready, gate_ready, gt_ready, gt_evac, gb_ready, gb_evac = (sem("rl_ready"), sem("gate_ready"), sem("gt_ready"),
                                                                      sem("gt_evac"), sem("gb_ready"), sem("gb_evac"))
        rexp_in, rexp_out = sem("rexp_in"), sem("rexp_out")
        y_ready, y_evac = sem("y_ready"), sem("y_evac")
        outs_done, y_sent = sem("outs_done"), sem("y_sent")
        act_chain, dve_chain = sem("act_chain"), sem("dve_chain")

        NZ = ZITER * ZBODY * TILES
        NATT = TILES * 2 * AH
        NTM = TILES * 2

        def xu(L, stage):
            base = sum(KD * (1 + EXPERTS[l]) for l in range(L))
            return base + {"start": 0, "out": KD, "ffn": KD * (1 + EXPERTS[L])}[stage]

        fexp_base = [0, EXPERTS[0]]

        items = [(t, m, h) for t in (SAMPLE, 0, 1, 2, 3) for m in range(2) for h in range(AH)]

        def key_blocks(t):
            if t == SAMPLE:
                return [(0, PAST, "past"), (PAST, DEC, SAMPLE)]
            return [(s * P, P, s) for s in range(t + 1)]

        at_groups = [("past", None)] + [(kind, t) for t in range(TILES) for kind in ("a", "bq", "bk")]
        at_on_act = [kind in ("a", "bk") for kind, _ in at_groups]
        N_AT = len(at_groups)
        N_AT_ACT = sum(at_on_act)
        N_AT_DVE = N_AT - N_AT_ACT

        block = ctx.enter_context(nc.Block())

        @block.sync
        def _(sp):
            sp.dma_start(xin[:, 0:SAMPLE, :], t_in["x_prompt"][0].rearrange("(t p) d -> p t d", p=P)).then_inc(x_loaded, 16)
            sp.dma_start(xin[0:DEC, SAMPLE, :], t_in["x_sample"][0]).then_inc(x_loaded, 16)

            def fill(name, it, j, pieces):
                for kind, value in ring.free(name, it, j):
                    sp.wait_ge(block_begun if kind == "begun" else w_split, value)
                for dst, src in pieces:
                    sp.dma_start(dst, src).then_inc(slot_full[j % NSLOT], 16)

            def cols(j, w):
                return slots[:, j % NSLOT, 0:KD * w].rearrange("p (k n) -> p k n", k=KD)

            for L in range(DEPTH):
                ada = t_in["ada_w"][L].rearrange("(k p) n -> p k n", p=P)
                w_in = t_in["w_in"][L].rearrange("(k p) n -> p k n", p=P)
                w_br = [t_in[n][L].rearrange("(k p) n -> p k n", p=P) for n in ("w_br_a", "w_br_b", "w_br_c")]
                w_out = t_in["w_out"][L].rearrange("(k p) n -> p k n", p=P)

                def ada_fill(it):
                    for j in range(4):
                        fill(("ada", L), it, j, [(cols(j, 256), ada[:, :, ds(it * 1024 + j * 256, 256)])])

                if L == 0:
                    ada_fill(0)
                with sp.Fori(1 if L == 0 else 0, 6) as it:
                    if L == 0:
                        for j in range(4):
                            sp.wait_ge(block_begun, it * 4 + (j - 2))
                            sp.dma_start(cols(j, 256), ada[:, :, ds(it * 1024 + j * 256, 256)]).then_inc(slot_full[j], 16)
                    else:
                        ada_fill(it)
                with sp.Fori(0, ZITER) as it:
                    for j in range(ZBODY):
                        fill(("z", L), it, j, [(cols(j, ZB), w_in[:, :, ds(it * (ZBODY * ZB) + j * ZB, ZB)])])
                with sp.Fori(0, 3) as it:
                    for j in range(4):
                        fill(("gates", L), it, j, [(cols(j, 256), w_in[:, :, ds(it * 1024 + (GL + j * 256), 256)])])
                with sp.Fori(0, 2) as it:
                    for j in range(2):
                        dst = cols(j, 256)
                        fill(("branch", L), it, j,
                             [(dst[:, a:b, :], w_br[i][:, :, ds(it * 512 + j * 256, 256)])
                              for i, (a, b) in enumerate(((0, 3), (3, 6), (6, 8)))])
                with sp.Fori(0, 2) as it:
                    for j in range(2):
                        fill(("out", L), it, j, [(cols(j, 256), w_out[:, :, ds(it * 512 + j * 256, 256)])])
                def ffn_fill(it):
                    for j in range(FB + KD):
                        slot = slots[:, j % NSLOT, :]
                        if j < FB:
                            gu = slot.rearrange("p (w k n) -> p w k n", w=2, k=KD)
                            if L == 0:
                                srcs = [t_in[n][0].rearrange("(k p) n -> p k n", p=P)[:, :, ds(it * FEXP + j * P, P)]
                                        for n in ("ffn_w_gate", "ffn_w_up")]
                            else:
                                srcs = [t_in[n][0, ds(it, 1)].rearrange("e (k p) n -> p (e k) n", p=P)[:, :, j * P:(j + 1) * P]
                                        for n in ("moe_w_gate", "moe_w_up")]
                            fill(("ffn", L), it, j, [(gu[:, w], srcs[w]) for w in range(2)])
                        else:
                            d0 = (j - FB) * P
                            dst = slot[:, 0:FB * P].rearrange("p (f n) -> p f n", f=FB)
                            if L == 0:
                                src = t_in["ffn_w_down"][0, ds(it * FEXP, FEXP)].rearrange("(f p) n -> p f n", p=P)
                            else:
                                src = t_in["moe_w_down"][0, ds(it, 1)].rearrange("e (f p) n -> p (e f) n", p=P)
                            fill(("ffn", L), it, j, [(dst, src[:, :, d0:d0 + P])])

                if L == 0:
                    for it in range(EXPERTS[0]):
                        ffn_fill(it)
                else:
                    with sp.Fori(0, EXPERTS[L]) as it:
                        ffn_fill(it)
            sp.wait_ge(y_evac, 2 * TILES)
            sp.dma_start(t_out["y_prompt"][0].rearrange("(t p) d -> p t d", p=P), xin[:, 0:SAMPLE, :]).then_inc(y_sent, 16)
            sp.dma_start(t_out["y_sample"][0], xin[0:DEC, SAMPLE, :]).then_inc(y_sent, 16)
            sp.wait_ge(y_sent, 32)
            sp.wait_ge(outs_done, 160 * DEPTH)

        @block.gpsimd
        def _(pool):
            for L in range(DEPTH):
                for r, n, src in ((V_ADAB, 48, t_in["ada_b"][L]), (V_NMIX, 8, t_in["norm_mix_g"][L]),
                                  (V_NFFN, 8, t_in["norm_ffn_g"][L]), (V_PSC, 2, t_in["pool_scale"][L]),
                                  (V_FIN, 8, t_in["final_norm_g"]), (V_C, 8, t_in["c_prompt"][0]),
                                  (V_C + 8, 8, t_in["c_sample"][0])):
                    pool.dma_start(vrow[r:r + n, L, :], src.rearrange("(r n) -> r n", n=P)).then_inc(vrow_loaded, 16)
            for dst, src in ((ident, "c_ident"), (tri, "c_tri")):
                pool.dma_start(dst[:, :], t_in[src]).then_inc(consts_loaded, 16)
            pool.dma_start(cs[:, :, :, :].rearrange("p t a f -> p (t a f)"), t_in["c_rope"]).then_inc(consts_loaded, 16)
            pool.dma_start(bfb[:, :, :].rearrange("p l h -> p (l h)"),
                           t_in["b_forget"].rearrange("l h -> (l h)").partition_broadcast(P)).then_inc(consts_loaded, 16)
            pool.dma_start(rb[:, :], t_in["moe_router_b"][0].partition_broadcast(P)).then_inc(consts_loaded, 16)
            pool.dma_start(rw[:, :, :], t_in["moe_router_w"][0].rearrange("(k p) e -> p k e", p=P)).then_inc(consts_loaded, 16)
            for L in range(DEPTH):
                if L:
                    pool.wait_ge(ot_evac, L * NTM)
                pool.dma_start(past[:, 0:192], t_in["cache_a_kvi"][L, 0].rearrange("t c d -> t (c d)")).then_inc(past_loaded, 16)
                pool.dma_start(past[:, 192:960], t_in["cache_b_kv"][L, 0].rearrange("t c h d -> t (c h d)")).then_inc(past_loaded, 16)
                pool.dma_start(past[:, 960:966], t_in["cache_b_logf"][L, 0]).then_inc(past_loaded, 16)
                pool.dma_start(poolm, t_in["c_pool"]).then_inc(pool_mats_loaded, 16)
                pool.wait_ge(rope_done, 6 * (L + 1))
                pool.wait_ge(logf_ready, L + 1)
                pool.wait_ge(z_evac, NZ * (L + 1))
                for pre, zz, nt in (("p", z[:, 0:SAMPLE, :], SEQ), ("s", z[0:DEC, SAMPLE:TILES, :], DEC)):
                    p = min(nt, P)

                    def rows(name):
                        a = t_out[name][L, 0]
                        return a

                    kvi = rows("a_kvi_" + pre).rearrange("(t p) c d -> p t (c d)", p=p)
                    pool.dma_start(kvi[:, :, 0:2 * HD], zz[:, :, AK:AK + 2 * HD]).then_inc(outs_done, 16)
                    pool.dma_start(kvi[:, :, 2 * HD:], zz[:, :, IK:IK + HD]).then_inc(outs_done, 16)
                    pool.dma_start(rows("b_kv_" + pre).rearrange("(t p) c h d -> p t (c h d)", p=p),
                                   zz[:, :, BK:BK + 2 * BH * HD]).then_inc(outs_done, 16)
                    lf = logf[:, 0:SAMPLE, :] if nt == SEQ else logf[0:DEC, SAMPLE:TILES, :]
                    pool.dma_start(rows("logf_" + pre).rearrange("(t p) h -> p t h", p=p), lf).then_inc(outs_done, 16)
                    last = nt // P - 1 if nt == SEQ else 0
                    pool.dma_start(rows("pool_" + pre), zz[p - HIST:p, last, CU:CU + PW]).then_inc(outs_done, 16)
                pool.wait_ge(is_ready, 16 * (L + 1))
                pool.memset(qk[0:HD, 512:1024], 0.0).then_inc(poolw_zero, 1)
                pool.dma_start(hist, t_in["state_c_pool"][L, 0]).then_inc(poolw_loaded, 16)
                pool.wait_ge(poolw_zero, L + 1)
                for g in range(4):
                    pool.dma_start(poolw[:, g, (g % 2) * HD:(g % 2 + 1) * HD], t_in["pool_w"][L, g]).then_inc(poolw_loaded, 16)

        @block.tensor
        def _(pe):
            mm = nc.tensor.matmul

            def landed(name, it, j):
                pe.wait_ge(slot_full[j % NSLOT], ring.full(name, it, j))

            pe.wait_ge(consts_loaded, 96)
            pe.wait_ge(x_loaded, 32)
            for t in range(TILES):
                for g in range(2):
                    i = 2 * t + g
                    if i >= 8:
                        pe.wait_ge(xt_evac, i - 7)
                    for q in range(4):
                        last = nc.tensor.transpose(ps[:, i % 8, q * P:q * P + ROWS[t]],
                                                   xin[0:ROWS[t], t, (4 * g + q) * P:(4 * g + q + 1) * P],
                                                   ident[0:ROWS[t], 0:ROWS[t]])
                    last.then_inc(xt_ready, 1)
            pe.wait_ge(vrow_loaded, 16 * 14)
            pe.wait_ge(xt_evac, 10)
            for L in range(DEPTH):
                last = nc.tensor.transpose(ps[:, L, 0:V_ROWS], vrow[0:V_ROWS, L, :], ident[0:V_ROWS, 0:V_ROWS])
            last.then_inc(vt_ready, 1)
            pe.wait_ge(memsets, 1)

            def norm_sums(n, releases=False):
                for k in range(KD):
                    pe.wait_ge(sq_ready, KD * n + k + 1)
                    for h in range(2):
                        last = mm(ps[:, h, 0:HALF], ones[:, :], sqs[n % 2][:, k, h * HALF:(h + 1) * HALF],
                                  start=(k == 0), stop=(k == KD - 1))
                        if releases and k == h == 0:
                            last.then_inc(block_begun, 1)
                last.then_inc(ms_ready, 1)

            def features(out_pair, lhs, rhs, nk, begins=False, each=None):
                for k in range(nk):
                    if each:
                        each(k)
                    for h in range(2):
                        last = mm(ps[:, 2 * out_pair + h, 0:HALF], lhs(k), rhs(k)[:, h * HALF:(h + 1) * HALF],
                                  start=(k == 0), stop=(k == nk - 1))
                        if begins and k == h == 0:
                            last.then_inc(block_begun, 1)
                return last

            for L in range(DEPTH):
                if L == 0:
                    pe.wait_ge(csil_ready, 1)
                else:
                    pe.wait_ge(x_upd, xu(L - 1, "ffn"))
                with pe.Fori(0, 6) as it:
                    for j in range(4):
                        landed(("ada", L), it, j)
                        w = slots[:, j, :].rearrange("p (k n) -> p k n", k=KD)
                        for f in range(2):
                            for k in range(KD):
                                last = mm(ps[:, 7, ds(it * 16 + (j * 4 + f * 2), 2)], w[:, k, f * P:(f + 1) * P],
                                          csil[:, :, k], start=(k == 0), stop=(k == KD - 1))
                                if f == k == 0:
                                    last.then_inc(block_begun, 1)
                        last.then_inc(ada_done, 1)
                norm_sums(2 * L)
                pe.wait_ge(h_ready, KD * (2 * L + 1))
                with pe.Fori(0, ZITER) as it:
                    for j in range(ZBODY):
                        landed(("z", L), it, j)
                        w = slots[:, j, 0:KD * ZB].rearrange("p (k n) -> p k n", k=KD)
                        for t in range(TILES):
                            g = j * TILES + t
                            if g >= TILES - 1:
                                pe.wait_ge(z_evac, it * (ZBODY * TILES) + (NZ * L + g - TILES + 2))
                            for k in range(KD):
                                last = mm(ps[0:ROWS[t], t, 0:ZB], hT[:, k, tok(t)], w[:, k, :],
                                          start=(k == 0), stop=(k == KD - 1))
                                if t == k == 0:
                                    last.then_inc(block_begun, 1)
                            last.then_inc(z_ready, 1)
                    pe.wait_ge(z_evac, it * (ZBODY * TILES) + (NZ * L + ZBODY * TILES - 1))
                pe.wait_ge(z_evac, NZ * (L + 1))
                pe.wait_ge(rope_done, 6 * (L + 1))
                pe.wait_ge(past_loaded, 48 * (L + 1))

                nc.tensor.transpose(ps[0:HD, 5, 0:P], past[:, 128:192], ident[:, :]).then_inc(ti_ready, 1)
                for t in range(TILES):
                    r = ROWS[t]
                    for b in range(2):
                        nc.tensor.transpose(ps[:, t, b * P:b * P + r], z[0:r, t, IQ + b * P:IQ + (b + 1) * P],
                                            ident[0:r, 0:r])
                    nc.tensor.transpose(ps[0:HD, t, 256:256 + r], z[0:r, t, IK:IK + HD], ident[0:r, 0:r])\
                        .then_inc(ti_ready, 1)
                pe.wait_ge(ti_evac, 6 * (L + 1))
                q = 0
                for t in range(1, TILES):
                    for h in range(IH):
                        if q >= 4:
                            pe.wait_ge(is_relu, 16 * L + q - 3)
                        p0 = (h % 2) * HD
                        mm(ps[0:ROWS[t], q % 4, 0:KW[t]], iqT[p0:p0 + HD, h // 2, tok(t)],
                           ikT[p0:p0 + HD, KCOL[t]:KCOL[t] + KW[t]], start=True, stop=True).then_inc(is_ready, 1)
                        q += 1
                pe.wait_ge(is_relu, 16 * (L + 1))
                with pe.Fori(0, 3) as it:
                    for j in range(4):
                        landed(("gates", L), it, j)
                        w = slots[:, j, :].rearrange("p (k n) -> p k n", k=KD)
                        for f in range(2):
                            g = 2 * j + f
                            if g >= 3:
                                pe.wait_ge(g_evac, it * 8 + (24 * L + g - 2))
                            last = features(g % 4, lambda k: w[:, k, f * P:(f + 1) * P], lambda k: hT[:, k, :], KD, f == 0)
                            last.then_inc(g_ready, 1)
                    pe.wait_ge(g_evac, it * 8 + (24 * L + 7))
                pe.wait_ge(g_evac, 24 * (L + 1))
                pe.wait_ge(logf_ready, L + 1)
                for t in range(SAMPLE):
                    for s in range(t + 1):
                        mm(ps[0:BH, 6, t * P:(t + 1) * P], logf[:, s, :], (tri if s == t else ones)[:, :],
                           start=(s == 0), stop=(s == t))
                plf = past[:, 960:966]
                mm(ps[0:BH, 7, 0:PAST], plf, tri[:, :], start=True, stop=True)
                mm(ps[0:BH, 7, PAST:PAST + DEC], plf, ones[:, 0:DEC], start=True, stop=False)
                mm(ps[0:BH, 7, PAST:PAST + DEC], logf[:, SAMPLE, :], tri[:, 0:DEC], start=False, stop=True)\
                    .then_inc(cum_ready, 1)
                pe.wait_ge(pool_mats_loaded, 16 * (L + 1))
                pe.wait_ge(poolw_loaded, 80 * (L + 1))
                for t in range(TILES):
                    r = ROWS[t]
                    for g in range(4):
                        c0 = CU + g * HD
                        o = ps[0:HD, t, g * P:g * P + r]
                        if t == SAMPLE:
                            mm(o, hist[:, g * HD:(g + 1) * HD], poolm[0:HIST, 3, P + g * DEC:P + (g + 1) * DEC],
                               start=True, stop=False)
                            last = mm(o, z[0:DEC, t, c0:c0 + HD], poolm[0:DEC, 3, g * DEC:(g + 1) * DEC],
                                      start=False, stop=True)
                            continue
                        last = mm(o, z[:, t, c0:c0 + HD], poolm[:, 1 if t == 0 else 0, g * P:(g + 1) * P],
                                  start=True, stop=(t == 0))
                        if t:
                            last = mm(o, z[:, t - 1, c0:c0 + HD], poolm[:, 2, g * P:(g + 1) * P],
                                      start=False, stop=True)
                    last.then_inc(pm_ready, 1)
                for t in range(TILES):
                    r = ROWS[t]
                    pe.wait_ge(pm_evac, TILES * L + t + 1)
                    if t:
                        pe.wait_ge(po_evac, TILES * L + t)
                    for pr in range(2):
                        for i in range(2):
                            g = 2 * pr + i
                            last = mm(ps[:, 5, pr * P:pr * P + r], poolw[:, g, :], pooled[:, g * P:g * P + r],
                                      start=(i == 0), stop=(i == 1))
                    last.then_inc(po_ready, 1)
                pe.wait_ge(po_evac, TILES * (L + 1))
                pe.wait_ge(cum_evac, L + 1)
                for i, (kind, t) in enumerate(at_groups):
                    if i >= 8:
                        if at_on_act[i - 8]:
                            pe.wait_ge(at_evac_act, N_AT_ACT * L + sum(at_on_act[:i - 7]))
                        else:
                            pe.wait_ge(at_evac_dve, N_AT_DVE * L + (i - 7) - sum(at_on_act[:i - 7]))
                    b = i % 8
                    if kind == "past":
                        nc.tensor.transpose(ps[0:HD, b, 0:P], past[:, 0:HD], ident[:, :])
                        src = [past[:, 192 + q * P:192 + (q + 1) * P] for q in range(3)]
                        first, r = 1, P
                    else:
                        r = ROWS[t]
                        c0 = {"a": AQ, "bq": BQ, "bk": BK}[kind]
                        src = [z[0:r, t, c0 + q * P:c0 + (q + 1) * P] for q in range(3)]
                        first = 0
                        if kind == "a":
                            nc.tensor.transpose(ps[0:HD, b, 3 * P:3 * P + r], z[0:r, t, AK:AK + HD], ident[0:r, 0:r])
                    for q, s in enumerate(src):
                        last = nc.tensor.transpose(ps[:, b, (first + q) * P:(first + q) * P + r], s, ident[0:r, 0:r])
                    last.then_inc(at_ready, 1)
                pe.wait_ge(at_evac_act, N_AT_ACT * (L + 1))
                pe.wait_ge(at_evac_dve, N_AT_DVE * (L + 1))
                pe.wait_ge(mask_ready, 4 * (L + 1))
                pe.wait_ge(identb_ready, 1)
                base = NATT * L
                for i in range(NATT + 4):
                    if i < NATT:
                        t, m, h = items[i]
                        r, w = ROWS[t], KW[t]
                        if i >= 3:
                            pe.wait_ge(p_ready, base + i - 2)
                        p0 = (h % 2) * HD
                        qT, kT = (aqT[p0:p0 + HD, h // 2], akT[p0:p0 + HD, :]) if m == 0 else \
                                 (bqT[p0:p0 + HD, h // 2], bkT[p0:p0 + HD, h // 2])
                        out = ps[0:r, i % 3, 0:w]
                        mm(out, qT[:, tok(t)], kT[:, KCOL[t]:KCOL[t] + w], start=True, stop=False)
                        if m == 0:
                            last = mm(out, identb[0:r, 0:r], amask[0:r, MOFF[t]:MOFF[t] + w], start=False, stop=True)
                        else:
                            mm(out, ident[0:BH, h:h + 1].to_broadcast([BH, r]), negcum[:, KCOL[t]:KCOL[t] + w],
                               start=False, stop=False)
                            last = mm(ps[0:r, i % 3, w - r:w], identb[0:r, 0:r], cmask[0:r, 0:r], start=False, stop=True)
                        last.then_inc(s_ready, 1)
                    j = i - 1
                    if 0 <= j < NATT:
                        t, m, h = items[j]
                        pe.wait_ge(p_ready, base + j + 1)
                        if j >= 2:
                            pe.wait_ge(pt_evac, base + j - 1)
                        r = ROWS[t]
                        for b, (c0, kr, _) in enumerate(key_blocks(t)):
                            last = nc.tensor.transpose(ps[0:kr, 3 + j % 2, b * P:b * P + r],
                                                       probs[j % 2][0:r, c0:c0 + kr], ident[0:r, 0:r])
                        last.then_inc(pt_ready, 1)
                    j = i - 2
                    if 0 <= j < NATT:
                        t, m, h = items[j]
                        tm = j // AH
                        pe.wait_ge(pt_evac, base + j + 1)
                        if h == 0 and tm >= 2:
                            pe.wait_ge(o_evac, NTM * L + tm - 1)
                        blocks = key_blocks(t)
                        for b, (c0, kr, src) in enumerate(blocks):
                            if src == "past":
                                v = past[:, HD:2 * HD] if m == 0 else past[:, 576 + h * HD:576 + (h + 1) * HD]
                            else:
                                c = AV if m == 0 else BV + h * HD
                                v = z[0:kr, src, c:c + HD]
                            last = mm(ps[0:ROWS[t], 5 + tm % 2, h * HD:(h + 1) * HD], probsT[j % 2][0:kr, b * P:b * P + ROWS[t]],
                                      v, start=(b == 0), stop=(b == len(blocks) - 1))
                        last.then_inc(pv_done, 1)
                    j = i - 3
                    if 0 <= j < NATT and j % AH == AH - 1:
                        t, m, h = items[j]
                        tm = j // AH
                        pe.wait_ge(o_evac, NTM * L + tm + 1)
                        if tm:
                            pe.wait_ge(ot_evac, NTM * L + tm)
                        r = ROWS[t]
                        c = BQ if m else AQ
                        for q in range(3):
                            last = nc.tensor.transpose(ps[:, 7, q * P:q * P + r], z[0:r, t, c + q * P:c + (q + 1) * P],
                                                       ident[0:r, 0:r])
                        last.then_inc(ot_ready, 1)
                pe.wait_ge(ot_evac, NTM * (L + 1))
                with pe.Fori(0, 2) as it:
                    for j in range(2):
                        landed(("branch", L), it, j)
                        w = slots[:, j, :].rearrange("p (k n) -> p k n", k=KD)
                        for f in range(2):
                            for i, (a, b) in enumerate(((0, 3), (3, 6), (6, 8))):
                                g = (2 * j + f) * 3 + i
                                if g >= 3:
                                    pe.wait_ge(b_evac, it * 12 + (24 * L + g - 2))
                                last = features(g % 4, lambda k: w[:, a + k, f * P:(f + 1) * P],
                                                lambda k: oT[:, a + k, :], b - a, f == i == 0)
                                last.then_inc(b_ready, 1)
                    pe.wait_ge(b_evac, it * 12 + (24 * L + 11))
                pe.wait_ge(b_evac, 24 * (L + 1))
                with pe.Fori(0, 2) as it:
                    pe.wait_ge(m_ready, KD * (L + 1))
                    for j in range(2):
                        landed(("out", L), it, j)
                        w = slots[:, j, :].rearrange("p (k n) -> p k n", k=KD)
                        for f in range(2):
                            g = 2 * j + f
                            if g == 3:
                                pe.wait_ge(x_upd, it * 4 + (xu(L, "start") + 1))
                            last = features(g, lambda k: w[:, k, f * P:(f + 1) * P], lambda k: gT[:, k, :], KD, f == 0)
                            last.then_inc(r_ready, 1)
                    pe.wait_ge(x_upd, it * 4 + (xu(L, "start") + 3))
                pe.wait_ge(x_upd, xu(L, "out"))
                norm_sums(2 * L + 1, releases=True)
                pe.wait_ge(h_ready, KD * (2 * L + 2))
                if L == 1:
                    for t in range(TILES):
                        for k in range(KD):
                            last = mm(ps[0:ROWS[t], 4, t * NEXP:(t + 1) * NEXP], hT[:, k, tok(t)], rw[:, k, :],
                                      start=(k == 0), stop=(k == KD - 1))
                    last.then_inc(rl_ready, 1)
                    pe.wait_ge(gate_ready, 1)
                    for t in range(TILES):
                        bank, c0 = (5, t * P) if t < SAMPLE else (6, 0)
                        last = nc.tensor.transpose(ps[0:NEXP, bank, c0:c0 + ROWS[t]], rt[6][0:ROWS[t], t, :],
                                                   ident[0:ROWS[t], 0:ROWS[t]])
                    last.then_inc(gt_ready, 1)
                    pe.wait_ge(gt_evac, 1)
                    for e in range(NEXP):
                        if e >= 2:
                            pe.wait_ge(gb_evac, e - 1)
                        for h in range(2):
                            last = mm(ps[:, 2 * (e % 2) + h, 0:HALF], ident[0:NEXP, e:e + 1].to_broadcast([NEXP, P]),
                                      gateT[:, h * HALF:(h + 1) * HALF], start=True, stop=True)
                        last.then_inc(gb_ready, 1)
                    pe.wait_ge(gb_evac, NEXP)
                pe.wait_ge(h_split, KD * (L + 1))
                if L == 0:
                    pe.wait_ge(m_ready, KD)

                def split_product(out_pair, buf, nk, rhs, first, last_part, each=None):
                    for k in range(nk):
                        if each:
                            each(k)
                        for h in range(2):
                            c = slice(h * HALF, (h + 1) * HALF)
                            for i, (a, b) in enumerate(((0, 0), (0, 1), (1, 0))):
                                last = mm(ps[:, 2 * out_pair + h, 0:HALF], wR[:, buf, a, k * P:(k + 1) * P], rhs(k, b)[:, c],
                                          start=(first and k == 0 and i == 0), stop=(last_part and k == nk - 1 and i == 2))
                    last.then_inc(unit_done[buf], 1)

                with pe.Fori(0, EXPERTS[L]) as it:
                    n0 = fexp_base[L]
                    units = 2 * (FB + KD)

                    def unit_split(j, w):
                        pe.wait_ge(w_split, it * units + (n0 * units + 2 * j + w + 1))

                    for f in range(FB):
                        q = 2 * (f % 2)
                        if f < 2:
                            pe.wait_ge(x_upd, it * KD + (xu(L, "out") - (1 if f == 0 else 0)))
                        else:
                            pe.wait_ge(sg_ready, it * FB + (n0 * FB + f - 1))
                        unit_split(f, 0)
                        split_product(q, 0, KD, lambda k, b: hR[:, b, k, :], True, True)
                        if f == 0:
                            pe.wait_ge(x_upd, it * KD + xu(L, "out"))
                        if f >= 2:
                            pe.wait_ge(hid_ready, it * FB + (n0 * FB + f - 1))
                        unit_split(f, 1)
                        split_product(q + 1, 1, KD, lambda k, b: hR[:, b, k, :], True, True)
                    for d in range(KD):
                        if d < 2:
                            pe.wait_ge(hid_ready, it * FB + (n0 * FB + FB - 1))
                        elif d >= 4:
                            pe.wait_ge(x_upd, it * KD + (xu(L, "out") + d - 3))

                        def hid_there(k):
                            if d == 0 and k == FB - FLO - 1:
                                pe.wait_ge(hid_ready, it * FB + (n0 * FB + FB))

                        unit_split(FB + d, 0)
                        split_product((d + 2) % 4, 0, FLO, lambda k, b: hidR[:, b, k, :], True, False)
                        unit_split(FB + d, 1)
                        split_product((d + 2) % 4, 1, FB - FLO, lambda k, b: hidR[:, b, FLO + k, :], False, True, hid_there)
            pe.wait_ge(x_upd, xu(DEPTH - 1, "ffn"))
            norm_sums(2 * DEPTH)
            pe.wait_ge(h_ready, KD * (2 * DEPTH + 1))
            for t in range(TILES):
                for g in range(2):
                    i = 2 * t + g
                    if i >= 8:
                        pe.wait_ge(y_evac, i - 7)
                    for q in range(4):
                        last = nc.tensor.transpose(ps[0:ROWS[t], i % 8, q * P:(q + 1) * P], hT[:, 4 * g + q, tok(t)],
                                                   ident[:, :])
                    last.then_inc(y_ready, 1)

        @block.scalar
        def _(act):
            ch = Chain(act, act_chain)
            A = nc.scalar.activation

            for t in range(TILES):
                for g in range(2):
                    act.wait_ge(xt_ready, 2 * t + g + 1)
                    A(xT[:, 4 * g:4 * g + 4, tok(t)],
                      ps[:, (2 * t + g) % 8, :].rearrange("p (q n) -> p q n", q=4)[:, :, 0:ROWS[t]], ACT.Copy)\
                        .then_inc(xt_evac, 1)
            act.wait_ge(vt_evac, 1)
            A(csil[:, :, :], vecT[:, 0, V_C:V_C + 16].rearrange("p (s k) -> p s k", s=2), ACT.Silu).then_inc(csil_ready, 1)

            def norm(n, x_there, gain, shift, stage_mod):
                for k in range(KD):
                    if x_there is not None:
                        act.wait_ge(x_upd, x_there + k + 1)
                    elif k == 0:
                        act.wait_ge(xt_evac, 10)
                    A(sqs[n % 2][:, k, :], xT[:, k, :], ACT.Square).then_inc(sq_ready, 1)
                act.wait_ge(v_ready, n + 1)
                A(oT[:, 1, :], oT[:, 0, :], ACT.Sqrt).then_inc(root_ready, 1)
                if stage_mod:
                    act.wait_ge(mod_ready, stage_mod)
                for k in range(KD):
                    act.wait_ge(normed, KD * n + k + 1)
                    for s, c in ((0, slice(0, SEQ)), (1, slice(SEQ, NTOK))):
                        if shift is None:
                            last = A(hT[:, k, c], hT[:, k, c], ACT.Copy, scale=gain(k, s))
                        else:
                            last = A(hT[:, k, c], hT[:, k, c], ACT.Identity, scale=gain(k, s), bias=shift(k, s))
                    last.then_inc(h_ready, 1)

            for L in range(DEPTH):
                norm(2 * L, xu(L - 1, "ffn") - KD if L else None, lambda k, s: scl[:, 0, k, s:s + 1],
                     lambda k, s: mod[:, M_SH1 + k, s:s + 1], L + 1)
                with act.Fori(0, ZITER) as it:
                    for j in range(ZBODY):
                        for t in range(TILES):
                            act.wait_ge(z_ready, it * (ZBODY * TILES) + (NZ * L + j * TILES + t + 1))
                            A(z[0:ROWS[t], t, ds(it * (ZBODY * ZB) + j * ZB, ZB)], ps[0:ROWS[t], t, 0:ZB], ACT.Copy)\
                                .then_inc(z_evac, 1)
                act.wait_ge(lf_abs, L + 1)
                ch.link(A(lft[:, 2], lft[:, 1], ACT.Exp, scale=-1.0))
                A(lft[:, 2], lft[:, 2], ACT.Ln, bias=1.0).then_inc(lf_ln, 1)
                act.wait_ge(ti_ready, 6 * L + 1)
                A(ikT[0:HD, SEQ:SEQ + PAST], ps[0:HD, 5, 0:P], ACT.Copy)
                A(ikT[HD:P, SEQ:SEQ + PAST], ps[0:HD, 5, 0:P], ACT.Copy).then_inc(ti_evac, 1)
                for t in range(TILES):
                    act.wait_ge(ti_ready, 6 * L + t + 2)
                    A(iqT[:, :, tok(t)], ps[:, t, 0:256].rearrange("p (b n) -> p b n", b=2)[:, :, 0:ROWS[t]], ACT.Copy)
                    A(ikT[0:HD, keycol(t)], ps[0:HD, t, 256:256 + ROWS[t]], ACT.Copy)
                    A(ikT[HD:P, keycol(t)], ps[0:HD, t, 256:256 + ROWS[t]], ACT.Copy).then_inc(ti_evac, 1)
                q = 0
                for t in range(1, TILES):
                    for h in range(IH):
                        act.wait_ge(is_ready, 16 * L + q + 1)
                        if q >= 2:
                            act.wait_ge(is_acc, 16 * L + q - 1)
                        A(rel[q % 2][0:ROWS[t], 0:KW[t]], ps[0:ROWS[t], q % 4, 0:KW[t]], ACT.Relu).then_inc(is_relu, 1)
                        q += 1
                with act.Fori(0, 3) as it:
                    for g in range(8):
                        act.wait_ge(g_ready, it * 8 + (24 * L + g + 1))
                        A(gT[:, ds(it * 8 + g, 1), :].rearrange("p e (a n) -> p (e a) n", a=2), pair(g % 4), ACT.Sigmoid)\
                            .then_inc(g_evac, 1)
                for i, (kind, t) in enumerate(at_groups):
                    if not at_on_act[i]:
                        continue
                    act.wait_ge(at_ready, N_AT * L + i + 1)
                    src = ps[:, i % 8, :].rearrange("p (q n) -> p q n", q=4)[:, :, 0:ROWS[t]]
                    if kind == "a":
                        A(aqT[:, :, tok(t)], src[:, 0:3, :], ACT.Copy, scale=HD ** -0.5)
                        A(akT[0:HD, keycol(t)], src[0:HD, 3, :], ACT.Copy)
                        A(akT[HD:P, keycol(t)], src[0:HD, 3, :], ACT.Copy).then_inc(at_evac_act, 1)
                    else:
                        A(bkT[:, :, keycol(t)], src[:, 0:3, :], ACT.Copy).then_inc(at_evac_act, 1)
                base = NATT * L

                def ot_copy(j):
                    t, m, h = items[j]
                    tm = j // AH
                    act.wait_ge(ot_ready, NTM * L + tm + 1)
                    A(oT[:, 3 * m:3 * m + 3, tok(t)],
                      ps[:, 7, 0:384].rearrange("p (q n) -> p q n", q=3)[:, :, 0:ROWS[t]], ACT.Copy).then_inc(ot_evac, 1)

                for i in range(NATT):
                    t, m, h = items[i]
                    r, w = ROWS[t], KW[t]
                    tm = i // AH
                    act.wait_ge(mx_ready, base + i + 1)
                    if i >= 2:
                        act.wait_ge(pt_ready, base + i - 1)
                    if h == 0 and tm >= 2:
                        act.wait_ge(o_evac, NTM * L + tm - 1)
                    A(probs[i % 2][0:r, 0:w], ps[0:r, i % 3, 0:w], ACT.Exp, bias=nmax[0:r, i % 12:i % 12 + 1],
                      accum_out=rsum[0:r, tm % 2, h:h + 1]).then_inc(p_ready, 1)
                    if i >= 4 and (i - 4) % AH == AH - 1:
                        ot_copy(i - 4)
                ot_copy(NATT - 1)
                norm(2 * L + 1, xu(L, "start"), lambda k, s: scl[:, 1, k, s:s + 1],
                     lambda k, s: mod[:, M_SH2 + k, s:s + 1], 0)
                if L == 1:
                    act.wait_ge(rexp_in, 1)
                    A(rt[5], rt[5], ACT.Exp).then_inc(rexp_out, 1)
                    act.wait_ge(gt_ready, 1)
                    A(gateT[:, 0:SEQ], ps[0:NEXP, 5, :], ACT.Copy)
                    A(gateT[:, SEQ:NTOK], ps[0:NEXP, 6, 0:DEC], ACT.Copy).then_inc(gt_evac, 1)
                    for e in range(NEXP):
                        act.wait_ge(gb_ready, e + 1)
                        A(halves(gbc[:, e, :]), pair(e % 2), ACT.Copy).then_inc(gb_evac, 1)
                if L == 1:
                    act.wait_ge(rl_ready, 1)
                act.wait_ge(h_split, KD * (L + 1))
                with act.Fori(0, EXPERTS[L]) as it:
                    n0 = fexp_base[L]
                    nb = FB + KD

                    def high(j, w):
                        if w == 0:
                            act.wait_ge(slot_full[j % NSLOT], ring.full(("ffn", L), it, j))
                        if j:
                            act.wait_ge(unit_done[w], it * nb + (n0 * nb + j))
                        else:
                            act.wait_ge(x_upd, it * KD + xu(L, "out"))
                        n = KD * P if j < FB else (FLO if w == 0 else FB - FLO) * P
                        c0 = w * (KD * P if j < FB else FLO * P)
                        A(wR[:, w, 0, 0:n], slots[:, j % NSLOT, c0:c0 + n], ACT.Copy).then_inc(w_high, 1)

                    def silu(f):
                        act.wait_ge(unit_done[0], it * nb + (n0 * nb + f + 1))
                        if f >= 2:
                            act.wait_ge(hid_ready, it * FB + (n0 * FB + f - 1))
                        A(halves(sg[f % 2]), pair(2 * (f % 2)), ACT.Silu).then_inc(sg_ready, 1)

                    for j in range(FB + KD):
                        high(j, 0)
                        if 1 <= j <= FB:
                            silu(j - 1)
                        high(j, 1)
            norm(2 * DEPTH, xu(DEPTH - 1, "ffn") - KD, lambda k, s: vecT[:, 0, V_FIN + k:V_FIN + k + 1], None, 0)
            for i in range(2 * TILES):
                t, g = i // 2, i % 2
                act.wait_ge(y_ready, i + 1)
                A(xin[0:ROWS[t], t, g * 512:(g + 1) * 512], ps[0:ROWS[t], i % 8, :], ACT.Copy).then_inc(y_evac, 1)

        @block.vector
        def _(dve):
            ch = Chain(dve, dve_chain)
            V = nc.vector
            V.memset(ones[:, :], 1.0).then_inc(memsets, 1)
            ch.link(V.memset(amask[:, 0:P], 0.0))
            ch.link(V.memset(amask[0:HD, HD:P], NEG))
            ch.link(V.memset(logf[:, :, :], 0.0))
            ch.link(V.memset(lft[:, :, :, :], 0.0))
            dve.wait_ge(consts_loaded, 96)
            ch.link(V.tensor_tensor(score[:, 0:P], tri[:, :], ident[:, :], ALU.subtract))
            ch.link(V.tensor_scalar(cmask[:, :], score[:, 0:P], NEG, None, ALU.mult))
            V.tensor_copy(identb[:, :], ident[:, :]).then_inc(identb_ready, 1)
            dve.wait_ge(vt_ready, 1)
            V.tensor_copy(vecT[:, :, :], ps[:, 0:2, 0:V_ROWS]).then_inc(vt_evac, 1)

            def stats(n):
                v, s, r, t = (oT[:, i, :] for i in range(4))
                dve.wait_ge(ms_ready, n + 1)
                V.tensor_scalar(halves(v), pair(0), 1.0 / D, NORM_EPS, ALU.mult, ALU.add).then_inc(v_ready, 1)
                dve.wait_ge(root_ready, n + 1)
                ch.link(V.reciprocal(r, s))
                ch.link(V.tensor_tensor(t, r, r, ALU.mult))
                ch.link(V.tensor_tensor(t, t, v, ALU.mult))
                ch.link(V.tensor_scalar(t, t, -0.5, 1.5, ALU.mult, ALU.add))
                ch.link(V.tensor_tensor(r, r, t, ALU.mult))
                for k in range(KD):
                    V.tensor_tensor(hT[:, k, :], xT[:, k, :], r, ALU.mult).then_inc(normed, 1)

            for L in range(DEPTH):
                dve.wait_ge(ada_done, 24 * (L + 1))
                bias = vecT[:, L, V_ADAB:V_ADAB + 48].unsqueeze(2).to_broadcast([P, 48, 2])
                ch.link(V.tensor_tensor(mod[:, :, :], ps[:, 7, 0:96].rearrange("p (b s) -> p b s", s=2), bias, ALU.add))
                for i, (sc0, g0) in enumerate(((M_SC1, V_NMIX), (M_SC2, V_NFFN))):
                    gain = vecT[:, L, g0:g0 + KD].unsqueeze(2).to_broadcast([P, KD, 2])
                    last = V.scalar_tensor_tensor(scl[:, i], mod[:, sc0:sc0 + KD, :], 1.0, gain, ALU.add, ALU.mult)
                last.then_inc(mod_ready, 1)
                stats(2 * L)
                tmpf = oT[:, :, :].rearrange("p k n -> p (k n)")

                ropes = [6 * L]

                def rope(c0, nh):
                    for a, b, r in ((0, SAMPLE, P), (SAMPLE, TILES, DEC)):
                        n = b - a
                        v = z[0:r, a:b, c0:c0 + nh * HD].rearrange("p t (h u f) -> p t h u f", h=nh, u=2)
                        x1, x2 = v[:, :, :, 0, :], v[:, :, :, 1, :]
                        cos = cs[0:r, a:b, 0, :].unsqueeze(2).to_broadcast([r, n, nh, 32])
                        sin = cs[0:r, a:b, 1, :].unsqueeze(2).to_broadcast([r, n, nh, 32])
                        tm = [tmpf[0:r, 896 * i:896 * i + n * nh * 32].rearrange("p (t h f) -> p t h f", t=n, h=nh)
                              for i in range(3)]
                        V.tensor_tensor(tm[0], x1, cos, ALU.mult)
                        V.tensor_tensor(tm[1], x2, sin, ALU.mult)
                        ch.link(V.tensor_tensor(tm[2], x1, sin, ALU.mult))
                        V.tensor_tensor(x1, tm[0], tm[1], ALU.subtract)
                        ch.link(V.tensor_tensor(x2, x2, cos, ALU.mult))
                        V.tensor_tensor(x2, x2, tm[2], ALU.add).then_inc(rope_done, 1)
                        ropes[0] += 1
                        dve.wait_ge(rope_done, ropes[0])

                dve.wait_ge(z_evac, NZ * L + 4 * TILES)
                rope(IQ, IH)
                rope(IK, 1)
                rope(AQ, AH + 1)
                dve.wait_ge(z_evac, NZ * L + 8 * TILES)
                for a, b, r in ((0, SAMPLE, P), (SAMPLE, TILES, DEC)):
                    bias = bfb[0:r, L, :].unsqueeze(1).to_broadcast([r, b - a, BH])
                    ch.link(V.tensor_tensor(lft[0:r, 0, a:b, :], z[0:r, a:b, BF_:BF_ + BH], bias, ALU.add))
                V.scalar_tensor_tensor(lft[:, 1], lft[:, 0], -1.0, lft[:, 0], ALU.mult, ALU.max).then_inc(lf_abs, 1)
                dve.wait_ge(lf_ln, L + 1)
                for a, b, r in ((0, SAMPLE, P), (SAMPLE, TILES, DEC)):
                    last = V.scalar_tensor_tensor(logf[0:r, a:b, :], lft[0:r, 0, a:b, :], 0.0, lft[0:r, 2, a:b, :],
                                                  ALU.min, ALU.subtract)
                last.then_inc(logf_ready, 1)
                q = 0
                for t in range(1, TILES):
                    r, w = ROWS[t], KW[t]
                    sc = score[0:r, SOFF[t]:SOFF[t] + w]
                    for h in range(IH):
                        dve.wait_ge(is_relu, 16 * L + q + 1)
                        wt = z[0:r, t, IW + h:IW + h + 1]
                        src = rel[q % 2][0:r, 0:w]
                        if h == 0:
                            last = V.tensor_scalar(sc, src, wt, None, ALU.mult)
                        else:
                            dve.wait_ge(is_acc, 16 * L + q)
                            last = V.scalar_tensor_tensor(sc, src, wt, sc, ALU.mult, ALU.add)
                        last.then_inc(is_acc, 1)
                        q += 1
                dve.wait_ge(is_acc, 16 * (L + 1))
                for t in range(1, SAMPLE):
                    last = V.memset(score[0:CHUNK, SOFF[t] + KW[t] - CHUNK:SOFF[t] + KW[t]], LOWEST)
                ch.link(last)
                for t in range(1, TILES):
                    r, w = ROWS[t], KW[t]
                    kk = K_SAMPLE if t == SAMPLE else K_PROMPT
                    sc, wk = score[0:r, SOFF[t]:SOFF[t] + w], work[0:r, 0:w]
                    ch.link(V.max(m8[0:r, :], sc))
                    ch.link(V.match_replace(wk, m8[0:r, :], sc, LOWEST))
                    rounds = kk // 8 - 2
                    for _ in range(rounds):
                        ch.link(V.max(m8[0:r, :], wk))
                        ch.link(V.match_replace(wk, m8[0:r, :], wk, LOWEST))
                    ch.link(V.max(m8[0:r, :], wk))
                    kth = m8[0:r, 7:8]
                    gt, eq, rk = isgt[0:r, 0:w], iseq[0:r, 0:w], rank[0:r, 0:w]
                    V.tensor_scalar(eq, sc, kth, None, ALU.is_equal)
                    ch.link(V.tensor_scalar(gt, sc, kth, None, ALU.is_gt, ALU.add, accum_out=stat[0:r, 0:1]))
                    ch.link(V.tensor_scalar(stat[0:r, 1:2], stat[0:r, 0:1], -1.0, float(kk), ALU.mult, ALU.add))
                    ch.link(V.tensor_tensor_scan(rk, eq, eq, 0.0, ALU.add, ALU.max))
                    ch.link(V.scalar_tensor_tensor(rk, rk, stat[0:r, 1:2], eq, ALU.is_le, ALU.mult))
                    ch.link(V.tensor_tensor(rk, rk, gt, ALU.add))
                    V.tensor_scalar(amask[0:r, MOFF[t]:MOFF[t] + w], rk, -NEG, NEG, ALU.mult, ALU.add).then_inc(mask_ready, 1)
                    dve.wait_ge(mask_ready, 4 * L + t)
                dve.wait_ge(cum_ready, L + 1)
                V.tensor_scalar(negcum[:, 0:SEQ], ps[0:BH, 6, :], -1.0, None, ALU.mult)
                V.tensor_scalar(negcum[:, SEQ:KEYS], ps[0:BH, 7, 0:PAST + DEC], -1.0, None, ALU.mult).then_inc(cum_evac, 1)
                for t in range(TILES):
                    r = ROWS[t]
                    dve.wait_ge(pm_ready, TILES * L + t + 1)
                    if t:
                        dve.wait_ge(po_ready, TILES * L + t)
                    v4 = lambda ap: ap.rearrange("p (g n) -> p g n", g=4)[:, :, 0:r]
                    V.tensor_copy(v4(pooled), v4(ps[0:HD, t, :])).then_inc(pm_evac, 1)
                    dve.wait_ge(po_ready, TILES * L + t + 1)
                    for pr in range(2):
                        last = V.tensor_scalar(oT[:, 6 + pr, tok(t)], ps[:, 5, pr * P:pr * P + r],
                                               vecT[:, L, V_PSC + pr:V_PSC + pr + 1], None, ALU.mult)
                    last.then_inc(po_evac, 1)
                for i, (kind, t) in enumerate(at_groups):
                    if at_on_act[i]:
                        continue
                    dve.wait_ge(at_ready, N_AT * L + i + 1)
                    src = ps[:, i % 8, :].rearrange("p (q n) -> p q n", q=4)
                    if kind == "past":
                        V.tensor_copy(akT[0:HD, SEQ:SEQ + PAST], src[0:HD, 0, :])
                        V.tensor_copy(akT[HD:P, SEQ:SEQ + PAST], src[0:HD, 0, :])
                        V.tensor_copy(bkT[:, :, SEQ:SEQ + PAST], src[:, 1:4, :]).then_inc(at_evac_dve, 1)
                    else:
                        V.tensor_scalar(bqT[:, :, tok(t)], src[:, 0:3, 0:ROWS[t]], HD ** -0.5, None, ALU.mult)\
                            .then_inc(at_evac_dve, 1)
                base = NATT * L
                for i in range(NATT + 2):
                    if i < NATT:
                        t, m, h = items[i]
                        r = ROWS[t]
                        dve.wait_ge(s_ready, base + i + 1)
                        V.tensor_reduce(nmax[0:r, i % 12:i % 12 + 1], ps[0:r, i % 3, 0:KW[t]], AX.X, ALU.max, negate=True)\
                            .then_inc(mx_ready, 1)
                    j = i - 1
                    if 0 <= j < NATT:
                        t, m, h = items[j]
                        r = ROWS[t]
                        dve.wait_ge(pt_ready, base + j + 1)
                        if j >= 2:
                            dve.wait_ge(pv_done, base + j - 1)
                        nb = len(key_blocks(t))
                        src = ps[:, 3 + j % 2, 0:nb * P].rearrange("p (b n) -> p b n", b=nb)
                        dst = probsT[j % 2][:, 0:nb * P].rearrange("p (b n) -> p b n", b=nb)
                        if t == SAMPLE:
                            V.tensor_copy(dst[:, 0, 0:r], src[:, 0, 0:r])
                            last = V.tensor_copy(dst[0:DEC, 1, 0:r], src[0:DEC, 1, 0:r])
                        else:
                            last = V.tensor_copy(dst, src)
                        last.then_inc(pt_evac, 1)
                    j = i - 2
                    if 0 <= j < NATT and j % AH == AH - 1:
                        t, m, h = items[j]
                        r, tm = ROWS[t], j // AH
                        dve.wait_ge(p_ready, base + j + 1)
                        ch.link(V.reciprocal(rinv[0:r, tm % 2, :], rsum[0:r, tm % 2, :]))
                        dve.wait_ge(pv_done, base + j + 1)
                        c = BQ if m else AQ
                        V.tensor_tensor(z[0:r, t, c:c + AH * HD].rearrange("p (h d) -> p h d", h=AH),
                                        ps[0:r, 5 + tm % 2, 0:AH * HD].rearrange("p (h d) -> p h d", h=AH),
                                        rinv[0:r, tm % 2, :].unsqueeze(2).to_broadcast([r, AH, HD]), ALU.mult)\
                            .then_inc(o_evac, 1)
                with dve.Fori(0, 2) as it:
                    ch.enter(it, 0, 4)
                    for d in range(4):
                        def blk(i):
                            return gT[:, ds(it * 4 + (i * KD + d), 1), :].rearrange("p e n -> p (e n)")
                        for i in range(3):
                            g = 3 * d + i
                            dve.wait_ge(b_ready, it * 12 + (24 * L + g + 1))
                            V.tensor_tensor(halves(blk(i)), pair(g % 4), halves(blk(i)), ALU.mult).then_inc(b_evac, 1)
                            dve.wait_ge(b_evac, it * 12 + (24 * L + g + 1))
                            if i == 1:
                                ch.link(V.tensor_tensor(blk(0), blk(0), blk(1), ALU.add))
                            if i == 2:
                                V.tensor_tensor(blk(0), blk(0), blk(2), ALU.add).then_inc(m_ready, 1)
                ch.leave(2)

                def residual(pr, k, gate):
                    for s, hh, a, b in ((0, 0, 0, HALF), (0, 1, HALF, SEQ), (1, 1, SEQ, NTOK)):
                        x = xT[:, k, a:b]
                        last = V.scalar_tensor_tensor(x, ps[:, 2 * pr + hh, a - hh * HALF:b - hh * HALF],
                                                      mod[:, gate + k, s:s + 1], x, ALU.mult, ALU.add)
                    last.then_inc(x_upd, 1)

                for d in range(KD):
                    dve.wait_ge(r_ready, KD * L + d + 1)
                    residual(d % 4, d, M_G1)
                dve.wait_ge(x_upd, xu(L, "out"))
                stats(2 * L + 1)
                dve.wait_ge(outs_done, 160 * (L + 1))
                for k in range(KD):
                    dve.wait_ge(h_ready, KD * (2 * L + 1) + k + 1)
                    ch.link(V.tensor_copy(hR[:, 0, k, :], hT[:, k, :]))
                    V.tensor_tensor(hR[:, 1, k, :], hT[:, k, :], hR[:, 0, k, :].bitcast(FP), ALU.subtract)\
                        .then_inc(h_split, 1)
                if L == 1:
                    lg, eq, gt, rk, pre, ex, ga, c2 = rt
                    dve.wait_ge(outs_done, 160 * 2)
                    ch.link(V.memset(lg, 0.0))
                    dve.wait_ge(rl_ready, 1)
                    for a, b, r in ((0, SAMPLE, P), (SAMPLE, TILES, DEC)):
                        ch.link(V.tensor_tensor(lg[0:r, a:b, :],
                                                ps[0:r, 4, a * NEXP:b * NEXP].rearrange("p (t e) -> p t e", e=NEXP),
                                                rb[0:r, :].unsqueeze(1).to_broadcast([r, b - a, NEXP]), ALU.add))
                    for t in range(TILES):
                        last = V.max(pre[:, t, :], lg[:, t, :])
                    ch.link(last)
                    first = pre[:, :, 0:1].to_broadcast([P, TILES, NEXP])
                    second = pre[:, :, 1:2].to_broadcast([P, TILES, NEXP])
                    V.tensor_tensor(ex, lg, first, ALU.subtract).then_inc(rexp_in, 1)
                    V.tensor_tensor(gt, lg, second, ALU.is_gt)
                    ch.link(V.tensor_tensor(eq, lg, second, ALU.is_equal))
                    for t in range(TILES):
                        last = V.tensor_tensor_scan(rk[:, t, :], eq[:, t, :], eq[:, t, :], 0.0, ALU.add, ALU.max)
                    ch.link(last)
                    ch.link(V.tensor_reduce(c2[:, :, 0:1], gt, AX.X, ALU.add))
                    ch.link(V.tensor_tensor(rk, rk, c2[:, :, 0:1].to_broadcast([P, TILES, NEXP]), ALU.add))
                    ch.link(V.scalar_tensor_tensor(rk, rk, 2.0, eq, ALU.is_le, ALU.mult))
                    ch.link(V.tensor_tensor(rk, rk, gt, ALU.add))
                    dve.wait_ge(rexp_out, 1)
                    ch.link(V.tensor_tensor(ex, ex, rk, ALU.mult))
                    ch.link(V.tensor_reduce(c2[:, :, 0:1], ex, AX.X, ALU.add))
                    ch.link(V.reciprocal(c2[:, :, 1:2], c2[:, :, 0:1]))
                    V.tensor_tensor(ga, ex, c2[:, :, 1:2].to_broadcast([P, TILES, NEXP]), ALU.mult).then_inc(gate_ready, 1)
                with dve.Fori(0, EXPERTS[L]) as it:
                    n0 = fexp_base[L]
                    units = 2 * (FB + KD)
                    nb = FB + KD
                    ch.enter(it, 0, 2 * FB)

                    def low(j, w):
                        dve.wait_ge(w_high, it * units + (n0 * units + 2 * j + w + 1))
                        n = KD * P if j < FB else (FLO if w == 0 else FB - FLO) * P
                        c0 = w * (KD * P if j < FB else FLO * P)
                        V.tensor_tensor(wR[:, w, 1, 0:n], slots[:, j % NSLOT, c0:c0 + n], wR[:, w, 0, 0:n].bitcast(FP),
                                        ALU.subtract).then_inc(w_split, 1)

                    def gated(f):
                        dve.wait_ge(sg_ready, it * FB + (n0 * FB + f + 1))
                        V.tensor_tensor(sg[f % 2], sg[f % 2], gbc[:, ds(it, 1), :].rearrange("p e n -> p (e n)"),
                                        ALU.mult).then_inc(sgg_ready, 1)

                    def hidden(f):
                        if L == 1:
                            dve.wait_ge(sgg_ready, it * FB + f + 1)
                        else:
                            dve.wait_ge(sg_ready, it * FB + (n0 * FB + f + 1))
                        dve.wait_ge(unit_done[1], it * nb + (n0 * nb + f + 1))
                        ch.link(V.tensor_tensor(halves(hidf), pair(2 * (f % 2) + 1), halves(sg[f % 2]), ALU.mult))
                        ch.link(V.tensor_copy(hidR[:, 0, f, :], hidf))
                        V.tensor_tensor(hidR[:, 1, f, :], hidf, hidR[:, 0, f, :].bitcast(FP), ALU.subtract)\
                            .then_inc(hid_ready, 1)
                        dve.wait_ge(hid_ready, it * FB + (n0 * FB + f + 1))

                    for j in range(FB + KD):
                        low(j, 0)
                        if L == 1 and 1 <= j <= FB:
                            gated(j - 1)
                        low(j, 1)
                        if 1 <= j <= FB:
                            hidden(j - 1)
                        d = j - FB - 1
                        if d >= 0:
                            dve.wait_ge(unit_done[1], it * nb + (n0 * nb + FB + d + 1))
                            dve.wait_ge(x_upd, it * KD + (xu(L, "out") + d))
                            residual((d + 2) % 4, d, M_G2)
                    dve.wait_ge(unit_done[1], it * nb + (n0 * nb + FB + KD))
                    dve.wait_ge(x_upd, it * KD + (xu(L, "out") + KD - 1))
                    residual((KD + 1) % 4, KD - 1, M_G2)
                ch.leave(EXPERTS[L])
            dve.wait_ge(x_upd, xu(DEPTH - 1, "ffn"))
            stats(2 * DEPTH)


INPUTS = ["x_prompt", "x_sample", "cache_a_kvi", "cache_b_kv", "cache_b_logf", "state_c_pool", "c_prompt", "c_sample",
          "ada_w", "ada_b", "norm_mix_g", "w_in", "b_forget", "pool_w", "pool_scale", "w_br_a", "w_br_b", "w_br_c",
          "w_out", "norm_ffn_g", "ffn_w_gate", "ffn_w_up", "ffn_w_down", "moe_router_w", "moe_router_b",
          "moe_w_gate", "moe_w_up", "moe_w_down", "final_norm_g"]
OUTPUTS = [("y_prompt", (1, SEQ, D)), ("y_sample", (1, DEC, D)),
           ("a_kvi_p", (DEPTH, 1, SEQ, 3, HD)), ("b_kv_p", (DEPTH, 1, SEQ, 2, BH, HD)),
           ("logf_p", (DEPTH, 1, SEQ, BH)), ("pool_p", (DEPTH, 1, HIST, PW)),
           ("a_kvi_s", (DEPTH, 1, DEC, 3, HD)), ("b_kv_s", (DEPTH, 1, DEC, 2, BH, HD)),
           ("logf_s", (DEPTH, 1, DEC, BH)), ("pool_s", (DEPTH, 1, HIST, PW))]


def constants():
    ident = np.eye(P, dtype=np.float32)
    tri = np.triu(np.ones((P, P), np.float32))
    half = HD // 2
    inv = (np.float32(10000.0) ** (-np.arange(half, dtype=np.float32) / np.float32(half))).astype(np.float32)
    pos = np.zeros((P, TILES), np.float32)
    for t in range(SAMPLE):
        pos[:, t] = t * P + np.arange(P)
    pos[0:DEC, SAMPLE] = PAST + np.arange(DEC)
    ang = (pos[:, :, None] * inv[None, None, :]).astype(np.float32)
    rope = np.stack([np.cos(ang), np.sin(ang)], axis=2).astype(np.float32).reshape(P, TILES * HD)
    pool = np.zeros((P, 4, 512), np.float32)
    s, t = np.arange(P)[:, None], np.arange(P)[None, :]
    for g, w in enumerate((2, 4, 8, 16)):
        c = slice(g * P, (g + 1) * P)
        here = ((t - s >= 0) & (t - s < w)).astype(np.float32)
        pool[:, 0, c] = here / w - ident
        pool[:, 1, c] = here / np.minimum(t + 1, w) - ident
        pool[:, 2, c] = ((t + P - s) < w).astype(np.float32) / w
        pool[0:DEC, 3, g * DEC:(g + 1) * DEC] = (here / w - ident)[0:DEC, 0:DEC]
        hs, ht = np.arange(HIST)[:, None], np.arange(DEC)[None, :]
        pool[0:HIST, 3, P + g * DEC:P + (g + 1) * DEC] = ((ht + HIST - hs) < w).astype(np.float32) / w
    return {"c_ident": ident, "c_tri": tri, "c_rope": rope, "c_pool": pool}


def kernel(**inputs):
    import concourse.bacc as bacc
    from concourse.bass_utils import run_bass_kernel_spmd

    nc = bacc.Bacc("TRN2", target_bir_lowering=False, num_devices=1)
    arrays, t_in, t_out = {}, {}, {}
    consts = constants()
    for name in INPUTS + list(consts):
        a = np.ascontiguousarray(consts[name] if name in consts else inputs[name])
        arrays["in_" + name] = a
        t_in[name] = nc.dram_tensor("in_" + name, a.shape, FP, kind="ExternalInput").ap()
    for name, shape in OUTPUTS:
        t_out[name] = nc.dram_tensor("out_" + name, shape, FP, kind="ExternalOutput").ap()
    encoder_step(nc, t_in, t_out)
    r = run_bass_kernel_spmd(nc, [arrays], core_ids=[0])
    return tuple(r.results[0]["out_" + name] for name, _ in OUTPUTS)
```

```python
import numpy as np
import concourse.bass as bass
from concourse import mybir
from concourse.alu_op_type import AluOpType as ALU
from contextlib import ExitStack

FP = mybir.dt.float32
BF = mybir.dt.bfloat16
FR = mybir.dt.float32r
ACT = mybir.ActivationFunctionType
AX = mybir.AxisListType
ds = bass.ds

P = 128
D = 1024
KD = D // P
SEQ, DEC, PAST = 512, 32, 128
NTOK = SEQ + DEC
HALF = NTOK // 2
DEPTH = 2
TILES = SEQ // P + 1
SAMPLE = TILES - 1
HD = 64
AH = BH = 6
IH = 4
CHUNK = 64
K_PROMPT = min(256, SEQ // 4)
K_SAMPLE = min(256, (DEC + PAST) // 4)
NEXP = 8
FEXP = 1408
FLO = 6
FB = FEXP // P
HALVES = 2
TOP = 2
CAP = 176
CH = CAP // 2
MAX_PASS = NEXP + TOP * NTOK // CAP + 1
NWB = 4
NORM_EPS = 1e-6
NEG = -1e30
LOWEST = -3e38

AQ, AK, AV, IQ = 0, 384, 448, 512
IW, IK = 768, 772
BQ, BK, BV = 836, 1220, 1604
BF_, CU, GL = 1988, 1994, 2250
ZW = GL
ZB = 250
ZITER, ZBODY = 3, 3
N_IN = GL + 3 * D
PW = 256
HIST = 15

NSLOT = 4
SLOT = 2048

V_ADAB, V_NMIX, V_NFFN, V_PSC, V_FIN, V_C, V_ROWS = 0, 48, 56, 64, 66, 74, 90
M_SH1, M_SC1, M_G1, M_SH2, M_SC2, M_G2 = 0, 8, 16, 24, 32, 40

KW = [128, 256, 384, 512, PAST + DEC]
ROWS = [P, P, P, P, DEC]
MOFF = [0, 128, 384, 768, 1280]
MTOT = 1440
KEYS = SEQ + PAST + DEC
KCOL = [0, 0, 0, 0, SEQ]


def tok(t):
    return slice(t * P, t * P + ROWS[t])


def keycol(t):
    return slice(t * P, (t + 1) * P) if t < SAMPLE else slice(SEQ + PAST, KEYS)


class Ring:

    def __init__(self):
        self.n = {"begun": 0, "split": 0}
        self.fills, self.last, self.plan = [0] * NSLOT, [None] * NSLOT, {}

    def phase(self, name, iters, dmas, kind="begun"):
        n, per, after, own, before = len(dmas), [0] * NSLOT, [], [], []
        for j, m in enumerate(dmas):
            per[j % NSLOT] += m
            after.append(per[j % NSLOT])
        for j in range(min(NSLOT, n)):
            mine = [i for i in range(n) if i % NSLOT == j][-1]
            own.append(n - mine if iters > 1 else None)
            before.append(self.last[j])
        self.plan[name] = (kind, self.n[kind], list(self.fills), per, after, n, own, before)
        for s in range(NSLOT):
            self.fills[s] += iters * per[s]
        for j in range(n):
            self.last[j % NSLOT] = (kind, self.n[kind] + (iters - 1) * n + j)
        self.n[kind] += iters * n

    def ghost(self):
        self.n["begun"] += 1

    def full(self, name, it, j):
        _, _, fills, per, after, _, _, _ = self.plan[name]
        return (it * per[j % NSLOT] + (fills[j % NSLOT] + after[j])) * 16

    def value(self, kind, index):
        return index + 2 if kind == "begun" else index * 2 + 2

    def free(self, name, it, j, late=0):
        kind, first, _, _, _, n, own, before = self.plan[name]
        if j >= NSLOT:
            return [(kind, self.value(kind, it * n + (first + j - NSLOT + late)))]
        out = []
        if own[j] is not None and not (isinstance(it, int) and it == 0):
            out.append((kind, self.value(kind, it * n + (first - own[j]))))
        if before[j] is not None:
            out.append((before[j][0], self.value(*before[j])))
        return out


class Chain:

    def __init__(self, eng, sem):
        self.eng, self.sem, self.base, self.k = eng, sem, 0, 0

    def link(self, ins):
        self.k += 1
        ins.then_inc(self.sem, 1)
        self.eng.wait_ge(self.sem, self.base + self.k)

    def enter(self, it, start, per):
        self.total = self.base + self.k
        self.base, self.k, self.per = (it - start) * per + self.total, 0, per

    def after_loop(self, iters, per):
        self.base, self.k = iters * per + self.total, 0

    def leave(self, iters):
        assert self.k == self.per, (self.k, self.per)
        self.base, self.k = self.total + iters * self.per, 0


def encoder_step(nc, t_in, t_out):
    ring = Ring()
    for L in range(DEPTH):
        ring.phase(("ada", L), 6, [1] * 4)
        ring.phase(("z", L), ZITER, [1] * ZBODY)
        ring.phase(("gates", L), 3, [1] * 4)
        ring.phase(("branch", L), 2, [3] * 2)
        ring.phase(("out", L), 2, [1] * 2)
        ring.ghost()
        ring.phase(("ffn", L), HALVES, [2] * FB + [1] * KD, "split")

    ctx = ExitStack()
    with ctx:
        start = nc.sbuf_base
        start += -start % 64
        size = nc.sbuf_usable_end - start - 64
        ctx.enter_context(nc.sbuf_tensor("arena", [P, size // 4], FP))
        place = {"next": start}

        def sb(name, shape, dt=FP, over=None):
            n = int(np.prod(shape[1:])) * (2 if dt == BF else 4)
            n += -n % 32
            if over is None:
                at = place["next"]
                place["next"] += n
                assert place["next"] <= start + size, name
            else:
                at, room = place[over]
                assert n <= room, name
            place[name] = (at, n)
            return nc.alloc_sbuf_tensor_at(name, shape, dt, offset=at)

        def sem(name):
            return ctx.enter_context(nc.semaphore(name))

        xT = sb("xT", [P, KD, NTOK])
        hT = sb("hT", [P, KD, NTOK])
        z = sb("z", [P, TILES, ZW])
        gT = sb("gT", [P, 3 * KD, NTOK])
        slots = sb("slots", [P, NSLOT, SLOT])
        oT = sb("oT", [P, KD, NTOK])
        qk = sb("qk", [P, 1760])
        pp = sb("pp", [P, 2, 2, 512])
        amask = sb("amask", [P, MTOT], BF)
        cmask = sb("cmask", [P, P], BF)
        ident = sb("ident", [P, P])
        identb = sb("identb", [P, P], BF)
        ones = sb("ones", [P, P])
        tri = sb("tri", [P, P])
        cs = sb("cs", [P, TILES, 2, 32])
        past = sb("past", [P, 966])
        vecT = sb("vecT", [P, DEPTH, V_ROWS])
        csil = sb("csil", [P, 2, KD])
        mod = sb("mod", [P, 48, 2])
        scl = sb("scl", [P, 2, KD, 2])
        negcum = sb("negcum", [BH, KEYS])
        logf = sb("logf", [P, TILES, BH])
        lft = sb("lft", [P, 3, TILES, BH])
        bfb = sb("bfb", [P, DEPTH, BH])
        rb = sb("rb", [P, NEXP])
        rw = sb("rw", [P, KD, NEXP])
        iota = sb("iota", [P, CAP + 2], over="amask")
        etab = sb("etab", [P, MAX_PASS + 1], mybir.dt.int32, over="cmask")
        m8 = sb("m8", [P, 8])
        stat = sb("stat", [P, 4])
        nmax = sb("nmax", [P, 12])
        rsum = sb("rsum", [P, 2, AH])
        rinv = sb("rinv", [P, 2, AH])

        hR = sb("hR", [P, 2, KD, NTOK], FR, over="z")
        hidR = sb("hidR", [P, 2, FB, NTOK], FR, over="gT")
        wR = sb("wR", [P, 2, 2, KD * P], FR, over="hT")

        hTok = sb("hTok", [P, 2, TILES, D], FR, over="z")
        g_at = {"next": place["gT"][0], "end": sum(place["gT"])}

        def over_gates(name, shape, dt):
            place["_piece"] = (g_at["next"], g_at["end"] - g_at["next"])
            t = sb(name, shape, dt, over="_piece")
            g_at["next"] = place[name][0] + place[name][1]
            return t

        hg = over_gates("hg", [P, KD, 2, CAP], FR)
        hidE = over_gates("hidE", [P, FB, 2, CAP], FR)
        w_extra = over_gates("w_extra", [P, 2, KD * P], FR)
        pick = over_gates("pick", [P, TILES, CAP], FR)
        pickT = over_gates("pickT", [CH, 2, NTOK], FR)
        yR = over_gates("yR", [CH, 2, 2, 2, P], FR)
        yT = over_gates("yT", [P, 2, CAP], FP)
        w_pp = sb("w_pp", [P, 2, KD * P], FR, over="pp")
        wE = [wR[:, 0], wR[:, 1], w_extra[:, :, :], w_pp[:, :, :]]

        xin = z[:, :, 0:D]
        vrow = gT[:, 0, 0:2 * P].rearrange("p (l n) -> p l n", l=2)
        oTf = oT[:, :, :].rearrange("p k n -> p (k n)")
        score = oTf[:, 0:1312]
        SOFF = [None, 0, 256, 640, 1152]
        rel = [oTf[:, 1312 + 512 * i:1824 + 512 * i] for i in range(2)]
        work = oTf[:, 2336:2848]
        isgt, iseq = rel
        rank = work
        iqT = qk[:, 0:2 * NTOK].rearrange("p (b n) -> p b n", b=2)
        ikT = qk[:, 2 * NTOK:2 * NTOK + KEYS]
        aqT = qk[:, 0:3 * NTOK].rearrange("p (b n) -> p b n", b=3)
        pooled = qk[0:HD, 0:512]
        poolw = qk[0:HD, 512:1024].rearrange("p (g d) -> p g d", g=4)
        hist = qk[0:HIST, 1024:1280]
        hTf = hT[:, :, :].rearrange("p k n -> p (k n)")
        bqT = hTf[:, 0:3 * NTOK].rearrange("p (b n) -> p b n", b=3)
        bkT = hTf[:, 3 * NTOK:3 * NTOK + 3 * KEYS].rearrange("p (b n) -> p b n", b=3)
        akT = hTf[:, 3 * NTOK + 3 * KEYS:3 * NTOK + 4 * KEYS]
        probs = [pp[:, 0, i, :] for i in range(2)]
        probsT = [pp[:, 1, i, :] for i in range(2)]
        poolm = pp[:, :, :, :].rearrange("p a b n -> p (a b) n")
        zf = z[:, :, :].rearrange("p t n -> p (t n)")
        sqs = [zf[:, 0:KD * NTOK].rearrange("p (k n) -> p k n", k=KD), hT]
        zq = 2 * KD * NTOK
        sg = [zf[:, zq + i * NTOK:zq + (i + 1) * NTOK] for i in range(2)]
        hidf = zf[:, zq + 2 * NTOK:zq + 3 * NTOK]
        ze = 2 * TILES * D
        sge = [zf[:, ze + i * CAP:ze + (i + 1) * CAP] for i in range(2)]
        hide = [zf[:, ze + (2 + i) * CAP:ze + (3 + i) * CAP] for i in range(2)]
        gcomp = zf[:, ze + 4 * CAP:ze + 5 * CAP]
        qf = qk[:, :]
        rt = [qf[:, 40 * i:40 * (i + 1)].rearrange("p (t e) -> p t e", t=TILES) for i in range(8)]
        rowno = qf[:, 320:360].rearrange("p (t e) -> p t e", t=TILES)
        tab = qf[:, 360:360 + 8 * 8]
        t3 = qf[:, 424:424 + MAX_PASS * NEXP].rearrange("p (n e) -> p n e", e=NEXP)
        q0 = 424 + MAX_PASS * NEXP
        epass, cpass, spass = (qf[:, q0 + i * MAX_PASS:q0 + (i + 1) * MAX_PASS] for i in range(3))
        q1 = q0 + 3 * MAX_PASS
        rcol, gcol, jcol = qf[:, q1:q1 + TILES], qf[:, q1 + 8:q1 + 8 + TILES], qf[:, q1 + 16:q1 + 18]
        rowT = qf[0:NEXP, q1 + 24:q1 + 24 + NTOK]
        q2 = q1 + 24 + NTOK
        gsum = [qf[:, q2 + i * CAP:q2 + (i + 1) * CAP] for i in range(2)]
        usum = qf[:, q2 + 2 * CAP:q2 + 3 * CAP]
        rbc = oT

        ps = ctx.enter_context(nc.psum_tensor("ps", [P, 8, 512], FP))

        def pair(i):
            return ps[:, 2 * i:2 * i + 2, 0:HALF]

        def halves(ap):
            return ap.rearrange("p (a n) -> p a n", a=2)

        slot_full = [sem(f"slot_full{s}") for s in range(NSLOT)]
        block_begun = sem("block_begun")
        w_high, w_split = sem("w_high"), sem("w_split")
        unit_done = [sem("unit_done0"), sem("unit_done1")]
        h_split = sem("h_split")
        tokpad, ht_ready, htok_high, htok_ready = sem("tokpad"), sem("ht_ready"), sem("htok_high"), sem("htok_ready")
        sel_ready, cnt_ready, table_ready = sem("sel_ready"), sem("cnt_ready"), sem("table_ready")
        pick_ready, pickT_ready = sem("pick_ready"), sem("pickT_ready")
        gath_ready, gath_evac, gc_ready, gc_evac = sem("gath_ready"), sem("gath_evac"), sem("gc_ready"), sem("gc_evac")
        yt_ready, yc_ready, ytok_ready, y_high, y_split, sc_ready = (sem("yt_ready"), sem("yc_ready"), sem("ytok_ready"),
                                                                     sem("y_high"), sem("y_split"), sem("sc_ready"))
        gsum_ready, usum_ready, hid_ready32, hid_high = (sem("gsum_ready"), sem("usum_ready"), sem("hid_ready32"),
                                                         sem("hid_high"))
        g_half, u_half, y_half = sem("g_half"), sem("u_half"), sem("y_half")
        e_gated, iota_loaded = sem("e_gated"), sem("iota_loaded")
        ada_done = sem("ada_done")
        x_loaded = sem("x_loaded")
        consts_loaded = sem("consts_loaded")
        vrow_loaded = sem("vrow_loaded")
        memsets = sem("memsets")
        identb_ready = sem("identb_ready")
        xt_ready, xt_evac = sem("xt_ready"), sem("xt_evac")
        vt_ready, vt_evac = sem("vt_ready"), sem("vt_evac")
        csil_ready = sem("csil_ready")
        mod_ready = sem("mod_ready")
        sq_ready, ms_ready, v_ready, root_ready = sem("sq_ready"), sem("ms_ready"), sem("v_ready"), sem("root_ready")
        normed, h_ready = sem("normed"), sem("h_ready")
        x_upd = sem("x_upd")
        z_ready, z_evac = sem("z_ready"), sem("z_evac")
        past_loaded = sem("past_loaded")
        pool_mats_loaded = sem("pool_mats_loaded")
        poolw_zero, poolw_loaded = sem("poolw_zero"), sem("poolw_loaded")
        rope_done = sem("rope_done")
        lf_abs, lf_ln, logf_ready = sem("lf_abs"), sem("lf_ln"), sem("logf_ready")
        ti_ready, ti_evac = sem("ti_ready"), sem("ti_evac")
        is_ready, is_relu, is_acc = sem("is_ready"), sem("is_relu"), sem("is_acc")
        mask_ready = sem("mask_ready")
        g_ready, g_evac = sem("g_ready"), sem("g_evac")
        cum_ready, cum_evac = sem("cum_ready"), sem("cum_evac")
        pm_ready, pm_evac, po_ready, po_evac = sem("pm_ready"), sem("pm_evac"), sem("po_ready"), sem("po_evac")
        at_ready, at_evac_act, at_evac_dve = sem("at_ready"), sem("at_evac_act"), sem("at_evac_dve")
        s_ready, mx_ready, p_ready = sem("s_ready"), sem("mx_ready"), sem("p_ready")
        pt_ready, pt_evac, pv_done = sem("pt_ready"), sem("pt_evac"), sem("pv_done")
        o_evac, ot_ready, ot_evac = sem("o_evac"), sem("ot_ready"), sem("ot_evac")
        b_ready, b_evac, m_ready = sem("b_ready"), sem("b_evac"), sem("m_ready")
        r_ready = sem("r_ready")
        sg_ready, hid_ready = sem("sg_ready"), sem("hid_ready")
        rl_ready, gate_ready, gt_ready, gt_evac, gb_ready, gb_evac = (sem("rl_ready"), sem("gate_ready"), sem("gt_ready"),
                                                                      sem("gt_evac"), sem("gb_ready"), sem("gb_evac"))
        rexp_in, rexp_out = sem("rexp_in"), sem("rexp_out")
        y_ready, y_evac = sem("y_ready"), sem("y_evac")
        outs_done, y_sent = sem("outs_done"), sem("y_sent")
        act_chain, dve_chain = sem("act_chain"), sem("dve_chain")

        NZ = ZITER * ZBODY * TILES
        NATT = TILES * 2 * AH
        NTM = TILES * 2

        def xu(L, stage):
            base = sum(KD * (1 + HALVES) for l in range(L))
            return base + {"start": 0, "out": KD, "ffn": KD * (1 + HALVES)}[stage]

        fexp_base = [0, HALVES]

        items = [(t, m, h) for t in (SAMPLE, 0, 1, 2, 3) for m in range(2) for h in range(AH)]

        def key_blocks(t):
            if t == SAMPLE:
                return [(0, PAST, "past"), (PAST, DEC, SAMPLE)]
            return [(s * P, P, s) for s in range(t + 1)]

        at_groups = [("past", None)] + [(kind, t) for t in range(TILES) for kind in ("a", "bq", "bk")]
        at_on_act = [kind in ("a", "bk") for kind, _ in at_groups]
        N_AT = len(at_groups)
        N_AT_ACT = sum(at_on_act)
        N_AT_DVE = N_AT - N_AT_ACT

        def order(j):
            return 1 - j if j < 2 else j

        def ahead(it, b):
            j = b + 2 - (FB + KD)
            return (it, b + 2) if j < 0 else (it + 1, order(j))

        block = ctx.enter_context(nc.Block())

        @block.sync
        def _(sp):
            sp.dma_start(xin[:, 0:SAMPLE, :], t_in["x_prompt"][0].rearrange("(t p) d -> p t d", p=P)).then_inc(x_loaded, 16)
            sp.dma_start(xin[0:DEC, SAMPLE, :], t_in["x_sample"][0]).then_inc(x_loaded, 16)

            def fill(name, it, j, pieces, late=0):
                for kind, value in ring.free(name, it, j, late):
                    sp.wait_ge(block_begun if kind == "begun" else w_split, value)
                for dst, src in pieces:
                    sp.dma_start(dst, src).then_inc(slot_full[j % NSLOT], 16)

            def cols(j, w):
                return slots[:, j % NSLOT, 0:KD * w].rearrange("p (k n) -> p k n", k=KD)

            for L in range(DEPTH):
                ada = t_in["ada_w"][L].rearrange("(k p) n -> p k n", p=P)
                w_in = t_in["w_in"][L].rearrange("(k p) n -> p k n", p=P)
                w_br = [t_in[n][L].rearrange("(k p) n -> p k n", p=P) for n in ("w_br_a", "w_br_b", "w_br_c")]
                w_out = t_in["w_out"][L].rearrange("(k p) n -> p k n", p=P)

                def ada_fill(it):
                    for j in range(4):
                        fill(("ada", L), it, j, [(cols(j, 256), ada[:, :, ds(it * 1024 + j * 256, 256)])])

                if L == 0:
                    ada_fill(0)
                with sp.Fori(1 if L == 0 else 0, 6) as it:
                    if L == 0:
                        for j in range(4):
                            sp.wait_ge(block_begun, it * 4 + (j - 2))
                            sp.dma_start(cols(j, 256), ada[:, :, ds(it * 1024 + j * 256, 256)]).then_inc(slot_full[j], 16)
                    else:
                        ada_fill(it)
                with sp.Fori(0, ZITER) as it:
                    for j in range(ZBODY):
                        fill(("z", L), it, j, [(cols(j, ZB), w_in[:, :, ds(it * (ZBODY * ZB) + j * ZB, ZB)])])
                with sp.Fori(0, 3) as it:
                    for j in range(4):
                        fill(("gates", L), it, j, [(cols(j, 256), w_in[:, :, ds(it * 1024 + (GL + j * 256), 256)])])
                with sp.Fori(0, 2) as it:
                    for j in range(2):
                        dst = cols(j, 256)
                        fill(("branch", L), it, j,
                             [(dst[:, a:b, :], w_br[i][:, :, ds(it * 512 + j * 256, 256)])
                              for i, (a, b) in enumerate(((0, 3), (3, 6), (6, 8)))])
                with sp.Fori(0, 2) as it:
                    for j in range(2):
                        fill(("out", L), it, j, [(cols(j, 256), w_out[:, :, ds(it * 512 + j * 256, 256)])])
                def ffn_fill(it, e=None, blocks=range(FB + KD)):
                    for j in blocks:
                        slot = slots[:, j % NSLOT, :]
                        if j < FB:
                            gu = slot.rearrange("p (w k n) -> p w k n", w=2, k=KD)
                            if L == 0:
                                srcs = [t_in[n][0].rearrange("(k p) n -> p k n", p=P)[:, :, ds(it * FEXP + j * P, P)]
                                        for n in ("ffn_w_gate", "ffn_w_up")]
                            else:
                                srcs = [t_in[n][0, ds(e, 1)].rearrange("e (k p) n -> p (e k) n", p=P)[:, :, j * P:(j + 1) * P]
                                        for n in ("moe_w_gate", "moe_w_up")]
                            fill(("ffn", L), it, j, [(gu[:, w], srcs[w]) for w in range(2)], late=int(L == 1 and j == NSLOT))
                        else:
                            d0 = (j - FB) * P
                            dst = slot[:, 0:FB * P].rearrange("p (f n) -> p f n", f=FB)
                            if L == 0:
                                src = t_in["ffn_w_down"][0, ds(it * FEXP, FEXP)].rearrange("(f p) n -> p f n", p=P)
                            else:
                                src = t_in["moe_w_down"][0, ds(e, 1)].rearrange("e (f p) n -> p (e f) n", p=P)
                            fill(("ffn", L), it, j, [(dst, src[:, :, d0:d0 + P])])

                if L == 0:
                    for it in range(HALVES):
                        ffn_fill(it)
                else:
                    sp.wait_ge(table_ready, 1)
                    passes = sp.value_load(etab[0:1, MAX_PASS:MAX_PASS + 1], min_val=NEXP, max_val=MAX_PASS - 1)
                    with sp.Fori(0, passes) as it:
                        expert = sp.value_load(etab[0:1, ds(it, 1)], min_val=0, max_val=NEXP - 1)
                        ffn_fill(it, expert)
                    ffn_fill(passes, 0, range(2))
            sp.wait_ge(y_evac, 2 * TILES)
            sp.dma_start(t_out["y_prompt"][0].rearrange("(t p) d -> p t d", p=P), xin[:, 0:SAMPLE, :]).then_inc(y_sent, 16)
            sp.dma_start(t_out["y_sample"][0], xin[0:DEC, SAMPLE, :]).then_inc(y_sent, 16)
            sp.wait_ge(y_sent, 32)
            sp.wait_ge(outs_done, 160 * DEPTH)

        @block.gpsimd
        def _(pool):
            G = nc.gpsimd
            for L in range(DEPTH):
                for r, n, src in ((V_ADAB, 48, t_in["ada_b"][L]), (V_NMIX, 8, t_in["norm_mix_g"][L]),
                                  (V_NFFN, 8, t_in["norm_ffn_g"][L]), (V_PSC, 2, t_in["pool_scale"][L]),
                                  (V_FIN, 8, t_in["final_norm_g"]), (V_C, 8, t_in["c_prompt"][0]),
                                  (V_C + 8, 8, t_in["c_sample"][0])):
                    pool.dma_start(vrow[r:r + n, L, :], src.rearrange("(r n) -> r n", n=P)).then_inc(vrow_loaded, 16)
            for dst, src in ((ident, "c_ident"), (tri, "c_tri")):
                pool.dma_start(dst[:, :], t_in[src]).then_inc(consts_loaded, 16)
            pool.dma_start(cs[:, :, :, :].rearrange("p t a f -> p (t a f)"), t_in["c_rope"]).then_inc(consts_loaded, 16)
            pool.dma_start(bfb[:, :, :].rearrange("p l h -> p (l h)"),
                           t_in["b_forget"].rearrange("l h -> (l h)").partition_broadcast(P)).then_inc(consts_loaded, 16)
            pool.dma_start(rb[:, :], t_in["moe_router_b"][0].partition_broadcast(P)).then_inc(consts_loaded, 16)
            pool.dma_start(rw[:, :, :], t_in["moe_router_w"][0].rearrange("(k p) e -> p k e", p=P)).then_inc(consts_loaded, 16)
            for L in range(DEPTH):
                if L:
                    pool.wait_ge(ot_evac, L * NTM)
                pool.dma_start(past[:, 0:192], t_in["cache_a_kvi"][L, 0].rearrange("t c d -> t (c d)")).then_inc(past_loaded, 16)
                pool.dma_start(past[:, 192:960], t_in["cache_b_kv"][L, 0].rearrange("t c h d -> t (c h d)")).then_inc(past_loaded, 16)
                pool.dma_start(past[:, 960:966], t_in["cache_b_logf"][L, 0]).then_inc(past_loaded, 16)
                pool.dma_start(poolm, t_in["c_pool"]).then_inc(pool_mats_loaded, 16)
                pool.wait_ge(rope_done, 6 * (L + 1))
                pool.wait_ge(logf_ready, L + 1)
                pool.wait_ge(z_evac, NZ * (L + 1))
                for pre, zz, nt in (("p", z[:, 0:SAMPLE, :], SEQ), ("s", z[0:DEC, SAMPLE:TILES, :], DEC)):
                    p = min(nt, P)

                    def rows(name):
                        a = t_out[name][L, 0]
                        return a

                    kvi = rows("a_kvi_" + pre).rearrange("(t p) c d -> p t (c d)", p=p)
                    pool.dma_start(kvi[:, :, 0:2 * HD], zz[:, :, AK:AK + 2 * HD]).then_inc(outs_done, 16)
                    pool.dma_start(kvi[:, :, 2 * HD:], zz[:, :, IK:IK + HD]).then_inc(outs_done, 16)
                    pool.dma_start(rows("b_kv_" + pre).rearrange("(t p) c h d -> p t (c h d)", p=p),
                                   zz[:, :, BK:BK + 2 * BH * HD]).then_inc(outs_done, 16)
                    lf = logf[:, 0:SAMPLE, :] if nt == SEQ else logf[0:DEC, SAMPLE:TILES, :]
                    pool.dma_start(rows("logf_" + pre).rearrange("(t p) h -> p t h", p=p), lf).then_inc(outs_done, 16)
                    last = nt // P - 1 if nt == SEQ else 0
                    pool.dma_start(rows("pool_" + pre), zz[p - HIST:p, last, CU:CU + PW]).then_inc(outs_done, 16)
                pool.wait_ge(is_ready, 16 * (L + 1))
                pool.memset(qk[0:HD, 512:1024], 0.0).then_inc(poolw_zero, 1)
                pool.dma_start(hist, t_in["state_c_pool"][L, 0]).then_inc(poolw_loaded, 16)
                pool.wait_ge(poolw_zero, L + 1)
                for g in range(4):
                    pool.dma_start(poolw[:, g, (g % 2) * HD:(g % 2 + 1) * HD], t_in["pool_w"][L, g]).then_inc(poolw_loaded, 16)
            pool.wait_ge(ot_evac, DEPTH * NTM)
            pool.dma_start(iota[:, :], t_in["c_iota"]).then_inc(iota_loaded, 16)
            pool.wait_ge(table_ready, 1)
            passes = pool.value_load(etab[0:1, MAX_PASS:MAX_PASS + 1], min_val=NEXP, max_val=MAX_PASS - 1)
            with pool.Fori(0, passes) as it:
                pool.wait_ge(gc_evac, it + 1)
                for f in range(FB):
                    pool.wait_ge(sg_ready, it * FB + (2 * FB + f + 1))
                    G.tensor_tensor(sge[f % 2], sge[f % 2], gcomp, ALU.mult).then_inc(e_gated, 1)
                    pool.wait_ge(hid_high, it * FB + (f + 1))
                    G.tensor_tensor(hidE[:, f, 1, :], hide[f % 2], hidE[:, f, 0, :].bitcast(FP), ALU.subtract)\
                        .then_inc(hid_ready, 1)

        @block.tensor
        def _(pe):
            mm = nc.tensor.matmul

            def landed(name, it, j):
                pe.wait_ge(slot_full[j % NSLOT], ring.full(name, it, j))

            pe.wait_ge(consts_loaded, 96)
            pe.wait_ge(x_loaded, 32)
            for t in range(TILES):
                for g in range(2):
                    i = 2 * t + g
                    if i >= 8:
                        pe.wait_ge(xt_evac, i - 7)
                    for q in range(4):
                        last = nc.tensor.transpose(ps[:, i % 8, q * P:q * P + ROWS[t]],
                                                   xin[0:ROWS[t], t, (4 * g + q) * P:(4 * g + q + 1) * P],
                                                   ident[0:ROWS[t], 0:ROWS[t]])
                    last.then_inc(xt_ready, 1)
            pe.wait_ge(vrow_loaded, 16 * 14)
            pe.wait_ge(xt_evac, 10)
            for L in range(DEPTH):
                last = nc.tensor.transpose(ps[:, L, 0:V_ROWS], vrow[0:V_ROWS, L, :], ident[0:V_ROWS, 0:V_ROWS])
            last.then_inc(vt_ready, 1)
            pe.wait_ge(memsets, 1)

            def norm_sums(n, releases=False):
                for k in range(KD):
                    pe.wait_ge(sq_ready, KD * n + k + 1)
                    for h in range(2):
                        last = mm(ps[:, h, 0:HALF], ones[:, :], sqs[n % 2][:, k, h * HALF:(h + 1) * HALF],
                                  start=(k == 0), stop=(k == KD - 1))
                        if releases and k == h == 0:
                            last.then_inc(block_begun, 1)
                last.then_inc(ms_ready, 1)

            def features(out_pair, lhs, rhs, nk, begins=False, each=None):
                for k in range(nk):
                    if each:
                        each(k)
                    for h in range(2):
                        last = mm(ps[:, 2 * out_pair + h, 0:HALF], lhs(k), rhs(k)[:, h * HALF:(h + 1) * HALF],
                                  start=(k == 0), stop=(k == nk - 1))
                        if begins and k == h == 0:
                            last.then_inc(block_begun, 1)
                return last

            for L in range(DEPTH):
                if L == 0:
                    pe.wait_ge(csil_ready, 1)
                else:
                    pe.wait_ge(x_upd, xu(L - 1, "ffn"))
                with pe.Fori(0, 6) as it:
                    for j in range(4):
                        landed(("ada", L), it, j)
                        w = slots[:, j, :].rearrange("p (k n) -> p k n", k=KD)
                        for f in range(2):
                            for k in range(KD):
                                last = mm(ps[:, 7, ds(it * 16 + (j * 4 + f * 2), 2)], w[:, k, f * P:(f + 1) * P],
                                          csil[:, :, k], start=(k == 0), stop=(k == KD - 1))
                                if f == k == 0:
                                    last.then_inc(block_begun, 1)
                        last.then_inc(ada_done, 1)
                norm_sums(2 * L)
                pe.wait_ge(h_ready, KD * (2 * L + 1))
                with pe.Fori(0, ZITER) as it:
                    for j in range(ZBODY):
                        landed(("z", L), it, j)
                        w = slots[:, j, 0:KD * ZB].rearrange("p (k n) -> p k n", k=KD)
                        for t in range(TILES):
                            g = j * TILES + t
                            if g >= TILES - 1:
                                pe.wait_ge(z_evac, it * (ZBODY * TILES) + (NZ * L + g - TILES + 2))
                            for k in range(KD):
                                last = mm(ps[0:ROWS[t], t, 0:ZB], hT[:, k, tok(t)], w[:, k, :],
                                          start=(k == 0), stop=(k == KD - 1))
                                if t == k == 0:
                                    last.then_inc(block_begun, 1)
                            last.then_inc(z_ready, 1)
                    pe.wait_ge(z_evac, it * (ZBODY * TILES) + (NZ * L + ZBODY * TILES - 1))
                pe.wait_ge(z_evac, NZ * (L + 1))
                pe.wait_ge(rope_done, 6 * (L + 1))
                pe.wait_ge(past_loaded, 48 * (L + 1))

                nc.tensor.transpose(ps[0:HD, 5, 0:P], past[:, 128:192], ident[:, :]).then_inc(ti_ready, 1)
                for t in range(TILES):
                    r = ROWS[t]
                    for b in range(2):
                        nc.tensor.transpose(ps[:, t, b * P:b * P + r], z[0:r, t, IQ + b * P:IQ + (b + 1) * P],
                                            ident[0:r, 0:r])
                    nc.tensor.transpose(ps[0:HD, t, 256:256 + r], z[0:r, t, IK:IK + HD], ident[0:r, 0:r])\
                        .then_inc(ti_ready, 1)
                pe.wait_ge(ti_evac, 6 * (L + 1))
                q = 0
                for t in range(1, TILES):
                    for h in range(IH):
                        if q >= 4:
                            pe.wait_ge(is_relu, 16 * L + q - 3)
                        p0 = (h % 2) * HD
                        mm(ps[0:ROWS[t], q % 4, 0:KW[t]], iqT[p0:p0 + HD, h // 2, tok(t)],
                           ikT[p0:p0 + HD, KCOL[t]:KCOL[t] + KW[t]], start=True, stop=True).then_inc(is_ready, 1)
                        q += 1
                pe.wait_ge(is_relu, 16 * (L + 1))
                with pe.Fori(0, 3) as it:
                    for j in range(4):
                        landed(("gates", L), it, j)
                        w = slots[:, j, :].rearrange("p (k n) -> p k n", k=KD)
                        for f in range(2):
                            g = 2 * j + f
                            if g >= 3:
                                pe.wait_ge(g_evac, it * 8 + (24 * L + g - 2))
                            last = features(g % 4, lambda k: w[:, k, f * P:(f + 1) * P], lambda k: hT[:, k, :], KD, f == 0)
                            last.then_inc(g_ready, 1)
                    pe.wait_ge(g_evac, it * 8 + (24 * L + 7))
                pe.wait_ge(g_evac, 24 * (L + 1))
                pe.wait_ge(logf_ready, L + 1)
                for t in range(SAMPLE):
                    for s in range(t + 1):
                        mm(ps[0:BH, 6, t * P:(t + 1) * P], logf[:, s, :], (tri if s == t else ones)[:, :],
                           start=(s == 0), stop=(s == t))
                plf = past[:, 960:966]
                mm(ps[0:BH, 7, 0:PAST], plf, tri[:, :], start=True, stop=True)
                mm(ps[0:BH, 7, PAST:PAST + DEC], plf, ones[:, 0:DEC], start=True, stop=False)
                mm(ps[0:BH, 7, PAST:PAST + DEC], logf[:, SAMPLE, :], tri[:, 0:DEC], start=False, stop=True)\
                    .then_inc(cum_ready, 1)
                pe.wait_ge(pool_mats_loaded, 16 * (L + 1))
                pe.wait_ge(poolw_loaded, 80 * (L + 1))
                for t in range(TILES):
                    r = ROWS[t]
                    for g in range(4):
                        c0 = CU + g * HD
                        o = ps[0:HD, t, g * P:g * P + r]
                        if t == SAMPLE:
                            mm(o, hist[:, g * HD:(g + 1) * HD], poolm[0:HIST, 3, P + g * DEC:P + (g + 1) * DEC],
                               start=True, stop=False)
                            last = mm(o, z[0:DEC, t, c0:c0 + HD], poolm[0:DEC, 3, g * DEC:(g + 1) * DEC],
                                      start=False, stop=True)
                            continue
                        last = mm(o, z[:, t, c0:c0 + HD], poolm[:, 1 if t == 0 else 0, g * P:(g + 1) * P],
                                  start=True, stop=(t == 0))
                        if t:
                            last = mm(o, z[:, t - 1, c0:c0 + HD], poolm[:, 2, g * P:(g + 1) * P],
                                      start=False, stop=True)
                    last.then_inc(pm_ready, 1)
                for t in range(TILES):
                    r = ROWS[t]
                    pe.wait_ge(pm_evac, TILES * L + t + 1)
                    if t:
                        pe.wait_ge(po_evac, TILES * L + t)
                    for pr in range(2):
                        for i in range(2):
                            g = 2 * pr + i
                            last = mm(ps[:, 5, pr * P:pr * P + r], poolw[:, g, :], pooled[:, g * P:g * P + r],
                                      start=(i == 0), stop=(i == 1))
                    last.then_inc(po_ready, 1)
                pe.wait_ge(po_evac, TILES * (L + 1))
                pe.wait_ge(cum_evac, L + 1)
                for i, (kind, t) in enumerate(at_groups):
                    if i >= 8:
                        if at_on_act[i - 8]:
                            pe.wait_ge(at_evac_act, N_AT_ACT * L + sum(at_on_act[:i - 7]))
                        else:
                            pe.wait_ge(at_evac_dve, N_AT_DVE * L + (i - 7) - sum(at_on_act[:i - 7]))
                    b = i % 8
                    if kind == "past":
                        nc.tensor.transpose(ps[0:HD, b, 0:P], past[:, 0:HD], ident[:, :])
                        src = [past[:, 192 + q * P:192 + (q + 1) * P] for q in range(3)]
                        first, r = 1, P
                    else:
                        r = ROWS[t]
                        c0 = {"a": AQ, "bq": BQ, "bk": BK}[kind]
                        src = [z[0:r, t, c0 + q * P:c0 + (q + 1) * P] for q in range(3)]
                        first = 0
                        if kind == "a":
                            nc.tensor.transpose(ps[0:HD, b, 3 * P:3 * P + r], z[0:r, t, AK:AK + HD], ident[0:r, 0:r])
                    for q, s in enumerate(src):
                        last = nc.tensor.transpose(ps[:, b, (first + q) * P:(first + q) * P + r], s, ident[0:r, 0:r])
                    last.then_inc(at_ready, 1)
                pe.wait_ge(at_evac_act, N_AT_ACT * (L + 1))
                pe.wait_ge(at_evac_dve, N_AT_DVE * (L + 1))
                pe.wait_ge(mask_ready, 4 * (L + 1))
                pe.wait_ge(identb_ready, 1)
                base = NATT * L
                for i in range(NATT + 4):
                    if i < NATT:
                        t, m, h = items[i]
                        r, w = ROWS[t], KW[t]
                        if i >= 3:
                            pe.wait_ge(p_ready, base + i - 2)
                        p0 = (h % 2) * HD
                        qT, kT = (aqT[p0:p0 + HD, h // 2], akT[p0:p0 + HD, :]) if m == 0 else \
                                 (bqT[p0:p0 + HD, h // 2], bkT[p0:p0 + HD, h // 2])
                        out = ps[0:r, i % 3, 0:w]
                        mm(out, qT[:, tok(t)], kT[:, KCOL[t]:KCOL[t] + w], start=True, stop=False)
                        if m == 0:
                            last = mm(out, identb[0:r, 0:r], amask[0:r, MOFF[t]:MOFF[t] + w], start=False, stop=True)
                        else:
                            mm(out, ident[0:BH, h:h + 1].to_broadcast([BH, r]), negcum[:, KCOL[t]:KCOL[t] + w],
                               start=False, stop=False)
                            last = mm(ps[0:r, i % 3, w - r:w], identb[0:r, 0:r], cmask[0:r, 0:r], start=False, stop=True)
                        last.then_inc(s_ready, 1)
                    j = i - 1
                    if 0 <= j < NATT:
                        t, m, h = items[j]
                        pe.wait_ge(p_ready, base + j + 1)
                        if j >= 2:
                            pe.wait_ge(pt_evac, base + j - 1)
                        r = ROWS[t]
                        for b, (c0, kr, _) in enumerate(key_blocks(t)):
                            last = nc.tensor.transpose(ps[0:kr, 3 + j % 2, b * P:b * P + r],
                                                       probs[j % 2][0:r, c0:c0 + kr], ident[0:r, 0:r])
                        last.then_inc(pt_ready, 1)
                    j = i - 2
                    if 0 <= j < NATT:
                        t, m, h = items[j]
                        tm = j // AH
                        pe.wait_ge(pt_evac, base + j + 1)
                        if h == 0 and tm >= 2:
                            pe.wait_ge(o_evac, NTM * L + tm - 1)
                        blocks = key_blocks(t)
                        for b, (c0, kr, src) in enumerate(blocks):
                            if src == "past":
                                v = past[:, HD:2 * HD] if m == 0 else past[:, 576 + h * HD:576 + (h + 1) * HD]
                            else:
                                c = AV if m == 0 else BV + h * HD
                                v = z[0:kr, src, c:c + HD]
                            last = mm(ps[0:ROWS[t], 5 + tm % 2, h * HD:(h + 1) * HD], probsT[j % 2][0:kr, b * P:b * P + ROWS[t]],
                                      v, start=(b == 0), stop=(b == len(blocks) - 1))
                        last.then_inc(pv_done, 1)
                    j = i - 3
                    if 0 <= j < NATT and j % AH == AH - 1:
                        t, m, h = items[j]
                        tm = j // AH
                        pe.wait_ge(o_evac, NTM * L + tm + 1)
                        if tm:
                            pe.wait_ge(ot_evac, NTM * L + tm)
                        r = ROWS[t]
                        c = BQ if m else AQ
                        for q in range(3):
                            last = nc.tensor.transpose(ps[:, 7, q * P:q * P + r], z[0:r, t, c + q * P:c + (q + 1) * P],
                                                       ident[0:r, 0:r])
                        last.then_inc(ot_ready, 1)
                pe.wait_ge(ot_evac, NTM * (L + 1))
                with pe.Fori(0, 2) as it:
                    for j in range(2):
                        landed(("branch", L), it, j)
                        w = slots[:, j, :].rearrange("p (k n) -> p k n", k=KD)
                        for f in range(2):
                            for i, (a, b) in enumerate(((0, 3), (3, 6), (6, 8))):
                                g = (2 * j + f) * 3 + i
                                if g >= 3:
                                    pe.wait_ge(b_evac, it * 12 + (24 * L + g - 2))
                                last = features(g % 4, lambda k: w[:, a + k, f * P:(f + 1) * P],
                                                lambda k: oT[:, a + k, :], b - a, f == i == 0)
                                last.then_inc(b_ready, 1)
                    pe.wait_ge(b_evac, it * 12 + (24 * L + 11))
                pe.wait_ge(b_evac, 24 * (L + 1))
                with pe.Fori(0, 2) as it:
                    pe.wait_ge(m_ready, KD * (L + 1))
                    for j in range(2):
                        landed(("out", L), it, j)
                        w = slots[:, j, :].rearrange("p (k n) -> p k n", k=KD)
                        for f in range(2):
                            g = 2 * j + f
                            if g == 3:
                                pe.wait_ge(x_upd, it * 4 + (xu(L, "start") + 1))
                            last = features(g, lambda k: w[:, k, f * P:(f + 1) * P], lambda k: gT[:, k, :], KD, f == 0)
                            last.then_inc(r_ready, 1)
                    pe.wait_ge(x_upd, it * 4 + (xu(L, "start") + 3))
                pe.wait_ge(x_upd, xu(L, "out"))
                norm_sums(2 * L + 1, releases=True)
                pe.wait_ge(h_ready, KD * (2 * L + 2))
                if L == 1:
                    for t in range(TILES):
                        for k in range(KD):
                            last = mm(ps[0:ROWS[t], 4, t * NEXP:(t + 1) * NEXP], hT[:, k, tok(t)], rw[:, k, :],
                                      start=(k == 0), stop=(k == KD - 1))
                    last.then_inc(rl_ready, 1)
                    for i in range(2 * TILES):
                        t, g = i // 2, i % 2
                        if i >= 4:
                            pe.wait_ge(htok_ready, i - 3)
                        for q in range(4):
                            last = nc.tensor.transpose(ps[0:ROWS[t], i % 4, q * P:(q + 1) * P], hT[:, 4 * g + q, tok(t)],
                                                       ident[:, :])
                        last.then_inc(ht_ready, 1)
                    pe.wait_ge(sel_ready, 1)
                    for t in range(TILES):
                        for q in range(t + 1):
                            mm(ps[:, 5, t * NEXP:(t + 1) * NEXP], (tri if q == t else ones)[:, :], rt[3][:, q, :],
                               start=(q == 0), stop=(q == t))
                    for t in range(TILES):
                        last = mm(ps[:, 5, TILES * NEXP:(TILES + 1) * NEXP], ones[:, :], rt[3][:, t, :],
                                  start=(t == 0), stop=(t == TILES - 1))
                    last.then_inc(cnt_ready, 1)
                    pe.wait_ge(gate_ready, 1)
                    for t in range(TILES):
                        bank, c0 = (6, t * P) if t < SAMPLE else (7, 0)
                        last = nc.tensor.transpose(ps[0:NEXP, bank, c0:c0 + ROWS[t]], rowno[0:ROWS[t], t, :],
                                                   ident[0:ROWS[t], 0:ROWS[t]])
                    last.then_inc(gt_ready, 1)
                    pe.wait_ge(gt_evac, 1)
                    pe.wait_ge(htok_ready, 2 * TILES)
                    for e in range(NEXP):
                        if e >= 2:
                            pe.wait_ge(gb_evac, e - 1)
                        for h in range(2):
                            last = mm(ps[:, 2 * (e % 2) + h, 0:HALF], ident[0:NEXP, e:e + 1].to_broadcast([NEXP, P]),
                                      rowT[:, h * HALF:(h + 1) * HALF], start=True, stop=True)
                        last.then_inc(gb_ready, 1)
                    pe.wait_ge(gb_evac, NEXP)
                    pe.wait_ge(table_ready, 1)
                    passes = pe.value_load(etab[0:1, MAX_PASS:MAX_PASS + 1], min_val=NEXP, max_val=MAX_PASS - 1)
                    U = 2 * (FB + KD)
                    w0 = HALVES * U

                    def gather(n):
                        pe.wait_ge(pick_ready, n + 1)
                        for k in range(KD):
                            b = 4 + k % 2
                            if k == 0:
                                pe.wait_ge(x_upd, (n - 1) * KD + xu(L, "out") if not isinstance(n, int) else xu(L, "out"))
                            if k >= 2:
                                pe.wait_ge(gath_evac, n * KD + (k - 1))
                            for part in range(2):
                                for t in range(TILES):
                                    last = mm(ps[:, b, part * CAP:(part + 1) * CAP], hTok[:, part, t, k * P:(k + 1) * P],
                                              pick[:, t, :], start=(t == 0), stop=(t == TILES - 1))
                            last.then_inc(gath_ready, 1)
                        for t in range(TILES):
                            last = mm(ps[:, 6, 0:CAP], gcol[:, t:t + 1].to_broadcast([P, P]), pick[:, t, :].bitcast(FP),
                                      start=(t == 0), stop=(t == TILES - 1))
                        last.then_inc(gc_ready, 1)

                    gather(0)
                    with pe.Fori(0, passes) as it:

                        def unit(bank, j, w, nk, rhs, first, final):
                            u = 2 * j + w
                            pe.wait_ge(w_split, it * U + (w0 + 2 * order(j) + w + 1))
                            for k in range(nk):
                                a, b = first and k == 0, final and k == nk - 1
                                parts = [(0, 2 * CAP), (1, CAP)]
                                for part, n in parts[::-1] if b else parts:
                                    last = mm(ps[:, bank, 0:n], wE[u % NWB][:, part, k * P:(k + 1) * P],
                                              rhs(k).rearrange("p a n -> p (a n)")[:, 0:n],
                                              start=a and part == 0, stop=b and part == 0)
                            last.then_inc(unit_done[0], 1)

                        pe.wait_ge(gath_evac, (it + 1) * KD)
                        for f in range(FB):
                            if f >= 2:
                                pe.wait_ge(gsum_ready, it * FB + (f - 1))
                            unit(f % 2, f, 0, KD, lambda k: hg[:, k], True, True)
                            if f >= 2:
                                pe.wait_ge(usum_ready, it * FB + (f - 1))
                            unit(2 + f % 2, f, 1, KD, lambda k: hg[:, k], True, True)
                        gather(it + 1)
                        pe.wait_ge(hid_ready, it * FB + 3 * FB)

                        def to_tokens(d):
                            pe.wait_ge(yc_ready, it * KD + (d + 1))
                            if d >= 2:
                                pe.wait_ge(y_split, it * KD + (d - 1))
                            for c in range(2):
                                last = nc.tensor.transpose(ps[0:CH, 2 + d % 2, c * P:(c + 1) * P],
                                                           yT[:, d % 2, c * CH:(c + 1) * CH], ident[:, :])
                            last.then_inc(ytok_ready, 1)

                        def scatter(d):
                            pe.wait_ge(y_split, it * KD + (d + 1))
                            if d == 0:
                                pe.wait_ge(pickT_ready, it + 1)
                                pe.wait_ge(gath_evac, (it + 1) * KD + KD)
                                pe.wait_ge(gc_evac, it + 2)
                            if d >= 2:
                                pe.wait_ge(x_upd, it * KD + (xu(L, "out") + d - 1))
                            for h in range(2):
                                i = 0
                                for c in range(2):
                                    for part in range(2):
                                        last = mm(ps[:, 4 + 2 * (d % 2) + h, 0:HALF], yR[:, d % 2, part, c, :],
                                                  pickT[:, c, h * HALF:(h + 1) * HALF], start=(i == 0), stop=(i == 3))
                                        i += 1
                            last.then_inc(sc_ready, 1)

                        for d in range(KD + 2):
                            if d < KD:
                                if d >= 2:
                                    pe.wait_ge(yc_ready, it * KD + (d - 1))
                                unit(d % 2, FB + d, 0, FLO, lambda k: hidE[:, k], True, False)
                                unit(d % 2, FB + d, 1, FB - FLO, lambda k: hidE[:, FLO + k], False, True)
                            if 1 <= d <= KD:
                                to_tokens(d - 1)
                            if d >= 2:
                                scatter(d - 2)
                    continue
                pe.wait_ge(h_split, KD * (L + 1))
                if L == 0:
                    pe.wait_ge(m_ready, KD)

                def split_product(out_pair, buf, nk, rhs, first, last_part, each=None):
                    for k in range(nk):
                        if each:
                            each(k)
                        for h in range(2):
                            c = slice(h * HALF, (h + 1) * HALF)
                            for i, (a, b) in enumerate(((0, 0), (0, 1), (1, 0))):
                                last = mm(ps[:, 2 * out_pair + h, 0:HALF], wR[:, buf, a, k * P:(k + 1) * P], rhs(k, b)[:, c],
                                          start=(first and k == 0 and i == 0), stop=(last_part and k == nk - 1 and i == 2))
                    last.then_inc(unit_done[buf], 1)

                with pe.Fori(0, HALVES) as it:
                    n0 = fexp_base[L]
                    units = 2 * (FB + KD)

                    def unit_split(j, w):
                        pe.wait_ge(w_split, it * units + (n0 * units + 2 * j + w + 1))

                    for f in range(FB):
                        q = 2 * (f % 2)
                        if f < 2:
                            pe.wait_ge(x_upd, it * KD + (xu(L, "out") - (1 if f == 0 else 0)))
                        else:
                            pe.wait_ge(sg_ready, it * FB + (n0 * FB + f - 1))
                        unit_split(f, 0)
                        split_product(q, 0, KD, lambda k, b: hR[:, b, k, :], True, True)
                        if f == 0:
                            pe.wait_ge(x_upd, it * KD + xu(L, "out"))
                        if f >= 2:
                            pe.wait_ge(hid_ready, it * FB + (n0 * FB + f - 1))
                        unit_split(f, 1)
                        split_product(q + 1, 1, KD, lambda k, b: hR[:, b, k, :], True, True)
                    for d in range(KD):
                        if d < 2:
                            pe.wait_ge(hid_ready, it * FB + (n0 * FB + FB - 1))
                        elif d >= 4:
                            pe.wait_ge(x_upd, it * KD + (xu(L, "out") + d - 3))

                        def hid_there(k):
                            if d == 0 and k == FB - FLO - 1:
                                pe.wait_ge(hid_ready, it * FB + (n0 * FB + FB))

                        unit_split(FB + d, 0)
                        split_product((d + 2) % 4, 0, FLO, lambda k, b: hidR[:, b, k, :], True, False)
                        unit_split(FB + d, 1)
                        split_product((d + 2) % 4, 1, FB - FLO, lambda k, b: hidR[:, b, FLO + k, :], False, True, hid_there)
            pe.wait_ge(x_upd, passes * KD + xu(DEPTH - 1, "out"))
            norm_sums(2 * DEPTH)
            pe.wait_ge(h_ready, KD * (2 * DEPTH + 1))
            for t in range(TILES):
                for g in range(2):
                    i = 2 * t + g
                    if i >= 8:
                        pe.wait_ge(y_evac, i - 7)
                    for q in range(4):
                        last = nc.tensor.transpose(ps[0:ROWS[t], i % 8, q * P:(q + 1) * P], hT[:, 4 * g + q, tok(t)],
                                                   ident[:, :])
                    last.then_inc(y_ready, 1)

        @block.scalar
        def _(act):
            ch = Chain(act, act_chain)
            A = nc.scalar.activation

            for t in range(TILES):
                for g in range(2):
                    act.wait_ge(xt_ready, 2 * t + g + 1)
                    A(xT[:, 4 * g:4 * g + 4, tok(t)],
                      ps[:, (2 * t + g) % 8, :].rearrange("p (q n) -> p q n", q=4)[:, :, 0:ROWS[t]], ACT.Copy)\
                        .then_inc(xt_evac, 1)
            act.wait_ge(vt_evac, 1)
            A(csil[:, :, :], vecT[:, 0, V_C:V_C + 16].rearrange("p (s k) -> p s k", s=2), ACT.Silu).then_inc(csil_ready, 1)

            def norm(n, x_there, gain, shift, stage_mod):
                for k in range(KD):
                    if x_there is not None:
                        act.wait_ge(x_upd, x_there + k + 1)
                    elif k == 0:
                        act.wait_ge(xt_evac, 10)
                    A(sqs[n % 2][:, k, :], xT[:, k, :], ACT.Square).then_inc(sq_ready, 1)
                act.wait_ge(v_ready, n + 1)
                A(oT[:, 1, :], oT[:, 0, :], ACT.Sqrt).then_inc(root_ready, 1)
                if stage_mod:
                    act.wait_ge(mod_ready, stage_mod)
                for k in range(KD):
                    act.wait_ge(normed, KD * n + k + 1)
                    for s, c in ((0, slice(0, SEQ)), (1, slice(SEQ, NTOK))):
                        if shift is None:
                            last = A(hT[:, k, c], hT[:, k, c], ACT.Copy, scale=gain(k, s))
                        else:
                            last = A(hT[:, k, c], hT[:, k, c], ACT.Identity, scale=gain(k, s), bias=shift(k, s))
                    last.then_inc(h_ready, 1)

            for L in range(DEPTH):
                norm(2 * L, xu(L - 1, "ffn") - KD if L else None, lambda k, s: scl[:, 0, k, s:s + 1],
                     lambda k, s: mod[:, M_SH1 + k, s:s + 1], L + 1)
                with act.Fori(0, ZITER) as it:
                    for j in range(ZBODY):
                        for t in range(TILES):
                            act.wait_ge(z_ready, it * (ZBODY * TILES) + (NZ * L + j * TILES + t + 1))
                            A(z[0:ROWS[t], t, ds(it * (ZBODY * ZB) + j * ZB, ZB)], ps[0:ROWS[t], t, 0:ZB], ACT.Copy)\
                                .then_inc(z_evac, 1)
                act.wait_ge(lf_abs, L + 1)
                ch.link(A(lft[:, 2], lft[:, 1], ACT.Exp, scale=-1.0))
                A(lft[:, 2], lft[:, 2], ACT.Ln, bias=1.0).then_inc(lf_ln, 1)
                act.wait_ge(ti_ready, 6 * L + 1)
                A(ikT[0:HD, SEQ:SEQ + PAST], ps[0:HD, 5, 0:P], ACT.Copy)
                A(ikT[HD:P, SEQ:SEQ + PAST], ps[0:HD, 5, 0:P], ACT.Copy).then_inc(ti_evac, 1)
                for t in range(TILES):
                    act.wait_ge(ti_ready, 6 * L + t + 2)
                    A(iqT[:, :, tok(t)], ps[:, t, 0:256].rearrange("p (b n) -> p b n", b=2)[:, :, 0:ROWS[t]], ACT.Copy)
                    A(ikT[0:HD, keycol(t)], ps[0:HD, t, 256:256 + ROWS[t]], ACT.Copy)
                    A(ikT[HD:P, keycol(t)], ps[0:HD, t, 256:256 + ROWS[t]], ACT.Copy).then_inc(ti_evac, 1)
                q = 0
                for t in range(1, TILES):
                    for h in range(IH):
                        act.wait_ge(is_ready, 16 * L + q + 1)
                        if q >= 2:
                            act.wait_ge(is_acc, 16 * L + q - 1)
                        A(rel[q % 2][0:ROWS[t], 0:KW[t]], ps[0:ROWS[t], q % 4, 0:KW[t]], ACT.Relu).then_inc(is_relu, 1)
                        q += 1
                with act.Fori(0, 3) as it:
                    for g in range(8):
                        act.wait_ge(g_ready, it * 8 + (24 * L + g + 1))
                        A(gT[:, ds(it * 8 + g, 1), :].rearrange("p e (a n) -> p (e a) n", a=2), pair(g % 4), ACT.Sigmoid)\
                            .then_inc(g_evac, 1)
                for i, (kind, t) in enumerate(at_groups):
                    if not at_on_act[i]:
                        continue
                    act.wait_ge(at_ready, N_AT * L + i + 1)
                    src = ps[:, i % 8, :].rearrange("p (q n) -> p q n", q=4)[:, :, 0:ROWS[t]]
                    if kind == "a":
                        A(aqT[:, :, tok(t)], src[:, 0:3, :], ACT.Copy, scale=HD ** -0.5)
                        A(akT[0:HD, keycol(t)], src[0:HD, 3, :], ACT.Copy)
                        A(akT[HD:P, keycol(t)], src[0:HD, 3, :], ACT.Copy).then_inc(at_evac_act, 1)
                    else:
                        A(bkT[:, :, keycol(t)], src[:, 0:3, :], ACT.Copy).then_inc(at_evac_act, 1)
                base = NATT * L

                def ot_copy(j):
                    t, m, h = items[j]
                    tm = j // AH
                    act.wait_ge(ot_ready, NTM * L + tm + 1)
                    A(oT[:, 3 * m:3 * m + 3, tok(t)],
                      ps[:, 7, 0:384].rearrange("p (q n) -> p q n", q=3)[:, :, 0:ROWS[t]], ACT.Copy).then_inc(ot_evac, 1)

                for i in range(NATT):
                    t, m, h = items[i]
                    r, w = ROWS[t], KW[t]
                    tm = i // AH
                    act.wait_ge(mx_ready, base + i + 1)
                    if i >= 2:
                        act.wait_ge(pt_ready, base + i - 1)
                    if h == 0 and tm >= 2:
                        act.wait_ge(o_evac, NTM * L + tm - 1)
                    A(probs[i % 2][0:r, 0:w], ps[0:r, i % 3, 0:w], ACT.Exp, bias=nmax[0:r, i % 12:i % 12 + 1],
                      accum_out=rsum[0:r, tm % 2, h:h + 1]).then_inc(p_ready, 1)
                    if i >= 4 and (i - 4) % AH == AH - 1:
                        ot_copy(i - 4)
                ot_copy(NATT - 1)
                norm(2 * L + 1, xu(L, "start"), lambda k, s: scl[:, 1, k, s:s + 1],
                     lambda k, s: mod[:, M_SH2 + k, s:s + 1], 0)
                if L == 1:
                    act.wait_ge(rexp_in, 1)
                    A(rt[5], rt[5], ACT.Exp).then_inc(rexp_out, 1)
                    for i in range(2 * TILES):
                        t, g = i // 2, i % 2
                        act.wait_ge(ht_ready, i + 1)
                        if t == SAMPLE:
                            act.wait_ge(tokpad, 1)
                        A(hTok[0:ROWS[t], 0, t, g * 512:(g + 1) * 512], ps[0:ROWS[t], i % 4, :], ACT.Copy)\
                            .then_inc(htok_high, 1)
                    act.wait_ge(gt_ready, 1)
                    A(rowT[:, 0:SEQ], ps[0:NEXP, 6, :], ACT.Copy)
                    A(rowT[:, SEQ:NTOK], ps[0:NEXP, 7, 0:DEC], ACT.Copy).then_inc(gt_evac, 1)
                    for e in range(NEXP):
                        act.wait_ge(gb_ready, e + 1)
                        A(halves(rbc[:, e, :]), pair(e % 2), ACT.Copy).then_inc(gb_evac, 1)
                    act.wait_ge(htok_ready, 2 * TILES)
                    act.wait_ge(table_ready, 1)
                    passes = act.value_load(etab[0:1, MAX_PASS:MAX_PASS + 1], min_val=NEXP, max_val=MAX_PASS - 1)
                    U = 2 * (FB + KD)
                    w0, done0 = HALVES * U, HALVES * (FB + KD)

                    def gathered(n):
                        for k in range(KD):
                            act.wait_ge(gath_ready, n * KD + (k + 1))
                            A(hg[:, k, :, :], ps[:, 4 + k % 2, 0:2 * CAP].rearrange("p (a n) -> p a n", a=2), ACT.Copy)\
                                .then_inc(gath_evac, 1)
                        act.wait_ge(gc_ready, n + 1)
                        A(gcomp, ps[:, 6, 0:CAP], ACT.Copy).then_inc(gc_evac, 1)

                    def high(n, j, w):
                        u = 2 * j + w
                        if w == 0:
                            act.wait_ge(slot_full[j % NSLOT], ring.full(("ffn", L), n, j))
                        if j >= 2:
                            act.wait_ge(unit_done[0], n * U + (done0 + u - NWB + 1))
                        elif not isinstance(n, int):
                            act.wait_ge(unit_done[0], n * U + (done0 + w + 1 - (2 if j == 0 else 4)))
                        size = KD * P if j < FB else (FLO if w == 0 else FB - FLO) * P
                        c0 = w * (KD * P if j < FB else FLO * P)
                        A(wE[u % NWB][:, 0, 0:size], slots[:, j % NSLOT, c0:c0 + size], ACT.Copy).then_inc(w_high, 1)

                    gathered(0)
                    for j, w in ((1, 0), (1, 1), (0, 0), (0, 1)):
                        high(0, j, w)
                    with act.Fori(0, passes) as it:

                        def gate_half(f):
                            act.wait_ge(unit_done[0], it * U + (done0 + 2 * f + 1))
                            if f >= 2:
                                act.wait_ge(sg_ready, it * FB + (2 * FB + f - 1))
                            A(gsum[f % 2], ps[:, f % 2, CAP:2 * CAP], ACT.Copy).then_inc(g_half, 1)

                        def up_half(f):
                            act.wait_ge(unit_done[0], it * U + (done0 + 2 * f + 2))
                            if f >= 1:
                                act.wait_ge(hid_ready32, it * FB + f)
                            A(usum, ps[:, 2 + f % 2, CAP:2 * CAP], ACT.Copy).then_inc(u_half, 1)

                        def y_half_part(d):
                            act.wait_ge(unit_done[0], it * U + (done0 + 2 * (FB + d) + 2))
                            if d >= 2:
                                act.wait_ge(ytok_ready, it * KD + (d - 1))
                            A(yT[:, d % 2, :], ps[:, d % 2, CAP:2 * CAP], ACT.Copy).then_inc(y_half, 1)

                        def silu(f):
                            act.wait_ge(gsum_ready, it * FB + (f + 1))
                            if f >= 2:
                                act.wait_ge(hid_ready32, it * FB + (f - 1))
                            A(sge[f % 2], gsum[f % 2], ACT.Silu).then_inc(sg_ready, 1)

                        def hid_high_part(f):
                            act.wait_ge(hid_ready32, it * FB + (f + 1))
                            A(hidE[:, f, 0, :], hide[f % 2], ACT.Copy).then_inc(hid_high, 1)

                        def y_high_part(d):
                            act.wait_ge(ytok_ready, it * KD + (d + 1))
                            if d >= 2:
                                act.wait_ge(sc_ready, it * KD + (d - 1))
                            A(yR[:, d % 2, 0, :, :], ps[0:CH, 2 + d % 2, 0:2 * P].rearrange("p (c n) -> p c n", c=2),
                              ACT.Copy).then_inc(y_high, 1)

                        for b in range(FB + KD):
                            n, j = ahead(it, b)
                            if b < FB:
                                gate_half(b)
                            high(n, j, 0)
                            if b < FB:
                                silu(b)
                                up_half(b)
                            else:
                                y_half_part(b - FB)
                            high(n, j, 1)
                            if b < FB:
                                hid_high_part(b)
                            if b == FB - 1:
                                act.wait_ge(e_gated, (it + 1) * FB)
                                gathered(it + 1)
                            if b > FB:
                                y_high_part(b - FB - 1)
                        y_high_part(KD - 1)
                    continue
                act.wait_ge(h_split, KD * (L + 1))
                with act.Fori(0, HALVES) as it:
                    n0 = fexp_base[L]
                    nb = FB + KD

                    def high(j, w):
                        if w == 0:
                            act.wait_ge(slot_full[j % NSLOT], ring.full(("ffn", L), it, j))
                        if j:
                            act.wait_ge(unit_done[w], it * nb + (n0 * nb + j))
                        else:
                            act.wait_ge(x_upd, it * KD + xu(L, "out"))
                        n = KD * P if j < FB else (FLO if w == 0 else FB - FLO) * P
                        c0 = w * (KD * P if j < FB else FLO * P)
                        A(wR[:, w, 0, 0:n], slots[:, j % NSLOT, c0:c0 + n], ACT.Copy).then_inc(w_high, 1)

                    def silu(f):
                        act.wait_ge(unit_done[0], it * nb + (n0 * nb + f + 1))
                        if f >= 2:
                            act.wait_ge(hid_ready, it * FB + (n0 * FB + f - 1))
                        A(halves(sg[f % 2]), pair(2 * (f % 2)), ACT.Silu).then_inc(sg_ready, 1)

                    for j in range(FB + KD):
                        high(j, 0)
                        if 1 <= j <= FB:
                            silu(j - 1)
                        high(j, 1)
            norm(2 * DEPTH, passes * KD + (xu(DEPTH - 1, "out") - KD), lambda k, s: vecT[:, 0, V_FIN + k:V_FIN + k + 1], None, 0)
            for i in range(2 * TILES):
                t, g = i // 2, i % 2
                act.wait_ge(y_ready, i + 1)
                A(xin[0:ROWS[t], t, g * 512:(g + 1) * 512], ps[0:ROWS[t], i % 8, :], ACT.Copy).then_inc(y_evac, 1)

        @block.vector
        def _(dve):
            ch = Chain(dve, dve_chain)
            V = nc.vector
            V.memset(ones[:, :], 1.0).then_inc(memsets, 1)
            ch.link(V.memset(amask[:, 0:P], 0.0))
            ch.link(V.memset(amask[0:HD, HD:P], NEG))
            ch.link(V.memset(logf[:, :, :], 0.0))
            ch.link(V.memset(lft[:, :, :, :], 0.0))
            dve.wait_ge(consts_loaded, 96)
            ch.link(V.tensor_tensor(score[:, 0:P], tri[:, :], ident[:, :], ALU.subtract))
            ch.link(V.tensor_scalar(cmask[:, :], score[:, 0:P], NEG, None, ALU.mult))
            V.tensor_copy(identb[:, :], ident[:, :]).then_inc(identb_ready, 1)
            dve.wait_ge(vt_ready, 1)
            V.tensor_copy(vecT[:, :, :], ps[:, 0:2, 0:V_ROWS]).then_inc(vt_evac, 1)

            def stats(n):
                v, s, r, t = (oT[:, i, :] for i in range(4))
                dve.wait_ge(ms_ready, n + 1)
                V.tensor_scalar(halves(v), pair(0), 1.0 / D, NORM_EPS, ALU.mult, ALU.add).then_inc(v_ready, 1)
                dve.wait_ge(root_ready, n + 1)
                ch.link(V.reciprocal(r, s))
                ch.link(V.tensor_tensor(t, r, r, ALU.mult))
                ch.link(V.tensor_tensor(t, t, v, ALU.mult))
                ch.link(V.tensor_scalar(t, t, -0.5, 1.5, ALU.mult, ALU.add))
                ch.link(V.tensor_tensor(r, r, t, ALU.mult))
                for k in range(KD):
                    V.tensor_tensor(hT[:, k, :], xT[:, k, :], r, ALU.mult).then_inc(normed, 1)

            for L in range(DEPTH):
                dve.wait_ge(ada_done, 24 * (L + 1))
                bias = vecT[:, L, V_ADAB:V_ADAB + 48].unsqueeze(2).to_broadcast([P, 48, 2])
                ch.link(V.tensor_tensor(mod[:, :, :], ps[:, 7, 0:96].rearrange("p (b s) -> p b s", s=2), bias, ALU.add))
                for i, (sc0, g0) in enumerate(((M_SC1, V_NMIX), (M_SC2, V_NFFN))):
                    gain = vecT[:, L, g0:g0 + KD].unsqueeze(2).to_broadcast([P, KD, 2])
                    last = V.scalar_tensor_tensor(scl[:, i], mod[:, sc0:sc0 + KD, :], 1.0, gain, ALU.add, ALU.mult)
                last.then_inc(mod_ready, 1)
                stats(2 * L)
                tmpf = oT[:, :, :].rearrange("p k n -> p (k n)")

                ropes = [6 * L]

                def rope(c0, nh):
                    for a, b, r in ((0, SAMPLE, P), (SAMPLE, TILES, DEC)):
                        n = b - a
                        v = z[0:r, a:b, c0:c0 + nh * HD].rearrange("p t (h u f) -> p t h u f", h=nh, u=2)
                        x1, x2 = v[:, :, :, 0, :], v[:, :, :, 1, :]
                        cos = cs[0:r, a:b, 0, :].unsqueeze(2).to_broadcast([r, n, nh, 32])
                        sin = cs[0:r, a:b, 1, :].unsqueeze(2).to_broadcast([r, n, nh, 32])
                        tm = [tmpf[0:r, 896 * i:896 * i + n * nh * 32].rearrange("p (t h f) -> p t h f", t=n, h=nh)
                              for i in range(3)]
                        V.tensor_tensor(tm[0], x1, cos, ALU.mult)
                        V.tensor_tensor(tm[1], x2, sin, ALU.mult)
                        ch.link(V.tensor_tensor(tm[2], x1, sin, ALU.mult))
                        V.tensor_tensor(x1, tm[0], tm[1], ALU.subtract)
                        ch.link(V.tensor_tensor(x2, x2, cos, ALU.mult))
                        V.tensor_tensor(x2, x2, tm[2], ALU.add).then_inc(rope_done, 1)
                        ropes[0] += 1
                        dve.wait_ge(rope_done, ropes[0])

                dve.wait_ge(z_evac, NZ * L + 4 * TILES)
                rope(IQ, IH)
                rope(IK, 1)
                rope(AQ, AH + 1)
                dve.wait_ge(z_evac, NZ * L + 8 * TILES)
                for a, b, r in ((0, SAMPLE, P), (SAMPLE, TILES, DEC)):
                    bias = bfb[0:r, L, :].unsqueeze(1).to_broadcast([r, b - a, BH])
                    ch.link(V.tensor_tensor(lft[0:r, 0, a:b, :], z[0:r, a:b, BF_:BF_ + BH], bias, ALU.add))
                V.scalar_tensor_tensor(lft[:, 1], lft[:, 0], -1.0, lft[:, 0], ALU.mult, ALU.max).then_inc(lf_abs, 1)
                dve.wait_ge(lf_ln, L + 1)
                for a, b, r in ((0, SAMPLE, P), (SAMPLE, TILES, DEC)):
                    last = V.scalar_tensor_tensor(logf[0:r, a:b, :], lft[0:r, 0, a:b, :], 0.0, lft[0:r, 2, a:b, :],
                                                  ALU.min, ALU.subtract)
                last.then_inc(logf_ready, 1)
                q = 0
                for t in range(1, TILES):
                    r, w = ROWS[t], KW[t]
                    sc = score[0:r, SOFF[t]:SOFF[t] + w]
                    for h in range(IH):
                        dve.wait_ge(is_relu, 16 * L + q + 1)
                        wt = z[0:r, t, IW + h:IW + h + 1]
                        src = rel[q % 2][0:r, 0:w]
                        if h == 0:
                            last = V.tensor_scalar(sc, src, wt, None, ALU.mult)
                        else:
                            dve.wait_ge(is_acc, 16 * L + q)
                            last = V.scalar_tensor_tensor(sc, src, wt, sc, ALU.mult, ALU.add)
                        last.then_inc(is_acc, 1)
                        q += 1
                dve.wait_ge(is_acc, 16 * (L + 1))
                for t in range(1, SAMPLE):
                    last = V.memset(score[0:CHUNK, SOFF[t] + KW[t] - CHUNK:SOFF[t] + KW[t]], LOWEST)
                ch.link(last)
                for t in range(1, TILES):
                    r, w = ROWS[t], KW[t]
                    kk = K_SAMPLE if t == SAMPLE else K_PROMPT
                    sc, wk = score[0:r, SOFF[t]:SOFF[t] + w], work[0:r, 0:w]
                    ch.link(V.max(m8[0:r, :], sc))
                    ch.link(V.match_replace(wk, m8[0:r, :], sc, LOWEST))
                    rounds = kk // 8 - 2
                    for _ in range(rounds):
                        ch.link(V.max(m8[0:r, :], wk))
                        ch.link(V.match_replace(wk, m8[0:r, :], wk, LOWEST))
                    ch.link(V.max(m8[0:r, :], wk))
                    kth = m8[0:r, 7:8]
                    gt, eq, rk = isgt[0:r, 0:w], iseq[0:r, 0:w], rank[0:r, 0:w]
                    V.tensor_scalar(eq, sc, kth, None, ALU.is_equal)
                    ch.link(V.tensor_scalar(gt, sc, kth, None, ALU.is_gt, ALU.add, accum_out=stat[0:r, 0:1]))
                    ch.link(V.tensor_scalar(stat[0:r, 1:2], stat[0:r, 0:1], -1.0, float(kk), ALU.mult, ALU.add))
                    ch.link(V.tensor_tensor_scan(rk, eq, eq, 0.0, ALU.add, ALU.max))
                    ch.link(V.scalar_tensor_tensor(rk, rk, stat[0:r, 1:2], eq, ALU.is_le, ALU.mult))
                    ch.link(V.tensor_tensor(rk, rk, gt, ALU.add))
                    V.tensor_scalar(amask[0:r, MOFF[t]:MOFF[t] + w], rk, -NEG, NEG, ALU.mult, ALU.add).then_inc(mask_ready, 1)
                    dve.wait_ge(mask_ready, 4 * L + t)
                dve.wait_ge(cum_ready, L + 1)
                V.tensor_scalar(negcum[:, 0:SEQ], ps[0:BH, 6, :], -1.0, None, ALU.mult)
                V.tensor_scalar(negcum[:, SEQ:KEYS], ps[0:BH, 7, 0:PAST + DEC], -1.0, None, ALU.mult).then_inc(cum_evac, 1)
                for t in range(TILES):
                    r = ROWS[t]
                    dve.wait_ge(pm_ready, TILES * L + t + 1)
                    if t:
                        dve.wait_ge(po_ready, TILES * L + t)
                    v4 = lambda ap: ap.rearrange("p (g n) -> p g n", g=4)[:, :, 0:r]
                    V.tensor_copy(v4(pooled), v4(ps[0:HD, t, :])).then_inc(pm_evac, 1)
                    dve.wait_ge(po_ready, TILES * L + t + 1)
                    for pr in range(2):
                        last = V.tensor_scalar(oT[:, 6 + pr, tok(t)], ps[:, 5, pr * P:pr * P + r],
                                               vecT[:, L, V_PSC + pr:V_PSC + pr + 1], None, ALU.mult)
                    last.then_inc(po_evac, 1)
                for i, (kind, t) in enumerate(at_groups):
                    if at_on_act[i]:
                        continue
                    dve.wait_ge(at_ready, N_AT * L + i + 1)
                    src = ps[:, i % 8, :].rearrange("p (q n) -> p q n", q=4)
                    if kind == "past":
                        V.tensor_copy(akT[0:HD, SEQ:SEQ + PAST], src[0:HD, 0, :])
                        V.tensor_copy(akT[HD:P, SEQ:SEQ + PAST], src[0:HD, 0, :])
                        V.tensor_copy(bkT[:, :, SEQ:SEQ + PAST], src[:, 1:4, :]).then_inc(at_evac_dve, 1)
                    else:
                        V.tensor_scalar(bqT[:, :, tok(t)], src[:, 0:3, 0:ROWS[t]], HD ** -0.5, None, ALU.mult)\
                            .then_inc(at_evac_dve, 1)
                base = NATT * L
                for i in range(NATT + 2):
                    if i < NATT:
                        t, m, h = items[i]
                        r = ROWS[t]
                        dve.wait_ge(s_ready, base + i + 1)
                        V.tensor_reduce(nmax[0:r, i % 12:i % 12 + 1], ps[0:r, i % 3, 0:KW[t]], AX.X, ALU.max, negate=True)\
                            .then_inc(mx_ready, 1)
                    j = i - 1
                    if 0 <= j < NATT:
                        t, m, h = items[j]
                        r = ROWS[t]
                        dve.wait_ge(pt_ready, base + j + 1)
                        if j >= 2:
                            dve.wait_ge(pv_done, base + j - 1)
                        nb = len(key_blocks(t))
                        src = ps[:, 3 + j % 2, 0:nb * P].rearrange("p (b n) -> p b n", b=nb)
                        dst = probsT[j % 2][:, 0:nb * P].rearrange("p (b n) -> p b n", b=nb)
                        if t == SAMPLE:
                            V.tensor_copy(dst[:, 0, 0:r], src[:, 0, 0:r])
                            last = V.tensor_copy(dst[0:DEC, 1, 0:r], src[0:DEC, 1, 0:r])
                        else:
                            last = V.tensor_copy(dst, src)
                        last.then_inc(pt_evac, 1)
                    j = i - 2
                    if 0 <= j < NATT and j % AH == AH - 1:
                        t, m, h = items[j]
                        r, tm = ROWS[t], j // AH
                        dve.wait_ge(p_ready, base + j + 1)
                        ch.link(V.reciprocal(rinv[0:r, tm % 2, :], rsum[0:r, tm % 2, :]))
                        dve.wait_ge(pv_done, base + j + 1)
                        c = BQ if m else AQ
                        V.tensor_tensor(z[0:r, t, c:c + AH * HD].rearrange("p (h d) -> p h d", h=AH),
                                        ps[0:r, 5 + tm % 2, 0:AH * HD].rearrange("p (h d) -> p h d", h=AH),
                                        rinv[0:r, tm % 2, :].unsqueeze(2).to_broadcast([r, AH, HD]), ALU.mult)\
                            .then_inc(o_evac, 1)
                with dve.Fori(0, 2) as it:
                    ch.enter(it, 0, 4)
                    for d in range(4):
                        def blk(i):
                            return gT[:, ds(it * 4 + (i * KD + d), 1), :].rearrange("p e n -> p (e n)")
                        for i in range(3):
                            g = 3 * d + i
                            dve.wait_ge(b_ready, it * 12 + (24 * L + g + 1))
                            V.tensor_tensor(halves(blk(i)), pair(g % 4), halves(blk(i)), ALU.mult).then_inc(b_evac, 1)
                            dve.wait_ge(b_evac, it * 12 + (24 * L + g + 1))
                            if i == 1:
                                ch.link(V.tensor_tensor(blk(0), blk(0), blk(1), ALU.add))
                            if i == 2:
                                V.tensor_tensor(blk(0), blk(0), blk(2), ALU.add).then_inc(m_ready, 1)
                ch.leave(2)

                def residual(pr, k, gate):
                    for s, hh, a, b in ((0, 0, 0, HALF), (0, 1, HALF, SEQ), (1, 1, SEQ, NTOK)):
                        x = xT[:, k, a:b]
                        last = V.scalar_tensor_tensor(x, ps[:, 2 * pr + hh, a - hh * HALF:b - hh * HALF],
                                                      mod[:, gate + k, s:s + 1], x, ALU.mult, ALU.add)
                    last.then_inc(x_upd, 1)

                for d in range(KD):
                    dve.wait_ge(r_ready, KD * L + d + 1)
                    residual(d % 4, d, M_G1)
                dve.wait_ge(x_upd, xu(L, "out"))
                stats(2 * L + 1)
                dve.wait_ge(outs_done, 160 * (L + 1))
                for k in range(KD if L == 0 else 0):
                    dve.wait_ge(h_ready, KD * (2 * L + 1) + k + 1)
                    ch.link(V.tensor_copy(hR[:, 0, k, :], hT[:, k, :]))
                    V.tensor_tensor(hR[:, 1, k, :], hT[:, k, :], hR[:, 0, k, :].bitcast(FP), ALU.subtract)\
                        .then_inc(h_split, 1)
                if L == 1:
                    lg, eq, gt, rk, pre, ex, ga, c2 = rt
                    V.memset(hTok[:, :, SAMPLE, :].bitcast(FP), 0.0).then_inc(tokpad, 1)
                    dve.wait_ge(rl_ready, 1)
                    ch.link(V.memset(lg, 0.0))
                    dve.wait_ge(rl_ready, 1)
                    for a, b, r in ((0, SAMPLE, P), (SAMPLE, TILES, DEC)):
                        ch.link(V.tensor_tensor(lg[0:r, a:b, :],
                                                ps[0:r, 4, a * NEXP:b * NEXP].rearrange("p (t e) -> p t e", e=NEXP),
                                                rb[0:r, :].unsqueeze(1).to_broadcast([r, b - a, NEXP]), ALU.add))
                    for t in range(TILES):
                        last = V.max(pre[:, t, :], lg[:, t, :])
                    ch.link(last)
                    first = pre[:, :, 0:1].to_broadcast([P, TILES, NEXP])
                    second = pre[:, :, 1:2].to_broadcast([P, TILES, NEXP])
                    V.tensor_tensor(ex, lg, first, ALU.subtract).then_inc(rexp_in, 1)
                    V.tensor_tensor(gt, lg, second, ALU.is_gt)
                    ch.link(V.tensor_tensor(eq, lg, second, ALU.is_equal))
                    for t in range(TILES):
                        last = V.tensor_tensor_scan(rk[:, t, :], eq[:, t, :], eq[:, t, :], 0.0, ALU.add, ALU.max)
                    ch.link(last)
                    ch.link(V.tensor_reduce(c2[:, :, 0:1], gt, AX.X, ALU.add))
                    ch.link(V.tensor_tensor(rk, rk, c2[:, :, 0:1].to_broadcast([P, TILES, NEXP]), ALU.add))
                    ch.link(V.scalar_tensor_tensor(rk, rk, 2.0, eq, ALU.is_le, ALU.mult))
                    ch.link(V.tensor_tensor(rk, rk, gt, ALU.add))
                    dve.wait_ge(rexp_out, 1)
                    ch.link(V.tensor_tensor(ex, ex, rk, ALU.mult))
                    ch.link(V.tensor_reduce(c2[:, :, 0:1], ex, AX.X, ALU.add))
                    ch.link(V.reciprocal(c2[:, :, 1:2], c2[:, :, 0:1]))
                    ch.link(V.tensor_tensor(ga, ex, c2[:, :, 1:2].to_broadcast([P, TILES, NEXP]), ALU.mult))
                    for a, b in ((DEC, 2 * DEC), (2 * DEC, P)):
                        last = V.memset(rk[a:b, SAMPLE, :], 0.0)
                    last.then_inc(sel_ready, 1)
                    dve.wait_ge(sel_ready, 1)
                    for i in range(2 * TILES):
                        t, g = i // 2, i % 2
                        dve.wait_ge(htok_high, i + 1)
                        r, c = ROWS[t], slice(g * 512, (g + 1) * 512)
                        V.tensor_tensor(hTok[0:r, 1, t, c], ps[0:r, i % 4, :], hTok[0:r, 0, t, c].bitcast(FP), ALU.subtract)\
                            .then_inc(htok_ready, 1)
                    dve.wait_ge(cnt_ready, 1)
                    ch.link(V.scalar_tensor_tensor(rowno, ps[:, 5, 0:TILES * NEXP].rearrange("p (t e) -> p t e", t=TILES),
                                                   9999.0, rk, ALU.add, ALU.mult))
                    V.tensor_scalar(rowno, rowno, -10000.0, None, ALU.add).then_inc(gate_ready, 1)
                    cnt, m1, cumm = tab[:, 0:8], tab[:, 8:16], tab[:, 16:24]
                    ch.link(V.tensor_copy(cnt, ps[:, 5, TILES * NEXP:(TILES + 1) * NEXP]))
                    ch.link(V.memset(m1, 1.0))
                    for c in range(1, -(-NTOK // CAP)):
                        ch.link(V.scalar_tensor_tensor(m1, cnt, float(c * CAP), m1, ALU.is_gt, ALU.add))
                    ch.link(V.tensor_tensor_scan(cumm, m1, m1, 0.0, ALU.add, ALU.max))
                    number = iota[:, 0:MAX_PASS]
                    dve.wait_ge(iota_loaded, 16)
                    ch.link(V.tensor_tensor(t3, cumm.unsqueeze(1).to_broadcast([P, MAX_PASS, NEXP]),
                                            number.unsqueeze(2).to_broadcast([P, MAX_PASS, NEXP]), ALU.is_le))
                    ch.link(V.tensor_reduce(epass, t3, AX.X, ALU.add))
                    ch.link(V.tensor_tensor(t3, t3, m1.unsqueeze(1).to_broadcast([P, MAX_PASS, NEXP]), ALU.mult))
                    ch.link(V.tensor_reduce(spass, t3, AX.X, ALU.add))
                    ch.link(V.tensor_scalar(epass, epass, float(NEXP - 1), None, ALU.min))
                    ch.link(V.tensor_tensor(cpass, spass, number, ALU.subtract))
                    ch.link(V.tensor_scalar(cpass, cpass, float(CAP), None, ALU.mult))
                    ch.link(V.tensor_copy(etab[:, 0:MAX_PASS], epass))
                    V.tensor_copy(etab[:, MAX_PASS:MAX_PASS + 1], cumm[:, NEXP - 1:NEXP]).then_inc(table_ready, 1)
                    dve.wait_ge(table_ready, 1)
                    passes = dve.value_load(etab[0:1, MAX_PASS:MAX_PASS + 1], min_val=NEXP, max_val=MAX_PASS - 1)
                    U = 2 * (FB + KD)
                    w0, done0 = HALVES * U, HALVES * (FB + KD)

                    def select(n, e):
                        V.tensor_copy(gcol, ga[:, :, ds(e, 1)].rearrange("p t e -> p (t e)"))
                        ch.link(V.tensor_scalar(rcol, rowno[:, :, ds(e, 1)].rearrange("p t e -> p (t e)"),
                                                cpass[:, ds(n, 1)], None, ALU.add))
                        for t in range(TILES):
                            last = V.tensor_scalar(pick[:, t, :], iota[:, 0:CAP], rcol[:, t:t + 1], None, ALU.is_equal)
                        last.then_inc(pick_ready, 1)

                    dve.wait_ge(gate_ready, 1)
                    first = dve.value_load(etab[0:1, 0:1], min_val=0, max_val=NEXP - 1)
                    select(0, first)
                    dve.wait_ge(gb_evac, NEXP)

                    def low(n, j, w):
                        u = 2 * j + w
                        dve.wait_ge(w_high, n * U + (w0 + 2 * order(j) + w + 1))
                        size = KD * P if j < FB else (FLO if w == 0 else FB - FLO) * P
                        c0 = w * (KD * P if j < FB else FLO * P)
                        V.tensor_tensor(wE[u % NWB][:, 1, 0:size], slots[:, j % NSLOT, c0:c0 + size],
                                        wE[u % NWB][:, 0, 0:size].bitcast(FP), ALU.subtract).then_inc(w_split, 1)

                    for j, w in ((1, 0), (1, 1), (0, 0), (0, 1)):
                        low(0, j, w)
                    with dve.Fori(0, passes) as it:
                        ch.enter(it, 0, 2)
                        expert = dve.value_load(etab[0:1, ds(it, 1)], min_val=0, max_val=NEXP - 1)
                        after = dve.value_load(etab[0:1, ds(it + 1, 1)], min_val=0, max_val=NEXP - 1)

                        def gate_sum(f):
                            dve.wait_ge(g_half, it * FB + (f + 1))
                            V.tensor_tensor(gsum[f % 2], ps[:, f % 2, 0:CAP], gsum[f % 2], ALU.add).then_inc(gsum_ready, 1)

                        def hidden(f):
                            dve.wait_ge(u_half, it * FB + (f + 1))
                            V.tensor_tensor(usum, ps[:, 2 + f % 2, 0:CAP], usum, ALU.add).then_inc(usum_ready, 1)
                            dve.wait_ge(usum_ready, it * FB + (f + 1))
                            dve.wait_ge(e_gated, it * FB + (f + 1))
                            if f >= 2:
                                dve.wait_ge(hid_ready, it * FB + (2 * FB + f - 1))
                            V.tensor_tensor(hide[f % 2], usum, sge[f % 2], ALU.mult).then_inc(hid_ready32, 1)

                        def y_sum(d):
                            dve.wait_ge(y_half, it * KD + (d + 1))
                            V.tensor_tensor(yT[:, d % 2, :], ps[:, d % 2, 0:CAP], yT[:, d % 2, :], ALU.add).then_inc(yc_ready, 1)

                        def y_low(d):
                            dve.wait_ge(y_high, it * KD + (d + 1))
                            V.tensor_tensor(yR[:, d % 2, 1, :, :], ps[0:CH, 2 + d % 2, 0:2 * P].rearrange("p (c n) -> p c n", c=2),
                                            yR[:, d % 2, 0, :, :].bitcast(FP), ALU.subtract).then_inc(y_split, 1)

                        def add_out(d):
                            dve.wait_ge(sc_ready, it * KD + (d + 1))
                            dve.wait_ge(x_upd, it * KD + (xu(L, "out") + d))
                            residual(2 + d % 2, d, M_G2)

                        for b in range(FB + KD):
                            n, j = ahead(it, b)
                            if b < FB:
                                gate_sum(b)
                            low(n, j, 0)
                            if b < FB:
                                hidden(b)
                            else:
                                y_sum(b - FB)
                            low(n, j, 1)
                            if b == 0:
                                ch.link(V.tensor_scalar(jcol, iota[:, CAP:CAP + 2], cpass[:, ds(it, 1)], None, ALU.subtract))
                                for c in range(2):
                                    last = V.tensor_scalar(pickT[:, c, :], rbc[0:CH, ds(expert, 1), :].rearrange("p e n -> p (e n)"),
                                                           jcol[0:CH, c:c + 1], None, ALU.is_equal)
                                last.then_inc(pickT_ready, 1)
                            if b == 1:
                                dve.wait_ge(gc_ready, it + 1)
                                select(it + 1, after)
                            if b > FB:
                                y_low(b - FB - 1)
                            if b > FB + 1:
                                add_out(b - FB - 2)
                        add_out(KD - 2)
                        y_low(KD - 1)
                        add_out(KD - 1)
                    ch.leave(0)
                    continue
                with dve.Fori(0, HALVES) as it:
                    n0 = fexp_base[L]
                    units = 2 * (FB + KD)
                    nb = FB + KD
                    ch.enter(it, 0, 2 * FB)

                    def low(j, w):
                        dve.wait_ge(w_high, it * units + (n0 * units + 2 * j + w + 1))
                        n = KD * P if j < FB else (FLO if w == 0 else FB - FLO) * P
                        c0 = w * (KD * P if j < FB else FLO * P)
                        V.tensor_tensor(wR[:, w, 1, 0:n], slots[:, j % NSLOT, c0:c0 + n], wR[:, w, 0, 0:n].bitcast(FP),
                                        ALU.subtract).then_inc(w_split, 1)

                    def hidden(f):
                        dve.wait_ge(sg_ready, it * FB + (n0 * FB + f + 1))
                        dve.wait_ge(unit_done[1], it * nb + (n0 * nb + f + 1))
                        ch.link(V.tensor_tensor(halves(hidf), pair(2 * (f % 2) + 1), halves(sg[f % 2]), ALU.mult))
                        ch.link(V.tensor_copy(hidR[:, 0, f, :], hidf))
                        V.tensor_tensor(hidR[:, 1, f, :], hidf, hidR[:, 0, f, :].bitcast(FP), ALU.subtract)\
                            .then_inc(hid_ready, 1)
                        dve.wait_ge(hid_ready, it * FB + (n0 * FB + f + 1))

                    for j in range(FB + KD):
                        low(j, 0)
                        low(j, 1)
                        if 1 <= j <= FB:
                            hidden(j - 1)
                        d = j - FB - 1
                        if d >= 0:
                            dve.wait_ge(unit_done[1], it * nb + (n0 * nb + FB + d + 1))
                            dve.wait_ge(x_upd, it * KD + (xu(L, "out") + d))
                            residual((d + 2) % 4, d, M_G2)
                    dve.wait_ge(unit_done[1], it * nb + (n0 * nb + FB + KD))
                    dve.wait_ge(x_upd, it * KD + (xu(L, "out") + KD - 1))
                    residual((KD + 1) % 4, KD - 1, M_G2)
                ch.leave(HALVES)
            dve.wait_ge(x_upd, passes * KD + xu(DEPTH - 1, "out"))
            ch.after_loop(passes, 2)
            stats(2 * DEPTH)


INPUTS = ["x_prompt", "x_sample", "cache_a_kvi", "cache_b_kv", "cache_b_logf", "state_c_pool", "c_prompt", "c_sample",
          "ada_w", "ada_b", "norm_mix_g", "w_in", "b_forget", "pool_w", "pool_scale", "w_br_a", "w_br_b", "w_br_c",
          "w_out", "norm_ffn_g", "ffn_w_gate", "ffn_w_up", "ffn_w_down", "moe_router_w", "moe_router_b",
          "moe_w_gate", "moe_w_up", "moe_w_down", "final_norm_g"]
OUTPUTS = [("y_prompt", (1, SEQ, D)), ("y_sample", (1, DEC, D)),
           ("a_kvi_p", (DEPTH, 1, SEQ, 3, HD)), ("b_kv_p", (DEPTH, 1, SEQ, 2, BH, HD)),
           ("logf_p", (DEPTH, 1, SEQ, BH)), ("pool_p", (DEPTH, 1, HIST, PW)),
           ("a_kvi_s", (DEPTH, 1, DEC, 3, HD)), ("b_kv_s", (DEPTH, 1, DEC, 2, BH, HD)),
           ("logf_s", (DEPTH, 1, DEC, BH)), ("pool_s", (DEPTH, 1, HIST, PW))]


def constants():
    ident = np.eye(P, dtype=np.float32)
    tri = np.triu(np.ones((P, P), np.float32))
    half = HD // 2
    inv = (np.float32(10000.0) ** (-np.arange(half, dtype=np.float32) / np.float32(half))).astype(np.float32)
    pos = np.zeros((P, TILES), np.float32)
    for t in range(SAMPLE):
        pos[:, t] = t * P + np.arange(P)
    pos[0:DEC, SAMPLE] = PAST + np.arange(DEC)
    ang = (pos[:, :, None] * inv[None, None, :]).astype(np.float32)
    rope = np.stack([np.cos(ang), np.sin(ang)], axis=2).astype(np.float32).reshape(P, TILES * HD)
    pool = np.zeros((P, 4, 512), np.float32)
    s, t = np.arange(P)[:, None], np.arange(P)[None, :]
    for g, w in enumerate((2, 4, 8, 16)):
        c = slice(g * P, (g + 1) * P)
        here = ((t - s >= 0) & (t - s < w)).astype(np.float32)
        pool[:, 0, c] = here / w - ident
        pool[:, 1, c] = here / np.minimum(t + 1, w) - ident
        pool[:, 2, c] = ((t + P - s) < w).astype(np.float32) / w
        pool[0:DEC, 3, g * DEC:(g + 1) * DEC] = (here / w - ident)[0:DEC, 0:DEC]
        hs, ht = np.arange(HIST)[:, None], np.arange(DEC)[None, :]
        pool[0:HIST, 3, P + g * DEC:P + (g + 1) * DEC] = ((ht + HIST - hs) < w).astype(np.float32) / w
    iota = np.concatenate([np.broadcast_to(np.arange(CAP), (P, CAP)), np.arange(P)[:, None], np.arange(P)[:, None] + CH],
                          axis=1).astype(np.float32)
    return {"c_iota": iota, "c_ident": ident, "c_tri": tri, "c_rope": rope, "c_pool": pool}


def kernel(**inputs):
    import concourse.bacc as bacc
    from concourse.bass_utils import run_bass_kernel_spmd

    nc = bacc.Bacc("TRN2", target_bir_lowering=False, num_devices=1)
    arrays, t_in, t_out = {}, {}, {}
    consts = constants()
    for name in INPUTS + list(consts):
        a = np.ascontiguousarray(consts[name] if name in consts else inputs[name])
        arrays["in_" + name] = a
        t_in[name] = nc.dram_tensor("in_" + name, a.shape, FP, kind="ExternalInput").ap()
    for name, shape in OUTPUTS:
        t_out[name] = nc.dram_tensor("out_" + name, shape, FP, kind="ExternalOutput").ap()
    encoder_step(nc, t_in, t_out)
    r = run_bass_kernel_spmd(nc, [arrays], core_ids=[0])
    return tuple(r.results[0]["out_" + name] for name, _ in OUTPUTS)
```

```python
import numpy as np
import concourse.bass as bass
from concourse import mybir
from concourse.alu_op_type import AluOpType as ALU
from contextlib import ExitStack

FP = mybir.dt.float32
BF = mybir.dt.bfloat16
FR = mybir.dt.float32r
ACT = mybir.ActivationFunctionType
AX = mybir.AxisListType
ds = bass.ds

P = 128
D = 1024
KD = D // P
SEQ, DEC, PAST = 512, 32, 128
NTOK = SEQ + DEC
HALF = NTOK // 2
DEPTH = 2
TILES = SEQ // P + 1
SAMPLE = TILES - 1
HD = 64
AH = BH = 6
IH = 4
CHUNK = 64
K_PROMPT = min(256, SEQ // 4)
K_SAMPLE = min(256, (DEC + PAST) // 4)
NEXP = 8
FEXP = 1408
FLO = 6
FB = FEXP // P
HALVES = 2
TOP = 2
CAP = 160
CH = CAP // 2
MAX_PASS = NEXP + TOP * NTOK // CAP + 1
NWB = 4
NORM_EPS = 1e-6
NEG = -1e30
LOWEST = -3e38

AQ, AK, AV, IQ = 0, 384, 448, 512
IW, IK = 768, 772
BQ, BK, BV = 836, 1220, 1604
BF_, CU, GL = 1988, 1994, 2250
ZW = GL
ZB = 250
ZITER, ZBODY = 3, 3
GITER, GBODY = 3, 4
N_IN = GL + 3 * D
PW = 256
HIST = 15

NSLOT = 4
SLOT = 2048

V_ADAB, V_NMIX, V_NFFN, V_PSC, V_FIN, V_C, V_ROWS = 0, 48, 56, 64, 66, 74, 90
M_SH1, M_SC1, M_G1, M_SH2, M_SC2, M_G2 = 0, 8, 16, 24, 32, 40

KW = [128, 256, 384, 512, PAST + DEC]
ROWS = [P, P, P, P, DEC]
MOFF = [0, 128, 384, 768, 1280]
MTOT = 1440
KEYS = SEQ + PAST + DEC
KCOL = [0, 0, 0, 0, SEQ]


def tok(t):
    return slice(t * P, t * P + ROWS[t])


def keycol(t):
    return slice(t * P, (t + 1) * P) if t < SAMPLE else slice(SEQ + PAST, KEYS)


class Ring:

    def __init__(self):
        self.n = {"begun": 0, "split": 0}
        self.fills, self.last, self.plan = [0] * NSLOT, [None] * NSLOT, {}

    def phase(self, name, iters, dmas, kind="begun", slots=NSLOT):
        n, per, after, own, before = len(dmas), [0] * NSLOT, [], [], []
        for j, m in enumerate(dmas):
            per[j % slots] += m
            after.append(per[j % slots])
        for j in range(min(slots, n)):
            mine = [i for i in range(n) if i % slots == j][-1]
            own.append(n - mine if iters > 1 else None)
            before.append(self.last[j])
        self.plan[name] = (kind, self.n[kind], list(self.fills), per, after, n, own, before, slots)
        for s in range(NSLOT):
            self.fills[s] += iters * per[s]
        for j in range(n):
            self.last[j % slots] = (kind, self.n[kind] + (iters - 1) * n + j)
        for s in range(slots, NSLOT):
            self.last[s] = (kind, self.n[kind] + iters * n - 1)
        self.n[kind] += iters * n

    def slot(self, name, j):
        return j % self.plan[name][-1]

    def released(self, name, it, j, back):
        return it * self.plan[name][5] + (self.plan[name][1] + j - back + 2)

    def ghost(self):
        self.n["begun"] += 1

    def full(self, name, it, j):
        _, _, fills, per, after, _, _, _, slots = self.plan[name]
        return (it * per[j % slots] + (fills[j % slots] + after[j])) * 16

    def value(self, kind, index):
        return index + 2 if kind == "begun" else index * 2 + 2

    def free(self, name, it, j, late=0):
        kind, first, _, _, _, n, own, before, slots = self.plan[name]
        if j >= slots:
            return [(kind, self.value(kind, it * n + (first + j - slots + late)))]
        out = []
        if own[j] is not None and not (isinstance(it, int) and it == 0):
            out.append((kind, self.value(kind, it * n + (first - own[j]))))
        if before[j] is not None:
            out.append((before[j][0], self.value(*before[j])))
        return out


class Chain:

    def __init__(self, eng, sem):
        self.eng, self.sem, self.base, self.k = eng, sem, 0, 0

    def link(self, ins):
        self.k += 1
        ins.then_inc(self.sem, 1)
        self.eng.wait_ge(self.sem, self.base + self.k)

    def enter(self, it, start, per):
        self.total = self.base + self.k
        self.base, self.k, self.per = (it - start) * per + self.total, 0, per

    def after_loop(self, iters, per):
        assert self.k == self.per, (self.k, self.per)
        self.base, self.k = iters * per + self.total, 0

    def leave(self, iters):
        assert self.k == self.per, (self.k, self.per)
        self.base, self.k = self.total + iters * self.per, 0


def encoder_step(nc, t_in, t_out):
    ring = Ring()
    for L in range(DEPTH):
        ring.phase(("ada", L), 6, [1] * 4)
        ring.phase(("z", L), ZITER, [1] * ZBODY)
        ring.phase(("gates", L), GITER, [1] * GBODY, slots=2)
        ring.phase(("pooled", L), 1, [1])
        ring.ghost()
        ring.phase(("branch", L), 2, [2] * 2)
        ring.phase(("out", L), 2, [1] * 2, slots=2)
        ring.ghost()
        ring.phase(("ffn", L), HALVES, [2] * FB + [1] * KD, "split")

    ctx = ExitStack()
    with ctx:
        start = nc.sbuf_base
        start += -start % 64
        size = nc.sbuf_usable_end - start - 64
        ctx.enter_context(nc.sbuf_tensor("arena", [P, size // 4], FP))
        place = {"next": start}

        def sb(name, shape, dt=FP, over=None):
            n = int(np.prod(shape[1:])) * (2 if dt == BF else 4)
            n += -n % 32
            if over is None:
                at = place["next"]
                place["next"] += n
                assert place["next"] <= start + size, name
            else:
                at, room = place[over]
                assert n <= room, name
            place[name] = (at, n)
            return nc.alloc_sbuf_tensor_at(name, shape, dt, offset=at)

        def sem(name):
            return ctx.enter_context(nc.semaphore(name))

        xT = sb("xT", [P, KD, NTOK])
        hT = sb("hT", [P, KD, NTOK])
        z = sb("z", [P, TILES, ZW])
        gT = sb("gT", [P, 3 * KD, NTOK])
        slots = sb("slots", [P, NSLOT, SLOT])
        oT = sb("oT", [P, KD, NTOK])
        qk = sb("qk", [P, 1760])
        pp = sb("pp", [P, 2, 2, 512])
        amask = sb("amask", [P, MTOT], BF)
        cmask = sb("cmask", [P, P], BF)
        ident = sb("ident", [P, P])
        identb = sb("identb", [P, P], BF)
        ones = sb("ones", [P, P])
        tri = sb("tri", [P, P])
        cs = sb("cs", [P, TILES, 2, 32])
        past = sb("past", [P, 966])
        vecT = sb("vecT", [P, DEPTH, V_ROWS])
        csil = sb("csil", [P, KD, 2])
        mod = sb("mod", [P, 48, 2])
        scl = sb("scl", [P, 2, KD, 2])
        negcum = sb("negcum", [BH, KEYS])
        logf = sb("logf", [P, TILES, BH])
        lft = sb("lft", [P, 3, TILES, BH])
        sel = sb("sel", [P, BH], BF)
        bfb = sb("bfb", [P, DEPTH, BH])
        rb = sb("rb", [P, NEXP])
        rw = sb("rw", [P, KD, NEXP])
        iota = sb("iota", [P, CAP + 2], over="amask")
        etab = sb("etab", [P, MAX_PASS + 1], mybir.dt.int32, over="cmask")
        m8 = sb("m8", [P, 8])
        stat = sb("stat", [P, 4])
        nmax = sb("nmax", [P, 12])
        rsum = sb("rsum", [P, 2, AH])
        rinv = sb("rinv", [P, 2, AH])

        hR = sb("hR", [P, 2, KD, NTOK], FR, over="z")
        hidR = sb("hidR", [P, 2, FB, NTOK], FR, over="gT")
        wR = sb("wR", [P, 2, 2, KD * P], FR, over="hT")

        hL = sb("hL", [P, KD, NTOK], FR, over="hT")
        gates_at = place["gT"][0]
        place["gT_last"] = (gates_at + 2 * KD * NTOK * 4, KD * NTOK * 4)
        hH = sb("hH", [P, KD, NTOK], FR, over="gT_last")
        hH2 = sb("hH2", [P, KD, NTOK], FR, over="oT")
        wz = sb("wz", [P, ZBODY, KD * ZB], FR, over="gT")
        gTr = sb("gTr", [P, 3 * KD, NTOK], FR, over="gT")
        slotsR = sb("slotsR", [P, NSLOT, SLOT], FR, over="slots")

        for i in (2, 3):
            place[f"slot{i}"] = (place["slots"][0] + i * SLOT * 4, SLOT * 4)
        negcum3 = sb("negcum3", [3 * 32, KEYS], BF, over="slot2")
        negpart = sb("negpart", [BH, KEYS], BF, over="slot3")

        hTok = sb("hTok", [P, 2, TILES, D], FR, over="z")
        g_at = {"next": place["gT"][0], "end": sum(place["gT"])}

        def over_gates(name, shape, dt):
            place["_piece"] = (g_at["next"], g_at["end"] - g_at["next"])
            t = sb(name, shape, dt, over="_piece")
            g_at["next"] = place[name][0] + place[name][1]
            return t

        hg = over_gates("hg", [P, KD, 2, CAP], FR)
        hidE = over_gates("hidE", [P, FB, 2, CAP], FR)
        w_extra = over_gates("w_extra", [P, 2, KD * P], FR)
        pick = over_gates("pick", [P, TILES, CAP], FR)
        pickT = over_gates("pickT", [CH, 2, NTOK], FR)
        yR = over_gates("yR", [CH, 2, 2, 2, P], FR)
        yT = over_gates("yT", [P, 2, CAP], FP)
        w_pp = sb("w_pp", [P, 2, KD * P], FR, over="pp")
        wE = [wR[:, 0], wR[:, 1], w_extra[:, :, :], w_pp[:, :, :]]

        xin = z[:, :, 0:D]
        vrow = gT[:, 0, 0:2 * P].rearrange("p (l n) -> p l n", l=2)
        oTf = oT[:, :, :].rearrange("p k n -> p (k n)")
        mrow = oTf[0:2, 4 * NTOK:4 * NTOK + 1024].rearrange("p (j n) -> p j n", j=4)
        score = oTf[:, 0:1312]
        SOFF = [None, 0, 256, 640, 1152]
        rel = [oTf[:, 1312 + 512 * i:1824 + 512 * i] for i in range(2)]
        work = oTf[:, 2336:2848]
        isgt, iseq = rel
        rank = work
        iqT = qk[:, 0:2 * NTOK].rearrange("p (b n) -> p b n", b=2)
        ikT = qk[:, 2 * NTOK:2 * NTOK + KEYS]
        aqT = qk[:, 0:3 * NTOK].rearrange("p (b n) -> p b n", b=3)
        pooled = qk[0:HD, 0:512]
        poolw = qk[0:HD, 512:1024].rearrange("p (g d) -> p g d", g=4)
        hist = qk[0:HIST, 1024:1280]
        hTf = hT[:, :, :].rearrange("p k n -> p (k n)")
        bqT = hTf[:, 0:3 * NTOK].rearrange("p (b n) -> p b n", b=3)
        bkT = hTf[:, 3 * NTOK:3 * NTOK + 3 * KEYS].rearrange("p (b n) -> p b n", b=3)
        akT = hTf[:, 3 * NTOK + 3 * KEYS:3 * NTOK + 4 * KEYS]
        probs = [pp[:, 0, i, :] for i in range(2)]
        probsT = [pp[:, 1, i, :] for i in range(2)]
        poolm = pp[:, :, :, :].rearrange("p a b n -> p (a b) n")
        zf = z[:, :, :].rearrange("p t n -> p (t n)")
        sqs = [zf[:, 0:KD * NTOK].rearrange("p (k n) -> p k n", k=KD), hT]
        zq = 2 * KD * NTOK
        sg = [zf[:, zq + i * NTOK:zq + (i + 1) * NTOK] for i in range(2)]
        hidf = zf[:, zq + 2 * NTOK:zq + 3 * NTOK]
        ze = 2 * TILES * D
        sge = [zf[:, ze + i * CAP:ze + (i + 1) * CAP] for i in range(2)]
        hide = [zf[:, ze + (2 + i) * CAP:ze + (3 + i) * CAP] for i in range(2)]
        gcomp = zf[:, ze + 4 * CAP:ze + 5 * CAP]
        qf = qk[:, :]
        rt = [qf[:, 40 * i:40 * (i + 1)].rearrange("p (t e) -> p t e", t=TILES) for i in range(8)]
        rowno = qf[:, 320:360].rearrange("p (t e) -> p t e", t=TILES)
        tab = qf[:, 360:360 + 8 * 8]
        t3 = qf[:, 424:424 + MAX_PASS * NEXP].rearrange("p (n e) -> p n e", e=NEXP)
        q0 = 424 + MAX_PASS * NEXP
        epass, cpass, spass = (qf[:, q0 + i * MAX_PASS:q0 + (i + 1) * MAX_PASS] for i in range(3))
        q1 = q0 + 3 * MAX_PASS
        rcol, gcol, jcol = qf[:, q1:q1 + TILES], qf[:, q1 + 8:q1 + 8 + TILES], qf[:, q1 + 16:q1 + 18]
        rowT = qf[0:NEXP, q1 + 24:q1 + 24 + NTOK]
        q2 = q1 + 24 + NTOK
        gsum = [qf[:, q2 + i * CAP:q2 + (i + 1) * CAP] for i in range(2)]
        usum = qf[:, q2 + 2 * CAP:q2 + 3 * CAP]
        rbc = oT

        ps = ctx.enter_context(nc.psum_tensor("ps", [P, 8, 512], FP))

        def pair(i):
            return ps[:, 2 * i:2 * i + 2, 0:HALF]

        def halves(ap):
            return ap.rearrange("p (a n) -> p a n", a=2)

        slot_full = [sem(f"slot_full{s}") for s in range(NSLOT)]
        block_begun = sem("block_begun")
        w_high, w_split = sem("w_high"), sem("w_split")
        unit_done = [sem("unit_done0"), sem("unit_done1")]
        h_split = sem("h_split")
        mh_ready, ml_ready, hh2_ready = sem("mh_ready"), sem("ml_ready"), sem("hh2_ready")
        hh_ready, hl_ready, hh_moved = sem("hh_ready"), sem("hl_ready"), sem("hh_moved")
        pw_high, pw_split = sem("pw_high"), sem("pw_split")
        rl_rows, rl_copied = sem("rl_rows"), sem("rl_copied")
        tokpad, ht_ready, htok_high, htok_ready = sem("tokpad"), sem("ht_ready"), sem("htok_high"), sem("htok_ready")
        sel_ready, cnt_ready, table_ready = sem("sel_ready"), sem("cnt_ready"), sem("table_ready")
        pick_ready, pickT_ready = sem("pick_ready"), sem("pickT_ready")
        gath_ready, gath_evac, gc_ready, gc_evac = sem("gath_ready"), sem("gath_evac"), sem("gc_ready"), sem("gc_evac")
        yc_ready, ytok_ready, y_high, y_split, sc_ready = (sem("yc_ready"), sem("ytok_ready"), sem("y_high"),
                                                           sem("y_split"), sem("sc_ready"))
        gsum_ready, usum_ready, hid_ready32, hid_high = (sem("gsum_ready"), sem("usum_ready"), sem("hid_ready32"),
                                                         sem("hid_high"))
        g_half, u_half, y_half = sem("g_half"), sem("u_half"), sem("y_half")
        e_gated, iota_loaded = sem("e_gated"), sem("iota_loaded")
        ada_row, ada_copied, ada_done = sem("ada_row"), sem("ada_copied"), sem("ada_done")
        x_loaded = sem("x_loaded")
        consts_loaded = sem("consts_loaded")
        vrow_loaded = sem("vrow_loaded")
        memsets = sem("memsets")
        identb_ready = sem("identb_ready")
        xt_ready, xt_evac = sem("xt_ready"), sem("xt_evac")
        vt_ready, vt_evac = sem("vt_ready"), sem("vt_evac")
        csil_ready = sem("csil_ready")
        mod_ready = sem("mod_ready")
        sq_ready, ms_ready, v_ready, root_ready = sem("sq_ready"), sem("ms_ready"), sem("v_ready"), sem("root_ready")
        normed, h_ready = sem("normed"), sem("h_ready")
        x_upd = sem("x_upd")
        z_ready, z_evac = sem("z_ready"), sem("z_evac")
        past_loaded = sem("past_loaded")
        pool_mats_loaded = sem("pool_mats_loaded")
        poolw_zero, poolw_loaded = sem("poolw_zero"), sem("poolw_loaded")
        rope_done = sem("rope_done")
        lf_abs, lf_ln, logf_ready = sem("lf_abs"), sem("lf_ln"), sem("logf_ready")
        ti_ready, ti_evac = sem("ti_ready"), sem("ti_evac")
        is_ready, is_relu, is_acc = sem("is_ready"), sem("is_relu"), sem("is_acc")
        mask_ready = sem("mask_ready")
        g_ready, g_evac = sem("g_ready"), sem("g_evac")
        cum_ready, cum_evac = sem("cum_ready"), sem("cum_evac")
        pm_ready, pm_evac, po_ready, po_evac = sem("pm_ready"), sem("pm_evac"), sem("po_ready"), sem("po_evac")
        at_ready, at_evac_act, at_evac_dve = sem("at_ready"), sem("at_evac_act"), sem("at_evac_dve")
        s_ready, mx_ready, p_ready = sem("s_ready"), sem("mx_ready"), sem("p_ready")
        pt_ready, pt_evac, pv_done = sem("pt_ready"), sem("pt_evac"), sem("pv_done")
        o_evac, ot_ready, ot_evac = sem("o_evac"), sem("ot_ready"), sem("ot_evac")
        b_ready, b_evac, m_ready = sem("b_ready"), sem("b_evac"), sem("m_ready")
        r_ready = sem("r_ready")
        sg_ready, hid_ready = sem("sg_ready"), sem("hid_ready")
        rl_ready, gate_ready, gt_ready, gt_evac, gb_ready, gb_evac = (sem("rl_ready"), sem("gate_ready"), sem("gt_ready"),
                                                                      sem("gt_evac"), sem("gb_ready"), sem("gb_evac"))
        rexp_in, rexp_out = sem("rexp_in"), sem("rexp_out")
        y_ready, y_evac = sem("y_ready"), sem("y_evac")
        outs_done, y_sent = sem("outs_done"), sem("y_sent")
        act_chain, dve_chain = sem("act_chain"), sem("dve_chain")

        NZ = ZITER * ZBODY * TILES
        NATT = TILES * 2 * AH
        NTM = TILES * 2

        def xu(L, stage):
            base = sum(KD * (1 + HALVES) for l in range(L))
            return base + {"start": 0, "out": KD, "ffn": KD * (1 + HALVES)}[stage]

        fexp_base = [0, HALVES]

        items = [(t, m, h) for t in (3, 2, 1, SAMPLE, 0) for m in range(2) for h in range(AH)]

        def key_blocks(t):
            if t == SAMPLE:
                return [(0, PAST, "past"), (PAST, DEC, SAMPLE)]
            return [(s * P, P, s) for s in range(t + 1)]

        at_groups = [("past", None)] + [(kind, t) for t in range(TILES) for kind in ("a", "bq", "bk")]
        at_on_act = [kind in ("a", "bk") for kind, _ in at_groups]
        N_AT = len(at_groups)
        N_AT_ACT = sum(at_on_act)
        N_AT_DVE = N_AT - N_AT_ACT

        NPW = 2 * (ZITER * ZBODY + GITER * GBODY + 4)

        def proj_halves(name, it, j):
            kind, L = name
            if kind == "z":
                return it * (2 * ZBODY) + (NPW * L + 2 * j + 1)
            if kind == "gates":
                return it * (2 * GBODY) + (NPW * L + 2 * ZITER * ZBODY + 2 * j + 1)
            return it * 4 + (NPW * (L + 1) - 8 + 2 * j + 1)

        def proj_parts(name, j):
            if name[0] == "z":
                return wz[:, j, :], slotsR[:, j, 0:KD * ZB], ZB
            return slotsR[:, 3 - j % 2, :], slotsR[:, j % 2, :], 2 * P

        def order(j):
            return 1 - j if j < 2 else j

        def ahead(it, b):
            j = b + 2 - (FB + KD)
            return (it, b + 2) if j < 0 else (it + 1, order(j))

        block = ctx.enter_context(nc.Block())

        @block.sync
        def _(sp):
            sp.dma_start(xin[:, 0:SAMPLE, :], t_in["x_prompt"][0].rearrange("(t p) d -> p t d", p=P)).then_inc(x_loaded, 16)
            sp.dma_start(xin[0:DEC, SAMPLE, :], t_in["x_sample"][0]).then_inc(x_loaded, 16)

            def fill(name, it, j, pieces, late=0):
                for kind, value in ring.free(name, it, j, late):
                    sp.wait_ge(block_begun if kind == "begun" else w_split, value)
                for dst, src in pieces:
                    sp.dma_start(dst, src).then_inc(slot_full[ring.slot(name, j)], 16)

            def cols(j, w, n=NSLOT):
                return slots[:, j % n, 0:KD * w].rearrange("p (k n) -> p k n", k=KD)

            for L in range(DEPTH):
                ada = t_in["ada_w"][L].rearrange("(k p) n -> p k n", p=P)
                w_in = t_in["w_in"][L].rearrange("(k p) n -> p k n", p=P)
                w_br = [t_in[n][L].rearrange("(k p) n -> p k n", p=P) for n in ("w_br_a", "w_br_b", "w_br_c")]
                w_out = t_in["w_out"][L].rearrange("(k p) n -> p k n", p=P)

                def ada_fill(it):
                    for j in range(4):
                        fill(("ada", L), it, j, [(cols(j, 256), ada[:, :, ds(it * 1024 + j * 256, 256)])])

                if L == 0:
                    ada_fill(0)
                with sp.Fori(1 if L == 0 else 0, 6) as it:
                    if L == 0:
                        for j in range(4):
                            sp.wait_ge(block_begun, it * 4 + (j - 2))
                            sp.dma_start(cols(j, 256), ada[:, :, ds(it * 1024 + j * 256, 256)]).then_inc(slot_full[j], 16)
                    else:
                        ada_fill(it)
                with sp.Fori(0, ZITER) as it:
                    for j in range(ZBODY):
                        fill(("z", L), it, j, [(cols(j, ZB), w_in[:, :, ds(it * (ZBODY * ZB) + j * ZB, ZB)])])
                with sp.Fori(0, GITER) as it:
                    for j in range(GBODY):
                        fill(("gates", L), it, j, [(cols(j, 256, 2), w_in[:, :, ds(it * 1024 + (GL + j * 256), 256)])])
                fill(("pooled", L), 0, 0, [(cols(0, 256).rearrange("p k n -> p (k n)").rearrange("p (k n) -> p k n", k=2), w_br[2])])
                with sp.Fori(0, 2) as it:
                    for j in range(2):
                        dst = cols(j, 256)
                        fill(("branch", L), it, j,
                             [(dst[:, a:b, :], w_br[i][:, :, ds(it * 512 + j * 256, 256)])
                              for i, (a, b) in enumerate(((0, 3), (3, 6)))])
                with sp.Fori(0, 2) as it:
                    for j in range(2):
                        fill(("out", L), it, j, [(cols(j, 256, 2), w_out[:, :, ds(it * 512 + j * 256, 256)])])
                def ffn_fill(it, e=None, blocks=range(FB + KD)):
                    for j in blocks:
                        slot = slots[:, j % NSLOT, :]
                        if j < FB:
                            gu = slot.rearrange("p (w k n) -> p w k n", w=2, k=KD)
                            if L == 0:
                                srcs = [t_in[n][0].rearrange("(k p) n -> p k n", p=P)[:, :, ds(it * FEXP + j * P, P)]
                                        for n in ("ffn_w_gate", "ffn_w_up")]
                            else:
                                srcs = [t_in[n][0, ds(e, 1)].rearrange("e (k p) n -> p (e k) n", p=P)[:, :, j * P:(j + 1) * P]
                                        for n in ("moe_w_gate", "moe_w_up")]
                            fill(("ffn", L), it, j, [(gu[:, w], srcs[w]) for w in range(2)], late=int(L == 1 and j == NSLOT))
                        else:
                            d0 = (j - FB) * P
                            dst = slot[:, 0:FB * P].rearrange("p (f n) -> p f n", f=FB)
                            if L == 0:
                                src = t_in["ffn_w_down"][0, ds(it * FEXP, FEXP)].rearrange("(f p) n -> p f n", p=P)
                            else:
                                src = t_in["moe_w_down"][0, ds(e, 1)].rearrange("e (f p) n -> p (e f) n", p=P)
                            fill(("ffn", L), it, j, [(dst, src[:, :, d0:d0 + P])])

                if L == 0:
                    for it in range(HALVES):
                        ffn_fill(it)
                else:
                    sp.wait_ge(table_ready, 1)
                    passes = sp.value_load(etab[0:1, MAX_PASS:MAX_PASS + 1], min_val=NEXP, max_val=MAX_PASS - 1)
                    with sp.Fori(0, passes) as it:
                        expert = sp.value_load(etab[0:1, ds(it, 1)], min_val=0, max_val=NEXP - 1)
                        ffn_fill(it, expert)
                    ffn_fill(passes, 0, range(2))
            for t in range(TILES):
                sp.wait_ge(y_evac, 2 * t + 2)
                dst = t_out["y_prompt"][0, t * P:(t + 1) * P] if t < SAMPLE else t_out["y_sample"][0]
                sp.dma_start(dst, xin[0:ROWS[t], t, :]).then_inc(y_sent, 16)
            sp.wait_ge(y_sent, 16 * TILES)
            sp.wait_ge(outs_done, 160 * DEPTH)

        @block.gpsimd
        def _(pool):
            G = nc.gpsimd
            for L in range(DEPTH):
                for r, n, src in ((V_ADAB, 48, t_in["ada_b"][L]), (V_NMIX, 8, t_in["norm_mix_g"][L]),
                                  (V_NFFN, 8, t_in["norm_ffn_g"][L]), (V_PSC, 2, t_in["pool_scale"][L]),
                                  (V_FIN, 8, t_in["final_norm_g"]), (V_C, 8, t_in["c_prompt"][0]),
                                  (V_C + 8, 8, t_in["c_sample"][0])):
                    pool.dma_start(vrow[r:r + n, L, :], src.rearrange("(r n) -> r n", n=P)).then_inc(vrow_loaded, 16)
            for dst, src in ((ident, "c_ident"), (tri, "c_tri")):
                pool.dma_start(dst[:, :], t_in[src]).then_inc(consts_loaded, 16)
            pool.dma_start(cs[:, :, :, :].rearrange("p t a f -> p (t a f)"), t_in["c_rope"]).then_inc(consts_loaded, 16)
            pool.dma_start(bfb[:, :, :].rearrange("p l h -> p (l h)"),
                           t_in["b_forget"].rearrange("l h -> (l h)").partition_broadcast(P)).then_inc(consts_loaded, 16)
            pool.dma_start(rb[:, :], t_in["moe_router_b"][0].partition_broadcast(P)).then_inc(consts_loaded, 16)
            pool.dma_start(rw[:, :, :], t_in["moe_router_w"][0].rearrange("(k p) e -> p k e", p=P)).then_inc(consts_loaded, 16)
            for L in range(DEPTH):
                if L:
                    pool.wait_ge(ot_evac, L * NTM)
                pool.dma_start(past[:, 0:192], t_in["cache_a_kvi"][L, 0].rearrange("t c d -> t (c d)")).then_inc(past_loaded, 16)
                pool.dma_start(past[:, 192:960], t_in["cache_b_kv"][L, 0].rearrange("t c h d -> t (c h d)")).then_inc(past_loaded, 16)
                pool.dma_start(past[:, 960:966], t_in["cache_b_logf"][L, 0]).then_inc(past_loaded, 16)
                pool.dma_start(poolm, t_in["c_pool"]).then_inc(pool_mats_loaded, 16)

                def low(name, it, j):
                    high, low_part, w = proj_parts(name, j)
                    raw = slots[:, ring.slot(name, j), 0:KD * w]
                    for half in range(2):
                        c = slice(half * 4 * w, (half + 1) * 4 * w)
                        pool.wait_ge(pw_high, proj_halves(name, it, j) + half)
                        G.tensor_tensor(low_part[:, c], raw[:, c], high[:, c].bitcast(FP), ALU.subtract).then_inc(pw_split, 1)

                with pool.Fori(0, ZITER) as it:
                    for j in range(ZBODY):
                        low(("z", L), it, j)
                low(("gates", L), 0, 0)
                pool.wait_ge(rope_done, 6 * (L + 1))
                pool.wait_ge(logf_ready, L + 1)
                pool.wait_ge(z_evac, NZ * (L + 1))
                for pre, zz, nt in (("p", z[:, 0:SAMPLE, :], SEQ), ("s", z[0:DEC, SAMPLE:TILES, :], DEC)):
                    p = min(nt, P)

                    def rows(name):
                        a = t_out[name][L, 0]
                        return a

                    kvi = rows("a_kvi_" + pre).rearrange("(t p) c d -> p t (c d)", p=p)
                    pool.dma_start(kvi[:, :, 0:2 * HD], zz[:, :, AK:AK + 2 * HD]).then_inc(outs_done, 16)
                    pool.dma_start(kvi[:, :, 2 * HD:], zz[:, :, IK:IK + HD]).then_inc(outs_done, 16)
                    pool.dma_start(rows("b_kv_" + pre).rearrange("(t p) c h d -> p t (c h d)", p=p),
                                   zz[:, :, BK:BK + 2 * BH * HD]).then_inc(outs_done, 16)
                    lf = logf[:, 0:SAMPLE, :] if nt == SEQ else logf[0:DEC, SAMPLE:TILES, :]
                    pool.dma_start(rows("logf_" + pre).rearrange("(t p) h -> p t h", p=p), lf).then_inc(outs_done, 16)
                    last = nt // P - 1 if nt == SEQ else 0
                    pool.dma_start(rows("pool_" + pre), zz[p - HIST:p, last, CU:CU + PW]).then_inc(outs_done, 16)
                pool.wait_ge(is_ready, 16 * (L + 1))
                pool.memset(qk[0:HD, 512:1024], 0.0).then_inc(poolw_zero, 1)
                pool.dma_start(hist, t_in["state_c_pool"][L, 0]).then_inc(poolw_loaded, 16)
                pool.wait_ge(poolw_zero, L + 1)
                for g in range(4):
                    pool.dma_start(poolw[:, g, (g % 2) * HD:(g % 2 + 1) * HD], t_in["pool_w"][L, g]).then_inc(poolw_loaded, 16)
                for j in range(1, GBODY):
                    low(("gates", L), 0, j)
                with pool.Fori(1, GITER) as it:
                    for j in range(GBODY):
                        low(("gates", L), it, j)
                with pool.Fori(0, 2) as it:
                    for j in range(2):
                        low(("out", L), it, j)
            pool.wait_ge(ot_evac, DEPTH * NTM)
            pool.dma_start(iota[:, :], t_in["c_iota"]).then_inc(iota_loaded, 16)
            pool.wait_ge(table_ready, 1)
            passes = pool.value_load(etab[0:1, MAX_PASS:MAX_PASS + 1], min_val=NEXP, max_val=MAX_PASS - 1)
            with pool.Fori(0, passes) as it:
                pool.wait_ge(gc_evac, it + 1)
                for f in range(FB):
                    pool.wait_ge(sg_ready, it * FB + (2 * FB + f + 1))
                    G.tensor_tensor(sge[f % 2], sge[f % 2], gcomp, ALU.mult).then_inc(e_gated, 1)
                    pool.wait_ge(hid_high, it * FB + (f + 1))
                    G.tensor_tensor(hidE[:, f, 1, :], hide[f % 2], hidE[:, f, 0, :].bitcast(FP), ALU.subtract)\
                        .then_inc(hid_ready, 1)

        @block.tensor
        def _(pe):
            mm = nc.tensor.matmul

            def landed(name, it, j):
                pe.wait_ge(slot_full[j % NSLOT], ring.full(name, it, j))

            pe.wait_ge(consts_loaded, 96)
            pe.wait_ge(x_loaded, 32)
            for t in range(TILES):
                for g in range(2):
                    i = 2 * t + g
                    if i >= 8:
                        pe.wait_ge(xt_evac, i - 7)
                    for q in range(4):
                        last = nc.tensor.transpose(ps[:, i % 8, q * P:q * P + ROWS[t]],
                                                   xin[0:ROWS[t], t, (4 * g + q) * P:(4 * g + q + 1) * P],
                                                   ident[0:ROWS[t], 0:ROWS[t]])
                    last.then_inc(xt_ready, 1)
            pe.wait_ge(vrow_loaded, 16 * 14)
            pe.wait_ge(xt_evac, 10)
            for L in range(DEPTH):
                last = nc.tensor.transpose(ps[:, L, 0:V_ROWS], vrow[0:V_ROWS, L, :], ident[0:V_ROWS, 0:V_ROWS])
            last.then_inc(vt_ready, 1)
            pe.wait_ge(memsets, 1)

            def norm_sums(n, releases=False):
                for k in range(KD):
                    pe.wait_ge(sq_ready, KD * n + k + 1)
                    for h in range(2):
                        last = mm(ps[:, h, 0:HALF], ones[:, :], sqs[n % 2][:, k, h * HALF:(h + 1) * HALF],
                                  start=(k == 0), stop=(k == KD - 1))
                        if releases and k == h == 0:
                            last.then_inc(block_begun, 1)
                last.then_inc(ms_ready, 1)

            def features(out_pair, lhs, rhs, nk, begins=False):
                for k in range(nk):
                    for h in range(2):
                        last = mm(ps[:, 2 * out_pair + h, 0:HALF], lhs(k), rhs(k)[:, h * HALF:(h + 1) * HALF],
                                  start=(k == 0), stop=(k == nk - 1))
                        if begins and k == h == 0:
                            last.then_inc(block_begun, 1)
                return last

            for L in range(DEPTH):
                if L:
                    pe.wait_ge(x_upd, xu(L - 1, "ffn"))
                norm_sums(2 * L)
                if L == 0:
                    pe.wait_ge(csil_ready, 1)
                pe.wait_ge(v_ready, 2 * L + 1)
                with pe.Fori(0, 6) as it:
                    for j in range(4):
                        landed(("ada", L), it, j)
                        w = slots[:, j, :].rearrange("p (k n) -> p k n", k=KD)
                        for k in range(KD):
                            last = mm(ps[0:2, j, 0:256], csil[:, k, :], w[:, k, :], start=(k == 0), stop=(k == KD - 1))
                            if k == 0:
                                last.then_inc(block_begun, 1)
                        last.then_inc(ada_row, 1)
                        for i in ([j - 1] if j else []) + ([3] if j == 3 else []):
                            pe.wait_ge(ada_copied, it * 4 + (24 * L + i + 1))
                            for f in range(2):
                                last = mm(ps[:, 7, ds(it * 16 + (i * 4 + f * 2), 2)], mrow[:, i, f * P:(f + 1) * P],
                                          ident[0:2, 0:2], start=True, stop=True)
                            last.then_inc(ada_done, 1)
                with pe.Fori(0, ZITER) as it:
                    for j in range(ZBODY):
                        wh, wl, _ = proj_parts(("z", L), j)
                        for t in range(TILES):
                            g = j * TILES + t
                            if g >= TILES - 1:
                                pe.wait_ge(z_evac, it * (ZBODY * TILES) + (NZ * L + g - TILES + 2))
                            for k in range(KD):
                                if g == 0:
                                    pe.wait_ge(hl_ready, KD * L + k + 1)
                                if t == 0 and k % 4 == 0:
                                    pe.wait_ge(pw_split, proj_halves(("z", L), it, j) + k // 4)
                                for i, (h, w) in enumerate(((hH, wh), (hH, wl), (hL, wh))):
                                    last = mm(ps[0:ROWS[t], t, 0:ZB], h[:, k, tok(t)], w[:, k * ZB:(k + 1) * ZB],
                                              start=(k == i == 0), stop=(k == KD - 1 and i == 2))
                                    if t == k == i == 0:
                                        last.then_inc(block_begun, 1)
                            last.then_inc(z_ready, 1)
                    pe.wait_ge(z_evac, it * (ZBODY * TILES) + (NZ * L + ZBODY * TILES - 1))
                pe.wait_ge(z_evac, NZ * (L + 1))
                pe.wait_ge(rope_done, 6 * (L + 1))
                pe.wait_ge(past_loaded, 48 * (L + 1))

                nc.tensor.transpose(ps[0:HD, 5, 0:P], past[:, 128:192], ident[:, :]).then_inc(ti_ready, 1)
                for t in range(TILES):
                    r = ROWS[t]
                    for b in range(2):
                        nc.tensor.transpose(ps[:, t, b * P:b * P + r], z[0:r, t, IQ + b * P:IQ + (b + 1) * P],
                                            ident[0:r, 0:r])
                    nc.tensor.transpose(ps[0:HD, t, 256:256 + r], z[0:r, t, IK:IK + HD], ident[0:r, 0:r])\
                        .then_inc(ti_ready, 1)
                pe.wait_ge(ti_evac, 6 * (L + 1))
                q = 0
                for t in range(1, TILES):
                    for h in range(IH):
                        if q >= 4:
                            pe.wait_ge(is_relu, 16 * L + q - 3)
                        p0 = (h % 2) * HD
                        mm(ps[0:ROWS[t], q % 4, 0:KW[t]], iqT[p0:p0 + HD, h // 2, tok(t)],
                           ikT[p0:p0 + HD, KCOL[t]:KCOL[t] + KW[t]], start=True, stop=True).then_inc(is_ready, 1)
                        q += 1
                pe.wait_ge(is_relu, 16 * (L + 1))
                def parts_product(out_pair, wh, wl, rh, rl, k, f, begins):
                    c = slice(k * 2 * P + f * P, k * 2 * P + (f + 1) * P)
                    for a in range(2):
                        n = slice(a * HALF, (a + 1) * HALF)
                        for i, (w, r) in enumerate(((wh, rh), (wl, rh), (wh, rl))):
                            last = mm(ps[:, 2 * out_pair + a, 0:HALF], w[:, c], r[:, n],
                                      start=(k == i == 0), stop=(k == KD - 1 and i == 2))
                            if begins and k == a == i == 0:
                                last.then_inc(block_begun, 1)
                    return last

                def gate_blocks(it, h_high):
                    for j in range(GBODY):
                        wh, wl, _ = proj_parts(("gates", L), j)
                        for f in range(2):
                            g = 2 * j + f
                            if g >= 3:
                                pe.wait_ge(g_evac, it * 8 + (24 * L + g - 2))
                            for k in range(KD):
                                if f == 0 and k % 4 == 0:
                                    pe.wait_ge(pw_split, proj_halves(("gates", L), it, j) + k // 4)
                                last = parts_product(g % 4, wh, wl, h_high[:, k], hL[:, k], k, f, f == 0)
                            last.then_inc(g_ready, 1)
                    pe.wait_ge(g_evac, it * 8 + (24 * L + 7))

                with pe.Fori(0, GITER - 1) as it:
                    gate_blocks(it, hH)
                pe.wait_ge(hh_moved, KD * (L + 1))
                gate_blocks(GITER - 1, hH2)
                pe.wait_ge(g_evac, 24 * (L + 1))
                pe.wait_ge(logf_ready, L + 1)
                for t in range(SAMPLE):
                    for s in range(t + 1):
                        mm(ps[0:BH, 6, t * P:(t + 1) * P], logf[:, s, :], (tri if s == t else ones)[:, :],
                           start=(s == 0), stop=(s == t))
                plf = past[:, 960:966]
                mm(ps[0:BH, 7, 0:PAST], plf, tri[:, :], start=True, stop=True)
                mm(ps[0:BH, 7, PAST:PAST + DEC], plf, ones[:, 0:DEC], start=True, stop=False)
                mm(ps[0:BH, 7, PAST:PAST + DEC], logf[:, SAMPLE, :], tri[:, 0:DEC], start=False, stop=True)\
                    .then_inc(cum_ready, 1)
                pe.wait_ge(pool_mats_loaded, 16 * (L + 1))
                pe.wait_ge(poolw_loaded, 80 * (L + 1))
                for t in range(TILES):
                    r = ROWS[t]
                    for g in range(4):
                        c0 = CU + g * HD
                        o = ps[0:HD, t, g * P:g * P + r]
                        if t == SAMPLE:
                            mm(o, hist[:, g * HD:(g + 1) * HD], poolm[0:HIST, 3, P + g * DEC:P + (g + 1) * DEC],
                               start=True, stop=False)
                            last = mm(o, z[0:DEC, t, c0:c0 + HD], poolm[0:DEC, 3, g * DEC:(g + 1) * DEC],
                                      start=False, stop=True)
                            continue
                        last = mm(o, z[:, t, c0:c0 + HD], poolm[:, 1 if t == 0 else 0, g * P:(g + 1) * P],
                                  start=True, stop=(t == 0))
                        if t:
                            last = mm(o, z[:, t - 1, c0:c0 + HD], poolm[:, 2, g * P:(g + 1) * P],
                                      start=False, stop=True)
                    last.then_inc(pm_ready, 1)
                for t in range(TILES):
                    r = ROWS[t]
                    pe.wait_ge(pm_evac, TILES * L + t + 1)
                    if t:
                        pe.wait_ge(po_evac, TILES * L + t)
                    for pr in range(2):
                        for i in range(2):
                            g = 2 * pr + i
                            last = mm(ps[:, 5, pr * P:pr * P + r], poolw[:, g, :], pooled[:, g * P:g * P + r],
                                      start=(i == 0), stop=(i == 1))
                    last.then_inc(po_ready, 1)
                pe.wait_ge(po_evac, TILES * (L + 1))
                pe.wait_ge(cum_evac, L + 1)
                for i, (kind, t) in enumerate(at_groups):
                    if i >= 8:
                        if at_on_act[i - 8]:
                            pe.wait_ge(at_evac_act, N_AT_ACT * L + sum(at_on_act[:i - 7]))
                        else:
                            pe.wait_ge(at_evac_dve, N_AT_DVE * L + (i - 7) - sum(at_on_act[:i - 7]))
                    b = i % 8
                    if kind == "past":
                        nc.tensor.transpose(ps[0:HD, b, 0:P], past[:, 0:HD], ident[:, :])
                        src = [past[:, 192 + q * P:192 + (q + 1) * P] for q in range(3)]
                        first, r = 1, P
                    else:
                        r = ROWS[t]
                        c0 = {"a": AQ, "bq": BQ, "bk": BK}[kind]
                        src = [z[0:r, t, c0 + q * P:c0 + (q + 1) * P] for q in range(3)]
                        first = 0
                        if kind == "a":
                            nc.tensor.transpose(ps[0:HD, b, 3 * P:3 * P + r], z[0:r, t, AK:AK + HD], ident[0:r, 0:r])
                    for q, s in enumerate(src):
                        last = nc.tensor.transpose(ps[:, b, (first + q) * P:(first + q) * P + r], s, ident[0:r, 0:r])
                    last.then_inc(at_ready, 1)
                pe.wait_ge(at_evac_act, N_AT_ACT * (L + 1))
                pe.wait_ge(at_evac_dve, N_AT_DVE * (L + 1))
                pe.wait_ge(mask_ready, 4 * (L + 1))
                pe.wait_ge(identb_ready, 1)
                landed(("pooled", L), 0, 0)
                w = slots[:, 0, :].rearrange("p (k n) -> p k n", k=2)
                for f in range(KD):
                    if f >= 4:
                        pe.wait_ge(b_evac, 24 * L + f - 3)
                    features(f % 4, lambda k: w[:, k, f * P:(f + 1) * P], lambda k: oT[:, 6 + k, :], 2, f == 0)\
                        .then_inc(b_ready, 1)
                pe.wait_ge(b_evac, 24 * L + KD)
                base = NATT * L

                def transpose_block(j, b):
                    if not 0 <= j < NATT or b >= len(key_blocks(items[j][0])):
                        return
                    t = items[j][0]
                    if b == 0:
                        pe.wait_ge(p_ready, base + j + 1)
                        if j >= 2:
                            pe.wait_ge(pt_evac, base + j - 1)
                    c0, kr, _ = key_blocks(t)[b]
                    last = nc.tensor.transpose(ps[0:kr, 3 + j % 2, b * P:b * P + ROWS[t]],
                                               probs[j % 2][0:ROWS[t], c0:c0 + kr], ident[0:ROWS[t], 0:ROWS[t]])
                    if b == len(key_blocks(t)) - 1:
                        last.then_inc(pt_ready, 1)

                def value_block(j, b):
                    if not 0 <= j < NATT or b >= len(key_blocks(items[j][0])):
                        return
                    t, m, h = items[j]
                    tm = j // AH
                    if b == 0:
                        pe.wait_ge(pt_evac, base + j + 1)
                        if h == 0 and tm >= 2:
                            pe.wait_ge(o_evac, NTM * L + tm - 1)
                    _, kr, src = key_blocks(t)[b]
                    if src == "past":
                        v = past[:, HD:2 * HD] if m == 0 else past[:, 576 + h * HD:576 + (h + 1) * HD]
                    else:
                        c = AV if m == 0 else BV + h * HD
                        v = z[0:kr, src, c:c + HD]
                    final = b == len(key_blocks(t)) - 1
                    last = mm(ps[0:ROWS[t], 5 + tm % 2, h * HD:(h + 1) * HD], probsT[j % 2][0:kr, b * P:b * P + ROWS[t]],
                              v, start=(b == 0), stop=final)
                    if final:
                        last.then_inc(pv_done, 1)

                for i in range(NATT + 5):
                    rest = 0
                    if i < NATT:
                        t, m, h = items[i]
                        r, w = ROWS[t], KW[t]
                        if i >= 3:
                            pe.wait_ge(p_ready, base + i - 2)
                        p0 = (h % 2) * HD
                        qT, kT = (aqT[p0:p0 + HD, h // 2], akT[p0:p0 + HD, :]) if m == 0 else \
                                 (bqT[p0:p0 + HD, h // 2], bkT[p0:p0 + HD, h // 2])
                        out = ps[0:r, i % 3, 0:w]
                        first = mm(out, qT[:, tok(t)], kT[:, KCOL[t]:KCOL[t] + w], start=True, stop=False)
                        if i == 0:
                            first.then_inc(block_begun, 1)
                        transpose_block(i - 2, 0)
                        rest = 1
                        if m == 0:
                            last = mm(out, identb[0:r, 0:r], amask[0:r, MOFF[t]:MOFF[t] + w], start=False, stop=True)
                        else:
                            mm(out, sel[0:3 * 32, h:h + 1].to_broadcast([3 * 32, r]), negcum3[:, KCOL[t]:KCOL[t] + w],
                               start=False, stop=False)
                            transpose_block(i - 2, 1)
                            rest = 2
                            last = mm(ps[0:r, i % 3, w - r:w], identb[0:r, 0:r], cmask[0:r, 0:r], start=False, stop=True)
                        last.then_inc(s_ready, 1)
                    for b in range(SAMPLE):
                        transpose_block(i - 2, rest + b)
                        value_block(i - 3, b)
                    j = i - 4
                    if 0 <= j < NATT and j % AH == AH - 1:
                        t, m, h = items[j]
                        tm = j // AH
                        pe.wait_ge(o_evac, NTM * L + tm + 1)
                        if tm:
                            pe.wait_ge(ot_evac, NTM * L + tm)
                        r = ROWS[t]
                        c = BQ if m else AQ
                        for q in range(3):
                            last = nc.tensor.transpose(ps[:, 7, q * P:q * P + r], z[0:r, t, c + q * P:c + (q + 1) * P],
                                                       ident[0:r, 0:r])
                        last.then_inc(ot_ready, 1)
                pe.wait_ge(ot_evac, NTM * (L + 1))
                with pe.Fori(0, 2) as it:
                    for j in range(2):
                        landed(("branch", L), it, j)
                        w = slots[:, j, :].rearrange("p (k n) -> p k n", k=KD)
                        for f in range(2):
                            for i, (a, b) in enumerate(((0, 3), (3, 6))):
                                g = (2 * j + f) * 2 + i
                                if g >= 3:
                                    pe.wait_ge(b_evac, it * 8 + (24 * L + KD + g - 2))
                                last = features(g % 4, lambda k: w[:, a + k, f * P:(f + 1) * P],
                                                lambda k: oT[:, a + k, :], b - a, f == i == 0)
                                last.then_inc(b_ready, 1)
                    pe.wait_ge(b_evac, it * 8 + (24 * L + KD + 7))
                pe.wait_ge(b_evac, 24 * (L + 1))
                with pe.Fori(0, 2) as it:
                    for j in range(2):
                        wh, wl, _ = proj_parts(("out", L), j)
                        for f in range(2):
                            g = 2 * j + f
                            if g == 3:
                                pe.wait_ge(x_upd, it * 4 + (xu(L, "start") + 1))
                            for k in range(KD):
                                if f == 0 and k % 4 == 0:
                                    pe.wait_ge(pw_split, proj_halves(("out", L), it, j) + k // 4)
                                if g == 0:
                                    pe.wait_ge(ml_ready, KD * L + k + 1)
                                last = parts_product(g, wh, wl, hR[:, 0, k], gTr[:, k], k, f, f == 0)
                            last.then_inc(r_ready, 1)
                    pe.wait_ge(x_upd, it * 4 + (xu(L, "start") + 3))
                pe.wait_ge(x_upd, xu(L, "out"))
                norm_sums(2 * L + 1, releases=True)
                if L == 1:
                    for k in range(KD):
                        pe.wait_ge(h_ready, KD * (2 * L + 1) + k + 1)
                        for a in range(2):
                            last = mm(ps[0:NEXP, 4 + a, 0:HALF], rw[:, k, :], hT[:, k, a * HALF:(a + 1) * HALF],
                                      start=(k == 0), stop=(k == KD - 1))
                    last.then_inc(rl_rows, 1)
                    pe.wait_ge(rl_copied, 1)
                    for t in range(TILES):
                        last = nc.tensor.transpose(ps[0:ROWS[t], 6, t * NEXP:(t + 1) * NEXP], rowT[:, tok(t)],
                                                   ident[0:NEXP, 0:NEXP])
                    last.then_inc(rl_ready, 1)
                    for i in range(2 * TILES):
                        t, g = i // 2, i % 2
                        if i >= 4:
                            pe.wait_ge(htok_ready, i - 3)
                        for q in range(4):
                            last = nc.tensor.transpose(ps[0:ROWS[t], i % 4, q * P:(q + 1) * P], hT[:, 4 * g + q, tok(t)],
                                                       ident[:, :])
                        last.then_inc(ht_ready, 1)
                    pe.wait_ge(sel_ready, 1)
                    for t in range(TILES):
                        for q in range(t + 1):
                            mm(ps[:, 5, t * NEXP:(t + 1) * NEXP], (tri if q == t else ones)[:, :], rt[3][:, q, :],
                               start=(q == 0), stop=(q == t))
                    for t in range(TILES):
                        last = mm(ps[:, 5, TILES * NEXP:(TILES + 1) * NEXP], ones[:, :], rt[3][:, t, :],
                                  start=(t == 0), stop=(t == TILES - 1))
                    last.then_inc(cnt_ready, 1)
                    pe.wait_ge(gate_ready, 1)
                    for t in range(TILES):
                        bank, c0 = (6, t * P) if t < SAMPLE else (7, 0)
                        last = nc.tensor.transpose(ps[0:NEXP, bank, c0:c0 + ROWS[t]], rowno[0:ROWS[t], t, :],
                                                   ident[0:ROWS[t], 0:ROWS[t]])
                    last.then_inc(gt_ready, 1)
                    pe.wait_ge(gt_evac, 1)
                    pe.wait_ge(htok_ready, 2 * TILES)
                    for e in range(NEXP):
                        if e >= 2:
                            pe.wait_ge(gb_evac, e - 1)
                        for h in range(2):
                            last = mm(ps[:, 2 * (e % 2) + h, 0:HALF], ident[0:NEXP, e:e + 1].to_broadcast([NEXP, P]),
                                      rowT[:, h * HALF:(h + 1) * HALF], start=True, stop=True)
                        last.then_inc(gb_ready, 1)
                    pe.wait_ge(gb_evac, NEXP)
                    pe.wait_ge(table_ready, 1)
                    passes = pe.value_load(etab[0:1, MAX_PASS:MAX_PASS + 1], min_val=NEXP, max_val=MAX_PASS - 1)
                    U = 2 * (FB + KD)
                    w0 = HALVES * U

                    def gather(n):
                        pe.wait_ge(pick_ready, n + 1)
                        for k in range(KD):
                            b = 4 + k % 2
                            if k == 0:
                                pe.wait_ge(x_upd, (n - 1) * KD + xu(L, "out") if not isinstance(n, int) else xu(L, "out"))
                            if k >= 2:
                                pe.wait_ge(gath_evac, n * KD + (k - 1))
                            for part in range(2):
                                for t in range(TILES):
                                    last = mm(ps[:, b, part * CAP:(part + 1) * CAP], hTok[:, part, t, k * P:(k + 1) * P],
                                              pick[:, t, :], start=(t == 0), stop=(t == TILES - 1))
                            last.then_inc(gath_ready, 1)
                        for t in range(TILES):
                            last = mm(ps[:, 6, 0:CAP], gcol[:, t:t + 1].to_broadcast([P, P]), pick[:, t, :].bitcast(FP),
                                      start=(t == 0), stop=(t == TILES - 1))
                        last.then_inc(gc_ready, 1)

                    gather(0)
                    with pe.Fori(0, passes) as it:

                        def unit(bank, j, w, nk, rhs, first, final):
                            u = 2 * j + w
                            pe.wait_ge(w_split, it * U + (w0 + 2 * order(j) + w + 1))
                            for k in range(nk):
                                a, b = first and k == 0, final and k == nk - 1
                                parts = [(0, 2 * CAP), (1, CAP)]
                                for part, n in parts[::-1] if b else parts:
                                    last = mm(ps[:, bank, 0:n], wE[u % NWB][:, part, k * P:(k + 1) * P],
                                              rhs(k).rearrange("p a n -> p (a n)")[:, 0:n],
                                              start=a and part == 0, stop=b and part == 0)
                            last.then_inc(unit_done[0], 1)

                        pe.wait_ge(gath_evac, (it + 1) * KD)
                        for f in range(FB):
                            if f >= 2:
                                pe.wait_ge(gsum_ready, it * FB + (f - 1))
                            unit(f % 2, f, 0, KD, lambda k: hg[:, k], True, True)
                            if f >= 2:
                                pe.wait_ge(usum_ready, it * FB + (f - 1))
                            unit(2 + f % 2, f, 1, KD, lambda k: hg[:, k], True, True)
                        gather(it + 1)
                        pe.wait_ge(hid_ready, it * FB + 3 * FB)

                        def to_tokens(d):
                            pe.wait_ge(yc_ready, it * KD + (d + 1))
                            if d >= 2:
                                pe.wait_ge(y_split, it * KD + (d - 1))
                            for c in range(2):
                                last = nc.tensor.transpose(ps[0:CH, 2 + d % 2, c * P:(c + 1) * P],
                                                           yT[:, d % 2, c * CH:(c + 1) * CH], ident[:, :])
                            last.then_inc(ytok_ready, 1)

                        def scatter(d):
                            pe.wait_ge(y_split, it * KD + (d + 1))
                            if d == 0:
                                pe.wait_ge(pickT_ready, it + 1)
                                pe.wait_ge(gath_evac, (it + 1) * KD + KD)
                                pe.wait_ge(gc_evac, it + 2)
                            if d >= 2:
                                pe.wait_ge(x_upd, it * KD + (xu(L, "out") + d - 1))
                            for h in range(2):
                                i = 0
                                for c in range(2):
                                    for part in range(2):
                                        last = mm(ps[:, 4 + 2 * (d % 2) + h, 0:HALF], yR[:, d % 2, part, c, :],
                                                  pickT[:, c, h * HALF:(h + 1) * HALF], start=(i == 0), stop=(i == 3))
                                        i += 1
                            last.then_inc(sc_ready, 1)

                        for d in range(KD + 2):
                            if d < KD:
                                if d >= 2:
                                    pe.wait_ge(yc_ready, it * KD + (d - 1))
                                unit(d % 2, FB + d, 0, FLO, lambda k: hidE[:, k], True, False)
                                unit(d % 2, FB + d, 1, FB - FLO, lambda k: hidE[:, FLO + k], False, True)
                            if 1 <= d <= KD:
                                to_tokens(d - 1)
                            if d >= 2:
                                scatter(d - 2)
                    continue
                pe.wait_ge(h_split, KD * (L + 1))

                def split_product(out_pair, buf, nk, rhs, first, last_part, each=None):
                    for k in range(nk):
                        if each:
                            each(k)
                        for h in range(2):
                            c = slice(h * HALF, (h + 1) * HALF)
                            for i, (a, b) in enumerate(((0, 0), (0, 1), (1, 0))):
                                last = mm(ps[:, 2 * out_pair + h, 0:HALF], wR[:, buf, a, k * P:(k + 1) * P], rhs(k, b)[:, c],
                                          start=(first and k == 0 and i == 0), stop=(last_part and k == nk - 1 and i == 2))
                    last.then_inc(unit_done[buf], 1)

                with pe.Fori(0, HALVES) as it:
                    n0 = fexp_base[L]
                    units = 2 * (FB + KD)

                    def unit_split(j, w):
                        pe.wait_ge(w_split, it * units + (n0 * units + 2 * j + w + 1))

                    for f in range(FB):
                        q = 2 * (f % 2)
                        if f < 2:
                            pe.wait_ge(x_upd, it * KD + (xu(L, "out") - (1 if f == 0 else 0)))
                        else:
                            pe.wait_ge(sg_ready, it * FB + (n0 * FB + f - 1))
                        unit_split(f, 0)
                        split_product(q, 0, KD, lambda k, b: hR[:, b, k, :], True, True)
                        if f == 0:
                            pe.wait_ge(x_upd, it * KD + xu(L, "out"))
                        if f >= 2:
                            pe.wait_ge(hid_ready, it * FB + (n0 * FB + f - 1))
                        unit_split(f, 1)
                        split_product(q + 1, 1, KD, lambda k, b: hR[:, b, k, :], True, True)
                    for d in range(KD):
                        if d < 2:
                            pe.wait_ge(hid_ready, it * FB + (n0 * FB + FB - 1))
                        elif d >= 4:
                            pe.wait_ge(x_upd, it * KD + (xu(L, "out") + d - 3))

                        def hid_there(k):
                            if d == 0 and k == FB - FLO - 1:
                                pe.wait_ge(hid_ready, it * FB + (n0 * FB + FB))

                        unit_split(FB + d, 0)
                        split_product((d + 2) % 4, 0, FLO, lambda k, b: hidR[:, b, k, :], True, False)
                        unit_split(FB + d, 1)
                        split_product((d + 2) % 4, 1, FB - FLO, lambda k, b: hidR[:, b, FLO + k, :], False, True, hid_there)
            pe.wait_ge(x_upd, passes * KD + xu(DEPTH - 1, "out"))
            norm_sums(2 * DEPTH)
            pe.wait_ge(h_ready, KD * (2 * DEPTH + 1))
            for t in range(TILES):
                for g in range(2):
                    i = 2 * t + g
                    if i >= 8:
                        pe.wait_ge(y_evac, i - 7)
                    for q in range(4):
                        last = nc.tensor.transpose(ps[0:ROWS[t], i % 8, q * P:(q + 1) * P], hT[:, 4 * g + q, tok(t)],
                                                   ident[:, :])
                    last.then_inc(y_ready, 1)

        @block.scalar
        def _(act):
            ch = Chain(act, act_chain)
            A = nc.scalar.activation

            for t in range(TILES):
                for g in range(2):
                    act.wait_ge(xt_ready, 2 * t + g + 1)
                    A(xT[:, 4 * g:4 * g + 4, tok(t)],
                      ps[:, (2 * t + g) % 8, :].rearrange("p (q n) -> p q n", q=4)[:, :, 0:ROWS[t]], ACT.Copy)\
                        .then_inc(xt_evac, 1)
            act.wait_ge(vt_evac, 1)
            A(csil[:, :, :], vecT[:, 0, V_C:V_C + 16].rearrange("p (s k) -> p k s", s=2), ACT.Silu).then_inc(csil_ready, 1)

            def squares(n, x_there):
                for k in range(KD):
                    if x_there is not None:
                        act.wait_ge(x_upd, x_there + k + 1)
                    elif k == 0:
                        act.wait_ge(xt_evac, 10)
                    A(sqs[n % 2][:, k, :], xT[:, k, :], ACT.Square).then_inc(sq_ready, 1)

            def root(n):
                act.wait_ge(v_ready, n + 1)
                A(oT[:, 1, :], oT[:, 0, :], ACT.Sqrt).then_inc(root_ready, 1)

            def norm(n, gain, shift, stage_mod, split=False):
                if stage_mod:
                    act.wait_ge(mod_ready, stage_mod)
                for k in range(KD):
                    act.wait_ge(normed, KD * n + k + 1)
                    for s, c in ((0, slice(0, SEQ)), (1, slice(SEQ, NTOK))):
                        if shift is None:
                            last = A(hT[:, k, c], hT[:, k, c], ACT.Copy, scale=gain(k, s))
                        else:
                            last = A(hT[:, k, c], hT[:, k, c], ACT.Identity, scale=gain(k, s), bias=shift(k, s))
                    last.then_inc(h_ready, 1)
                    if n == 1:
                        act.wait_ge(h_ready, KD * n + k + 1)
                        A(hR[:, 0, k, :], hT[:, k, :], ACT.Copy).then_inc(hh2_ready, 1)
                    if split:
                        act.wait_ge(h_ready, KD * n + k + 1)
                        A(hH[:, k, :], hT[:, k, :], ACT.Copy).then_inc(hh_ready, 1)
                        if k == 1:
                            proj_high(("z", n // 2), 0, 0)

            for L in range(DEPTH):
                def proj_high(name, it, j):
                    high, _, w = proj_parts(name, j)
                    raw = slots[:, ring.slot(name, j), 0:KD * w]
                    act.wait_ge(slot_full[ring.slot(name, j)], ring.full(name, it, j))
                    act.wait_ge(block_begun, ring.released(name, it, j, ZBODY if name[0] == "z" else 2))
                    for half in range(2):
                        c = slice(half * 4 * w, (half + 1) * 4 * w)
                        A(high[:, c], raw[:, c], ACT.Copy).then_inc(pw_high, 1)

                squares(2 * L, xu(L - 1, "ffn") - KD if L else None)
                root(2 * L)
                with act.Fori(0, 6) as it:
                    for j in range(4):
                        act.wait_ge(ada_row, it * 4 + (24 * L + j + 1))
                        A(mrow[:, j, :], ps[0:2, j, 0:256], ACT.Copy).then_inc(ada_copied, 1)
                norm(2 * L, lambda k, s: scl[:, 0, k, s:s + 1],
                     lambda k, s: mod[:, M_SH1 + k, s:s + 1], L + 1, split=True)

                def z_blocks(it):
                    for j in range(ZBODY):
                        for t in range(TILES):
                            act.wait_ge(z_ready, it * (ZBODY * TILES) + (NZ * L + j * TILES + t + 1))
                            A(z[0:ROWS[t], t, ds(it * (ZBODY * ZB) + j * ZB, ZB)], ps[0:ROWS[t], t, 0:ZB], ACT.Copy)\
                                .then_inc(z_evac, 1)
                            if t == 0:
                                if j + 1 < ZBODY:
                                    proj_high(("z", L), it, j + 1)
                                elif isinstance(it, int):
                                    proj_high(("gates", L), 0, 0)
                                else:
                                    proj_high(("z", L), it + 1, 0)

                with act.Fori(0, ZITER - 1) as it:
                    z_blocks(it)
                z_blocks(ZITER - 1)
                act.wait_ge(lf_abs, L + 1)
                ch.link(A(lft[:, 2], lft[:, 1], ACT.Exp, scale=-1.0))
                A(lft[:, 2], lft[:, 2], ACT.Ln, bias=1.0).then_inc(lf_ln, 1)
                act.wait_ge(ti_ready, 6 * L + 1)
                A(ikT[0:HD, SEQ:SEQ + PAST], ps[0:HD, 5, 0:P], ACT.Copy)
                A(ikT[HD:P, SEQ:SEQ + PAST], ps[0:HD, 5, 0:P], ACT.Copy).then_inc(ti_evac, 1)
                for t in range(TILES):
                    act.wait_ge(ti_ready, 6 * L + t + 2)
                    A(iqT[:, :, tok(t)], ps[:, t, 0:256].rearrange("p (b n) -> p b n", b=2)[:, :, 0:ROWS[t]], ACT.Copy)
                    A(ikT[0:HD, keycol(t)], ps[0:HD, t, 256:256 + ROWS[t]], ACT.Copy)
                    A(ikT[HD:P, keycol(t)], ps[0:HD, t, 256:256 + ROWS[t]], ACT.Copy).then_inc(ti_evac, 1)
                q = 0
                for t in range(1, TILES):
                    for h in range(IH):
                        act.wait_ge(is_ready, 16 * L + q + 1)
                        if q >= 2:
                            act.wait_ge(is_acc, 16 * L + q - 1)
                        A(rel[q % 2][0:ROWS[t], 0:KW[t]], ps[0:ROWS[t], q % 4, 0:KW[t]], ACT.Relu).then_inc(is_relu, 1)
                        q += 1
                def gate_blocks(it):
                    for g in range(2 * GBODY):
                        if g % 2 == 0:
                            j = g // 2
                            if j + 1 < GBODY:
                                proj_high(("gates", L), it, j + 1)
                            elif not isinstance(it, int):
                                proj_high(("gates", L), it + 1, 0)
                        act.wait_ge(g_ready, it * 8 + (24 * L + g + 1))
                        A(gT[:, ds(it * 8 + g, 1), :].rearrange("p e (a n) -> p (e a) n", a=2), pair(g % 4), ACT.Sigmoid)\
                            .then_inc(g_evac, 1)

                with act.Fori(0, GITER - 1) as it:
                    gate_blocks(it)
                gate_blocks(GITER - 1)
                for i, (kind, t) in enumerate(at_groups):
                    if not at_on_act[i]:
                        continue
                    act.wait_ge(at_ready, N_AT * L + i + 1)
                    src = ps[:, i % 8, :].rearrange("p (q n) -> p q n", q=4)[:, :, 0:ROWS[t]]
                    if kind == "a":
                        A(aqT[:, :, tok(t)], src[:, 0:3, :], ACT.Copy, scale=HD ** -0.5)
                        A(akT[0:HD, keycol(t)], src[0:HD, 3, :], ACT.Copy)
                        A(akT[HD:P, keycol(t)], src[0:HD, 3, :], ACT.Copy).then_inc(at_evac_act, 1)
                    else:
                        A(bkT[:, :, keycol(t)], src[:, 0:3, :], ACT.Copy).then_inc(at_evac_act, 1)
                base = NATT * L

                def ot_copy(j):
                    t, m, h = items[j]
                    tm = j // AH
                    act.wait_ge(ot_ready, NTM * L + tm + 1)
                    A(oT[:, 3 * m:3 * m + 3, tok(t)],
                      ps[:, 7, 0:384].rearrange("p (q n) -> p q n", q=3)[:, :, 0:ROWS[t]], ACT.Copy).then_inc(ot_evac, 1)

                for i in range(NATT):
                    t, m, h = items[i]
                    r, w = ROWS[t], KW[t]
                    tm = i // AH
                    act.wait_ge(mx_ready, base + i + 1)
                    if i >= 2:
                        act.wait_ge(pt_ready, base + i - 1)
                    if h == 0 and tm >= 2:
                        act.wait_ge(o_evac, NTM * L + tm - 1)
                    A(probs[i % 2][0:r, 0:w], ps[0:r, i % 3, 0:w], ACT.Exp, bias=nmax[0:r, i % 12:i % 12 + 1],
                      accum_out=rsum[0:r, tm % 2, h:h + 1]).then_inc(p_ready, 1)
                    if i >= 5 and (i - 5) % AH == AH - 1:
                        ot_copy(i - 5)
                ot_copy(NATT - 1)
                proj_high(("out", L), 0, 0)
                act.wait_ge(outs_done, 160 * (L + 1))
                for k in range(KD):
                    act.wait_ge(m_ready, KD * L + k + 1)
                    A(hR[:, 0, k, :], gT[:, k, :], ACT.Copy).then_inc(mh_ready, 1)
                proj_high(("out", L), 0, 1)
                for j in range(2):
                    proj_high(("out", L), 1, j)
                squares(2 * L + 1, xu(L, "start"))
                root(2 * L + 1)
                norm(2 * L + 1, lambda k, s: scl[:, 1, k, s:s + 1],
                     lambda k, s: mod[:, M_SH2 + k, s:s + 1], 0)
                if L == 1:
                    act.wait_ge(rl_rows, 1)
                    A(halves(rowT), ps[0:NEXP, 4:6, 0:HALF], ACT.Copy).then_inc(rl_copied, 1)
                    act.wait_ge(rexp_in, 1)
                    A(rt[5], rt[5], ACT.Exp).then_inc(rexp_out, 1)
                    for i in range(2 * TILES):
                        t, g = i // 2, i % 2
                        act.wait_ge(ht_ready, i + 1)
                        if t == SAMPLE:
                            act.wait_ge(tokpad, 1)
                        A(hTok[0:ROWS[t], 0, t, g * 512:(g + 1) * 512], ps[0:ROWS[t], i % 4, :], ACT.Copy)\
                            .then_inc(htok_high, 1)
                    act.wait_ge(gt_ready, 1)
                    A(rowT[:, 0:SEQ], ps[0:NEXP, 6, :], ACT.Copy)
                    A(rowT[:, SEQ:NTOK], ps[0:NEXP, 7, 0:DEC], ACT.Copy).then_inc(gt_evac, 1)
                    for e in range(NEXP):
                        act.wait_ge(gb_ready, e + 1)
                        A(halves(rbc[:, e, :]), pair(e % 2), ACT.Copy).then_inc(gb_evac, 1)
                    act.wait_ge(htok_ready, 2 * TILES)
                    act.wait_ge(table_ready, 1)
                    passes = act.value_load(etab[0:1, MAX_PASS:MAX_PASS + 1], min_val=NEXP, max_val=MAX_PASS - 1)
                    U = 2 * (FB + KD)
                    w0, done0 = HALVES * U, HALVES * (FB + KD)

                    def gathered(n):
                        for k in range(KD):
                            act.wait_ge(gath_ready, n * KD + (k + 1))
                            A(hg[:, k, :, :], ps[:, 4 + k % 2, 0:2 * CAP].rearrange("p (a n) -> p a n", a=2), ACT.Copy)\
                                .then_inc(gath_evac, 1)
                        act.wait_ge(gc_ready, n + 1)
                        A(gcomp, ps[:, 6, 0:CAP], ACT.Copy).then_inc(gc_evac, 1)

                    def high(n, j, w):
                        u = 2 * j + w
                        if w == 0:
                            act.wait_ge(slot_full[j % NSLOT], ring.full(("ffn", L), n, j))
                        if j >= 2:
                            act.wait_ge(unit_done[0], n * U + (done0 + u - NWB + 1))
                        elif not isinstance(n, int):
                            act.wait_ge(unit_done[0], n * U + (done0 + w + 1 - (2 if j == 0 else 4)))
                        size = KD * P if j < FB else (FLO if w == 0 else FB - FLO) * P
                        c0 = w * (KD * P if j < FB else FLO * P)
                        A(wE[u % NWB][:, 0, 0:size], slots[:, j % NSLOT, c0:c0 + size], ACT.Copy).then_inc(w_high, 1)

                    gathered(0)
                    for j, w in ((1, 0), (1, 1), (0, 0), (0, 1)):
                        high(0, j, w)
                    with act.Fori(0, passes) as it:

                        def gate_half(f):
                            act.wait_ge(unit_done[0], it * U + (done0 + 2 * f + 1))
                            if f >= 2:
                                act.wait_ge(sg_ready, it * FB + (2 * FB + f - 1))
                            A(gsum[f % 2], ps[:, f % 2, CAP:2 * CAP], ACT.Copy).then_inc(g_half, 1)

                        def up_half(f):
                            act.wait_ge(unit_done[0], it * U + (done0 + 2 * f + 2))
                            if f >= 1:
                                act.wait_ge(hid_ready32, it * FB + f)
                            A(usum, ps[:, 2 + f % 2, CAP:2 * CAP], ACT.Copy).then_inc(u_half, 1)

                        def y_half_part(d):
                            act.wait_ge(unit_done[0], it * U + (done0 + 2 * (FB + d) + 2))
                            if d >= 2:
                                act.wait_ge(ytok_ready, it * KD + (d - 1))
                            A(yT[:, d % 2, :], ps[:, d % 2, CAP:2 * CAP], ACT.Copy).then_inc(y_half, 1)

                        def silu(f):
                            act.wait_ge(gsum_ready, it * FB + (f + 1))
                            if f >= 2:
                                act.wait_ge(hid_ready32, it * FB + (f - 1))
                            A(sge[f % 2], gsum[f % 2], ACT.Silu).then_inc(sg_ready, 1)

                        def hid_high_part(f):
                            act.wait_ge(hid_ready32, it * FB + (f + 1))
                            A(hidE[:, f, 0, :], hide[f % 2], ACT.Copy).then_inc(hid_high, 1)

                        def y_high_part(d):
                            act.wait_ge(ytok_ready, it * KD + (d + 1))
                            if d >= 2:
                                act.wait_ge(sc_ready, it * KD + (d - 1))
                            A(yR[:, d % 2, 0, :, :], ps[0:CH, 2 + d % 2, 0:2 * P].rearrange("p (c n) -> p c n", c=2),
                              ACT.Copy).then_inc(y_high, 1)

                        for b in range(FB + KD):
                            n, j = ahead(it, b)
                            if b < FB:
                                gate_half(b)
                            high(n, j, 0)
                            if b < FB:
                                silu(b)
                                up_half(b)
                            else:
                                y_half_part(b - FB)
                            high(n, j, 1)
                            if b < FB:
                                hid_high_part(b)
                            if b == FB - 1:
                                act.wait_ge(e_gated, (it + 1) * FB)
                                gathered(it + 1)
                            if b > FB:
                                y_high_part(b - FB - 1)
                        y_high_part(KD - 1)
                    continue
                act.wait_ge(h_split, KD * (L + 1))
                with act.Fori(0, HALVES) as it:
                    n0 = fexp_base[L]
                    nb = FB + KD

                    def high(j, w):
                        if w == 0:
                            act.wait_ge(slot_full[j % NSLOT], ring.full(("ffn", L), it, j))
                        if j:
                            act.wait_ge(unit_done[w], it * nb + (n0 * nb + j))
                        else:
                            act.wait_ge(x_upd, it * KD + xu(L, "out"))
                        n = KD * P if j < FB else (FLO if w == 0 else FB - FLO) * P
                        c0 = w * (KD * P if j < FB else FLO * P)
                        A(wR[:, w, 0, 0:n], slots[:, j % NSLOT, c0:c0 + n], ACT.Copy).then_inc(w_high, 1)

                    def silu(f):
                        act.wait_ge(unit_done[0], it * nb + (n0 * nb + f + 1))
                        if f >= 2:
                            act.wait_ge(hid_ready, it * FB + (n0 * FB + f - 1))
                        A(halves(sg[f % 2]), pair(2 * (f % 2)), ACT.Silu).then_inc(sg_ready, 1)

                    for j in range(FB + KD):
                        high(j, 0)
                        if 1 <= j <= FB:
                            silu(j - 1)
                        high(j, 1)
            squares(2 * DEPTH, passes * KD + (xu(DEPTH - 1, "out") - KD))
            root(2 * DEPTH)
            norm(2 * DEPTH, lambda k, s: vecT[:, 0, V_FIN + k:V_FIN + k + 1], None, 0)
            for i in range(2 * TILES):
                t, g = i // 2, i % 2
                act.wait_ge(y_ready, i + 1)
                A(xin[0:ROWS[t], t, g * 512:(g + 1) * 512], ps[0:ROWS[t], i % 8, :], ACT.Copy).then_inc(y_evac, 1)

        @block.vector
        def _(dve):
            ch = Chain(dve, dve_chain)
            V = nc.vector
            V.memset(ones[:, :], 1.0).then_inc(memsets, 1)
            ch.link(V.memset(amask[:, 0:P], 0.0))
            ch.link(V.memset(amask[0:HD, HD:P], NEG))
            ch.link(V.memset(logf[:, :, :], 0.0))
            ch.link(V.memset(lft[:, :, :, :], 0.0))
            dve.wait_ge(consts_loaded, 96)
            ch.link(V.tensor_tensor(score[:, 0:P], tri[:, :], ident[:, :], ALU.subtract))
            ch.link(V.tensor_scalar(cmask[:, :], score[:, 0:P], NEG, None, ALU.mult))
            ch.link(V.tensor_tensor(sel[:, :], ident[:, 0:BH], ident[:, 32:32 + BH], ALU.add))
            ch.link(V.tensor_tensor(sel[:, :], sel[:, :], ident[:, 64:64 + BH], ALU.add))
            V.tensor_copy(identb[:, :], ident[:, :]).then_inc(identb_ready, 1)
            dve.wait_ge(vt_ready, 1)
            V.tensor_copy(vecT[:, :, :], ps[:, 0:2, 0:V_ROWS]).then_inc(vt_evac, 1)

            def stats(n):
                v, s, r, t = (oT[:, i, :] for i in range(4))
                dve.wait_ge(ms_ready, n + 1)
                V.tensor_scalar(halves(v), pair(0), 1.0 / D, NORM_EPS, ALU.mult, ALU.add).then_inc(v_ready, 1)
                dve.wait_ge(root_ready, n + 1)
                ch.link(V.reciprocal(r, s))
                ch.link(V.scalar_tensor_tensor(t, r, -0.5, r, ALU.mult, ALU.mult))
                ch.link(V.tensor_tensor(t, t, v, ALU.mult))
                ch.link(V.scalar_tensor_tensor(r, t, 1.5, r, ALU.add, ALU.mult))
                for k in range(KD):
                    V.tensor_tensor(hT[:, k, :], xT[:, k, :], r, ALU.mult).then_inc(normed, 1)

            for L in range(DEPTH):
                stats(2 * L)
                dve.wait_ge(ada_done, 24 * (L + 1))
                bias = vecT[:, L, V_ADAB:V_ADAB + 48].unsqueeze(2).to_broadcast([P, 48, 2])
                ch.link(V.tensor_tensor(mod[:, :, :], ps[:, 7, 0:96].rearrange("p (b s) -> p b s", s=2), bias, ALU.add))
                for i, (sc0, g0) in enumerate(((M_SC1, V_NMIX), (M_SC2, V_NFFN))):
                    gain = vecT[:, L, g0:g0 + KD].unsqueeze(2).to_broadcast([P, KD, 2])
                    last = V.scalar_tensor_tensor(scl[:, i], mod[:, sc0:sc0 + KD, :], 1.0, gain, ALU.add, ALU.mult)
                last.then_inc(mod_ready, 1)
                for k in range(KD):
                    dve.wait_ge(hh_ready, KD * L + k + 1)
                    V.tensor_tensor(hL[:, k, :], hT[:, k, :], hH[:, k, :].bitcast(FP), ALU.subtract).then_inc(hl_ready, 1)
                tmpf = oT[:, :, :].rearrange("p k n -> p (k n)")

                ropes = [6 * L]

                def rope(c0, nh):
                    for a, b, r in ((0, SAMPLE, P), (SAMPLE, TILES, DEC)):
                        n = b - a
                        v = z[0:r, a:b, c0:c0 + nh * HD].rearrange("p t (h u f) -> p t h u f", h=nh, u=2)
                        x1, x2 = v[:, :, :, 0, :], v[:, :, :, 1, :]
                        cos = cs[0:r, a:b, 0, :].unsqueeze(2).to_broadcast([r, n, nh, 32])
                        sin = cs[0:r, a:b, 1, :].unsqueeze(2).to_broadcast([r, n, nh, 32])
                        tm = [tmpf[0:r, 896 * i:896 * i + n * nh * 32].rearrange("p (t h f) -> p t h f", t=n, h=nh)
                              for i in range(3)]
                        V.tensor_tensor(tm[0], x1, cos, ALU.mult)
                        V.tensor_tensor(tm[1], x2, sin, ALU.mult)
                        ch.link(V.tensor_tensor(tm[2], x1, sin, ALU.mult))
                        V.tensor_tensor(x1, tm[0], tm[1], ALU.subtract)
                        ch.link(V.tensor_tensor(x2, x2, cos, ALU.mult))
                        V.tensor_tensor(x2, x2, tm[2], ALU.add).then_inc(rope_done, 1)
                        ropes[0] += 1
                        dve.wait_ge(rope_done, ropes[0])

                dve.wait_ge(z_evac, NZ * L + 4 * TILES)
                rope(IQ, IH)
                rope(IK, 1)
                rope(AQ, AH + 1)
                dve.wait_ge(z_evac, NZ * L + 8 * TILES)
                for a, b, r in ((0, SAMPLE, P), (SAMPLE, TILES, DEC)):
                    bias = bfb[0:r, L, :].unsqueeze(1).to_broadcast([r, b - a, BH])
                    ch.link(V.tensor_tensor(lft[0:r, 0, a:b, :], z[0:r, a:b, BF_:BF_ + BH], bias, ALU.add))
                V.scalar_tensor_tensor(lft[:, 1], lft[:, 0], -1.0, lft[:, 0], ALU.mult, ALU.max).then_inc(lf_abs, 1)
                dve.wait_ge(lf_ln, L + 1)
                for a, b, r in ((0, SAMPLE, P), (SAMPLE, TILES, DEC)):
                    last = V.scalar_tensor_tensor(logf[0:r, a:b, :], lft[0:r, 0, a:b, :], 0.0, lft[0:r, 2, a:b, :],
                                                  ALU.min, ALU.subtract)
                last.then_inc(logf_ready, 1)
                q = 0
                for t in range(1, TILES):
                    r, w = ROWS[t], KW[t]
                    sc = score[0:r, SOFF[t]:SOFF[t] + w]
                    for h in range(IH):
                        dve.wait_ge(is_relu, 16 * L + q + 1)
                        wt = z[0:r, t, IW + h:IW + h + 1]
                        src = rel[q % 2][0:r, 0:w]
                        if h == 0:
                            last = V.tensor_scalar(sc, src, wt, None, ALU.mult)
                        else:
                            dve.wait_ge(is_acc, 16 * L + q)
                            last = V.scalar_tensor_tensor(sc, src, wt, sc, ALU.mult, ALU.add)
                        last.then_inc(is_acc, 1)
                        q += 1
                dve.wait_ge(is_acc, 16 * (L + 1))
                for t in range(1, SAMPLE):
                    last = V.memset(score[0:CHUNK, SOFF[t] + KW[t] - CHUNK:SOFF[t] + KW[t]], LOWEST)
                ch.link(last)
                for t in range(1, TILES):
                    r, w = ROWS[t], KW[t]
                    kk = K_SAMPLE if t == SAMPLE else K_PROMPT
                    sc, wk = score[0:r, SOFF[t]:SOFF[t] + w], work[0:r, 0:w]
                    ch.link(V.max(m8[0:r, :], sc))
                    ch.link(V.match_replace(wk, m8[0:r, :], sc, LOWEST))
                    rounds = kk // 8 - 2
                    for _ in range(rounds):
                        ch.link(V.max(m8[0:r, :], wk))
                        ch.link(V.match_replace(wk, m8[0:r, :], wk, LOWEST))
                    ch.link(V.max(m8[0:r, :], wk))
                    kth = m8[0:r, 7:8]
                    gt, eq, rk = isgt[0:r, 0:w], iseq[0:r, 0:w], rank[0:r, 0:w]
                    V.tensor_scalar(eq, sc, kth, None, ALU.is_equal)
                    ch.link(V.tensor_scalar(gt, sc, kth, None, ALU.is_gt, ALU.add, accum_out=stat[0:r, 0:1]))
                    ch.link(V.tensor_scalar(stat[0:r, 1:2], stat[0:r, 0:1], -1.0, float(kk), ALU.mult, ALU.add))
                    ch.link(V.tensor_tensor_scan(rk, eq, eq, 0.0, ALU.add, ALU.max))
                    ch.link(V.scalar_tensor_tensor(rk, rk, stat[0:r, 1:2], eq, ALU.is_le, ALU.mult))
                    ch.link(V.tensor_tensor(rk, rk, gt, ALU.add))
                    V.tensor_scalar(amask[0:r, MOFF[t]:MOFF[t] + w], rk, -NEG, NEG, ALU.mult, ALU.add).then_inc(mask_ready, 1)
                    dve.wait_ge(mask_ready, 4 * L + t)
                for k in range(KD):
                    V.tensor_copy(hH2[:, k, :], hH[:, k, :].bitcast(FP)).then_inc(hh_moved, 1)
                dve.wait_ge(cum_ready, L + 1)
                ch.link(V.memset(negcum3[:, :], 0.0))
                V.tensor_scalar(negcum[:, 0:SEQ], ps[0:BH, 6, :], -1.0, None, ALU.mult)
                ch.link(V.tensor_scalar(negcum[:, SEQ:KEYS], ps[0:BH, 7, 0:PAST + DEC], -1.0, None, ALU.mult))
                for i in range(3):
                    ch.link(V.tensor_copy(negpart[:, :], negcum[:, :]))
                    last = V.tensor_copy(negcum3[32 * i:32 * i + BH, :], negpart[:, :])
                    if i < 2:
                        ch.link(last)
                        ch.link(V.tensor_tensor(negcum[:, :], negcum[:, :], negpart[:, :], ALU.subtract))
                last.then_inc(cum_evac, 1)
                for t in range(TILES):
                    r = ROWS[t]
                    dve.wait_ge(pm_ready, TILES * L + t + 1)
                    if t:
                        dve.wait_ge(po_ready, TILES * L + t)
                    v4 = lambda ap: ap.rearrange("p (g n) -> p g n", g=4)[:, :, 0:r]
                    V.tensor_copy(v4(pooled), v4(ps[0:HD, t, :])).then_inc(pm_evac, 1)
                    dve.wait_ge(po_ready, TILES * L + t + 1)
                    for pr in range(2):
                        last = V.tensor_scalar(oT[:, 6 + pr, tok(t)], ps[:, 5, pr * P:pr * P + r],
                                               vecT[:, L, V_PSC + pr:V_PSC + pr + 1], None, ALU.mult)
                    last.then_inc(po_evac, 1)
                for i, (kind, t) in enumerate(at_groups):
                    if at_on_act[i]:
                        continue
                    dve.wait_ge(at_ready, N_AT * L + i + 1)
                    src = ps[:, i % 8, :].rearrange("p (q n) -> p q n", q=4)
                    if kind == "past":
                        V.tensor_copy(akT[0:HD, SEQ:SEQ + PAST], src[0:HD, 0, :])
                        V.tensor_copy(akT[HD:P, SEQ:SEQ + PAST], src[0:HD, 0, :])
                        V.tensor_copy(bkT[:, :, SEQ:SEQ + PAST], src[:, 1:4, :]).then_inc(at_evac_dve, 1)
                    else:
                        V.tensor_scalar(bqT[:, :, tok(t)], src[:, 0:3, 0:ROWS[t]], HD ** -0.5, None, ALU.mult)\
                            .then_inc(at_evac_dve, 1)
                for f in range(KD):
                    dve.wait_ge(b_ready, 24 * L + f + 1)
                    gate = gT[:, 2 * KD + f, :]
                    V.tensor_tensor(halves(gate), pair(f % 4), halves(gate), ALU.mult).then_inc(b_evac, 1)
                base = NATT * L
                for i in range(NATT + 3):
                    if i < NATT:
                        t, m, h = items[i]
                        r = ROWS[t]
                        dve.wait_ge(s_ready, base + i + 1)
                        V.tensor_reduce(nmax[0:r, i % 12:i % 12 + 1], ps[0:r, i % 3, 0:KW[t]], AX.X, ALU.max, negate=True)\
                            .then_inc(mx_ready, 1)
                    j = i - 2
                    if 0 <= j < NATT:
                        t, m, h = items[j]
                        r = ROWS[t]
                        dve.wait_ge(pt_ready, base + j + 1)
                        if j >= 2:
                            dve.wait_ge(pv_done, base + j - 1)
                        nb = len(key_blocks(t))
                        src = ps[:, 3 + j % 2, 0:nb * P].rearrange("p (b n) -> p b n", b=nb)
                        dst = probsT[j % 2][:, 0:nb * P].rearrange("p (b n) -> p b n", b=nb)
                        if t == SAMPLE:
                            V.tensor_copy(dst[:, 0, 0:r], src[:, 0, 0:r])
                            last = V.tensor_copy(dst[0:DEC, 1, 0:r], src[0:DEC, 1, 0:r])
                        else:
                            last = V.tensor_copy(dst, src)
                        last.then_inc(pt_evac, 1)
                    j = i - 3
                    if 0 <= j < NATT and j % AH == AH - 1:
                        t, m, h = items[j]
                        r, tm = ROWS[t], j // AH
                        dve.wait_ge(p_ready, base + j + 1)
                        ch.link(V.reciprocal(rinv[0:r, tm % 2, :], rsum[0:r, tm % 2, :]))
                        dve.wait_ge(pv_done, base + j + 1)
                        c = BQ if m else AQ
                        V.tensor_tensor(z[0:r, t, c:c + AH * HD].rearrange("p (h d) -> p h d", h=AH),
                                        ps[0:r, 5 + tm % 2, 0:AH * HD].rearrange("p (h d) -> p h d", h=AH),
                                        rinv[0:r, tm % 2, :].unsqueeze(2).to_broadcast([r, AH, HD]), ALU.mult)\
                            .then_inc(o_evac, 1)
                with dve.Fori(0, 2) as it:
                    ch.enter(it, 0, 4)
                    for d in range(4):
                        def blk(i):
                            return gT[:, ds(it * 4 + (i * KD + d), 1), :].rearrange("p e n -> p (e n)")
                        for i in range(2):
                            g = 2 * d + i
                            dve.wait_ge(b_ready, it * 8 + (24 * L + KD + g + 1))
                            V.tensor_tensor(halves(blk(i)), pair(g % 4), halves(blk(i)), ALU.mult).then_inc(b_evac, 1)
                            dve.wait_ge(b_evac, it * 8 + (24 * L + KD + g + 1))
                        ch.link(V.tensor_tensor(blk(0), blk(0), blk(1), ALU.add))
                        V.tensor_tensor(blk(0), blk(0), blk(2), ALU.add).then_inc(m_ready, 1)
                ch.leave(2)

                for k in range(KD):
                    dve.wait_ge(mh_ready, KD * L + k + 1)
                    V.tensor_tensor(gTr[:, k, :], gT[:, k, :], hR[:, 0, k, :].bitcast(FP), ALU.subtract).then_inc(ml_ready, 1)

                def residual(pr, k, gate):
                    for s, hh, a, b in ((0, 0, 0, HALF), (0, 1, HALF, SEQ), (1, 1, SEQ, NTOK)):
                        x = xT[:, k, a:b]
                        last = V.scalar_tensor_tensor(x, ps[:, 2 * pr + hh, a - hh * HALF:b - hh * HALF],
                                                      mod[:, gate + k, s:s + 1], x, ALU.mult, ALU.add)
                    last.then_inc(x_upd, 1)

                for d in range(KD):
                    dve.wait_ge(r_ready, KD * L + d + 1)
                    residual(d % 4, d, M_G1)
                dve.wait_ge(x_upd, xu(L, "out"))
                stats(2 * L + 1)
                dve.wait_ge(outs_done, 160 * (L + 1))
                if L == 0:
                    for k in range(KD):
                        dve.wait_ge(hh2_ready, k + 1)
                        V.tensor_tensor(hR[:, 1, k, :], hT[:, k, :], hR[:, 0, k, :].bitcast(FP), ALU.subtract)\
                            .then_inc(h_split, 1)
                if L == 1:
                    lg, eq, gt, rk, pre, ex, ga, c2 = rt
                    V.memset(hTok[:, :, SAMPLE, :].bitcast(FP), 0.0).then_inc(tokpad, 1)
                    dve.wait_ge(rl_ready, 1)
                    ch.link(V.memset(lg, 0.0))
                    dve.wait_ge(rl_ready, 1)
                    for a, b, r in ((0, SAMPLE, P), (SAMPLE, TILES, DEC)):
                        ch.link(V.tensor_tensor(lg[0:r, a:b, :],
                                                ps[0:r, 6, a * NEXP:b * NEXP].rearrange("p (t e) -> p t e", e=NEXP),
                                                rb[0:r, :].unsqueeze(1).to_broadcast([r, b - a, NEXP]), ALU.add))
                    for t in range(TILES):
                        last = V.max(pre[:, t, :], lg[:, t, :])
                    ch.link(last)
                    first = pre[:, :, 0:1].to_broadcast([P, TILES, NEXP])
                    second = pre[:, :, 1:2].to_broadcast([P, TILES, NEXP])
                    V.tensor_tensor(ex, lg, first, ALU.subtract).then_inc(rexp_in, 1)
                    V.tensor_tensor(gt, lg, second, ALU.is_gt)
                    ch.link(V.tensor_tensor(eq, lg, second, ALU.is_equal))
                    for t in range(TILES):
                        last = V.tensor_tensor_scan(rk[:, t, :], eq[:, t, :], eq[:, t, :], 0.0, ALU.add, ALU.max)
                    ch.link(last)
                    ch.link(V.tensor_reduce(c2[:, :, 0:1], gt, AX.X, ALU.add))
                    ch.link(V.tensor_tensor(rk, rk, c2[:, :, 0:1].to_broadcast([P, TILES, NEXP]), ALU.add))
                    ch.link(V.scalar_tensor_tensor(rk, rk, 2.0, eq, ALU.is_le, ALU.mult))
                    ch.link(V.tensor_tensor(rk, rk, gt, ALU.add))
                    dve.wait_ge(rexp_out, 1)
                    ch.link(V.tensor_tensor(ex, ex, rk, ALU.mult))
                    ch.link(V.tensor_reduce(c2[:, :, 0:1], ex, AX.X, ALU.add))
                    ch.link(V.reciprocal(c2[:, :, 1:2], c2[:, :, 0:1]))
                    ch.link(V.tensor_tensor(ga, ex, c2[:, :, 1:2].to_broadcast([P, TILES, NEXP]), ALU.mult))
                    for a, b in ((DEC, 2 * DEC), (2 * DEC, P)):
                        last = V.memset(rk[a:b, SAMPLE, :], 0.0)
                    last.then_inc(sel_ready, 1)
                    dve.wait_ge(sel_ready, 1)
                    for i in range(2 * TILES):
                        t, g = i // 2, i % 2
                        dve.wait_ge(htok_high, i + 1)
                        r, c = ROWS[t], slice(g * 512, (g + 1) * 512)
                        V.tensor_tensor(hTok[0:r, 1, t, c], ps[0:r, i % 4, :], hTok[0:r, 0, t, c].bitcast(FP), ALU.subtract)\
                            .then_inc(htok_ready, 1)
                    dve.wait_ge(cnt_ready, 1)
                    ch.link(V.scalar_tensor_tensor(rowno, ps[:, 5, 0:TILES * NEXP].rearrange("p (t e) -> p t e", t=TILES),
                                                   9999.0, rk, ALU.add, ALU.mult))
                    V.tensor_scalar(rowno, rowno, -10000.0, None, ALU.add).then_inc(gate_ready, 1)
                    cnt, m1, cumm = tab[:, 0:8], tab[:, 8:16], tab[:, 16:24]
                    ch.link(V.tensor_copy(cnt, ps[:, 5, TILES * NEXP:(TILES + 1) * NEXP]))
                    ch.link(V.memset(m1, 1.0))
                    for c in range(1, -(-NTOK // CAP)):
                        ch.link(V.scalar_tensor_tensor(m1, cnt, float(c * CAP), m1, ALU.is_gt, ALU.add))
                    ch.link(V.tensor_tensor_scan(cumm, m1, m1, 0.0, ALU.add, ALU.max))
                    number = iota[:, 0:MAX_PASS]
                    dve.wait_ge(iota_loaded, 16)
                    ch.link(V.tensor_tensor(t3, cumm.unsqueeze(1).to_broadcast([P, MAX_PASS, NEXP]),
                                            number.unsqueeze(2).to_broadcast([P, MAX_PASS, NEXP]), ALU.is_le))
                    ch.link(V.tensor_reduce(epass, t3, AX.X, ALU.add))
                    ch.link(V.tensor_tensor(t3, t3, m1.unsqueeze(1).to_broadcast([P, MAX_PASS, NEXP]), ALU.mult))
                    ch.link(V.tensor_reduce(spass, t3, AX.X, ALU.add))
                    ch.link(V.tensor_scalar(epass, epass, float(NEXP - 1), None, ALU.min))
                    ch.link(V.tensor_tensor(cpass, spass, number, ALU.subtract))
                    ch.link(V.tensor_scalar(cpass, cpass, float(CAP), None, ALU.mult))
                    ch.link(V.tensor_copy(etab[:, 0:MAX_PASS], epass))
                    V.tensor_copy(etab[:, MAX_PASS:MAX_PASS + 1], cumm[:, NEXP - 1:NEXP]).then_inc(table_ready, 1)
                    dve.wait_ge(table_ready, 1)
                    passes = dve.value_load(etab[0:1, MAX_PASS:MAX_PASS + 1], min_val=NEXP, max_val=MAX_PASS - 1)
                    U = 2 * (FB + KD)
                    w0, done0 = HALVES * U, HALVES * (FB + KD)

                    def select(n, e):
                        V.tensor_copy(gcol, ga[:, :, ds(e, 1)].rearrange("p t e -> p (t e)"))
                        ch.link(V.tensor_scalar(rcol, rowno[:, :, ds(e, 1)].rearrange("p t e -> p (t e)"),
                                                cpass[:, ds(n, 1)], None, ALU.add))
                        for t in range(TILES):
                            last = V.tensor_scalar(pick[:, t, :], iota[:, 0:CAP], rcol[:, t:t + 1], None, ALU.is_equal)
                        last.then_inc(pick_ready, 1)

                    dve.wait_ge(gate_ready, 1)
                    first = dve.value_load(etab[0:1, 0:1], min_val=0, max_val=NEXP - 1)
                    select(0, first)
                    dve.wait_ge(gb_evac, NEXP)

                    def low(n, j, w):
                        u = 2 * j + w
                        dve.wait_ge(w_high, n * U + (w0 + 2 * order(j) + w + 1))
                        size = KD * P if j < FB else (FLO if w == 0 else FB - FLO) * P
                        c0 = w * (KD * P if j < FB else FLO * P)
                        V.tensor_tensor(wE[u % NWB][:, 1, 0:size], slots[:, j % NSLOT, c0:c0 + size],
                                        wE[u % NWB][:, 0, 0:size].bitcast(FP), ALU.subtract).then_inc(w_split, 1)

                    for j, w in ((1, 0), (1, 1), (0, 0), (0, 1)):
                        low(0, j, w)
                    with dve.Fori(0, passes) as it:
                        ch.enter(it, 0, 2)
                        expert = dve.value_load(etab[0:1, ds(it, 1)], min_val=0, max_val=NEXP - 1)
                        after = dve.value_load(etab[0:1, ds(it + 1, 1)], min_val=0, max_val=NEXP - 1)

                        def gate_sum(f):
                            dve.wait_ge(g_half, it * FB + (f + 1))
                            V.tensor_tensor(gsum[f % 2], ps[:, f % 2, 0:CAP], gsum[f % 2], ALU.add).then_inc(gsum_ready, 1)

                        def hidden(f):
                            dve.wait_ge(u_half, it * FB + (f + 1))
                            V.tensor_tensor(usum, ps[:, 2 + f % 2, 0:CAP], usum, ALU.add).then_inc(usum_ready, 1)
                            dve.wait_ge(usum_ready, it * FB + (f + 1))
                            dve.wait_ge(e_gated, it * FB + (f + 1))
                            if f >= 2:
                                dve.wait_ge(hid_ready, it * FB + (2 * FB + f - 1))
                            V.tensor_tensor(hide[f % 2], usum, sge[f % 2], ALU.mult).then_inc(hid_ready32, 1)

                        def y_sum(d):
                            dve.wait_ge(y_half, it * KD + (d + 1))
                            V.tensor_tensor(yT[:, d % 2, :], ps[:, d % 2, 0:CAP], yT[:, d % 2, :], ALU.add).then_inc(yc_ready, 1)

                        def y_low(d):
                            dve.wait_ge(y_high, it * KD + (d + 1))
                            V.tensor_tensor(yR[:, d % 2, 1, :, :], ps[0:CH, 2 + d % 2, 0:2 * P].rearrange("p (c n) -> p c n", c=2),
                                            yR[:, d % 2, 0, :, :].bitcast(FP), ALU.subtract).then_inc(y_split, 1)

                        def add_out(d):
                            dve.wait_ge(sc_ready, it * KD + (d + 1))
                            dve.wait_ge(x_upd, it * KD + (xu(L, "out") + d))
                            residual(2 + d % 2, d, M_G2)

                        for b in range(FB + KD):
                            n, j = ahead(it, b)
                            if b < FB:
                                gate_sum(b)
                            low(n, j, 0)
                            if b < FB:
                                hidden(b)
                            else:
                                y_sum(b - FB)
                            low(n, j, 1)
                            if b == 0:
                                ch.link(V.tensor_scalar(jcol, iota[:, CAP:CAP + 2], cpass[:, ds(it, 1)], None, ALU.subtract))
                                for c in range(2):
                                    last = V.tensor_scalar(pickT[:, c, :], rbc[0:CH, ds(expert, 1), :].rearrange("p e n -> p (e n)"),
                                                           jcol[0:CH, c:c + 1], None, ALU.is_equal)
                                last.then_inc(pickT_ready, 1)
                            if b == 1:
                                dve.wait_ge(gc_ready, it + 1)
                                select(it + 1, after)
                            if b > FB:
                                y_low(b - FB - 1)
                            if b > FB + 1:
                                add_out(b - FB - 2)
                        add_out(KD - 2)
                        y_low(KD - 1)
                        add_out(KD - 1)
                    continue
                with dve.Fori(0, HALVES) as it:
                    n0 = fexp_base[L]
                    units = 2 * (FB + KD)
                    nb = FB + KD
                    ch.enter(it, 0, 2 * FB)

                    def low(j, w):
                        dve.wait_ge(w_high, it * units + (n0 * units + 2 * j + w + 1))
                        n = KD * P if j < FB else (FLO if w == 0 else FB - FLO) * P
                        c0 = w * (KD * P if j < FB else FLO * P)
                        V.tensor_tensor(wR[:, w, 1, 0:n], slots[:, j % NSLOT, c0:c0 + n], wR[:, w, 0, 0:n].bitcast(FP),
                                        ALU.subtract).then_inc(w_split, 1)

                    def hidden(f):
                        dve.wait_ge(sg_ready, it * FB + (n0 * FB + f + 1))
                        dve.wait_ge(unit_done[1], it * nb + (n0 * nb + f + 1))
                        ch.link(V.tensor_tensor(halves(hidf), pair(2 * (f % 2) + 1), halves(sg[f % 2]), ALU.mult))
                        ch.link(V.tensor_copy(hidR[:, 0, f, :], hidf))
                        V.tensor_tensor(hidR[:, 1, f, :], hidf, hidR[:, 0, f, :].bitcast(FP), ALU.subtract)\
                            .then_inc(hid_ready, 1)
                        dve.wait_ge(hid_ready, it * FB + (n0 * FB + f + 1))

                    for j in range(FB + KD):
                        low(j, 0)
                        low(j, 1)
                        if 1 <= j <= FB:
                            hidden(j - 1)
                        d = j - FB - 1
                        if d >= 0:
                            dve.wait_ge(unit_done[1], it * nb + (n0 * nb + FB + d + 1))
                            dve.wait_ge(x_upd, it * KD + (xu(L, "out") + d))
                            residual((d + 2) % 4, d, M_G2)
                    dve.wait_ge(unit_done[1], it * nb + (n0 * nb + FB + KD))
                    dve.wait_ge(x_upd, it * KD + (xu(L, "out") + KD - 1))
                    residual((KD + 1) % 4, KD - 1, M_G2)
                ch.leave(HALVES)
            dve.wait_ge(x_upd, passes * KD + xu(DEPTH - 1, "out"))
            ch.after_loop(passes, 2)
            stats(2 * DEPTH)


INPUTS = ["x_prompt", "x_sample", "cache_a_kvi", "cache_b_kv", "cache_b_logf", "state_c_pool", "c_prompt", "c_sample",
          "ada_w", "ada_b", "norm_mix_g", "w_in", "b_forget", "pool_w", "pool_scale", "w_br_a", "w_br_b", "w_br_c",
          "w_out", "norm_ffn_g", "ffn_w_gate", "ffn_w_up", "ffn_w_down", "moe_router_w", "moe_router_b",
          "moe_w_gate", "moe_w_up", "moe_w_down", "final_norm_g"]
OUTPUTS = [("y_prompt", (1, SEQ, D)), ("y_sample", (1, DEC, D)),
           ("a_kvi_p", (DEPTH, 1, SEQ, 3, HD)), ("b_kv_p", (DEPTH, 1, SEQ, 2, BH, HD)),
           ("logf_p", (DEPTH, 1, SEQ, BH)), ("pool_p", (DEPTH, 1, HIST, PW)),
           ("a_kvi_s", (DEPTH, 1, DEC, 3, HD)), ("b_kv_s", (DEPTH, 1, DEC, 2, BH, HD)),
           ("logf_s", (DEPTH, 1, DEC, BH)), ("pool_s", (DEPTH, 1, HIST, PW))]


def constants():
    ident = np.eye(P, dtype=np.float32)
    tri = np.triu(np.ones((P, P), np.float32))
    half = HD // 2
    inv = (np.float32(10000.0) ** (-np.arange(half, dtype=np.float32) / np.float32(half))).astype(np.float32)
    pos = np.zeros((P, TILES), np.float32)
    for t in range(SAMPLE):
        pos[:, t] = t * P + np.arange(P)
    pos[0:DEC, SAMPLE] = PAST + np.arange(DEC)
    ang = (pos[:, :, None] * inv[None, None, :]).astype(np.float32)
    rope = np.stack([np.cos(ang), np.sin(ang)], axis=2).astype(np.float32).reshape(P, TILES * HD)
    pool = np.zeros((P, 4, 512), np.float32)
    s, t = np.arange(P)[:, None], np.arange(P)[None, :]
    for g, w in enumerate((2, 4, 8, 16)):
        c = slice(g * P, (g + 1) * P)
        here = ((t - s >= 0) & (t - s < w)).astype(np.float32)
        pool[:, 0, c] = here / w - ident
        pool[:, 1, c] = here / np.minimum(t + 1, w) - ident
        pool[:, 2, c] = ((t + P - s) < w).astype(np.float32) / w
        pool[0:DEC, 3, g * DEC:(g + 1) * DEC] = (here / w - ident)[0:DEC, 0:DEC]
        hs, ht = np.arange(HIST)[:, None], np.arange(DEC)[None, :]
        pool[0:HIST, 3, P + g * DEC:P + (g + 1) * DEC] = ((ht + HIST - hs) < w).astype(np.float32) / w
    iota = np.concatenate([np.broadcast_to(np.arange(CAP), (P, CAP)), np.arange(P)[:, None], np.arange(P)[:, None] + CH],
                          axis=1).astype(np.float32)
    return {"c_iota": iota, "c_ident": ident, "c_tri": tri, "c_rope": rope, "c_pool": pool}


def kernel(**inputs):
    import concourse.bacc as bacc
    from concourse.bass_utils import run_bass_kernel_spmd

    nc = bacc.Bacc("TRN2", target_bir_lowering=False, num_devices=1)
    arrays, t_in, t_out = {}, {}, {}
    consts = constants()
    for name in INPUTS + list(consts):
        a = np.ascontiguousarray(consts[name] if name in consts else inputs[name])
        arrays["in_" + name] = a
        t_in[name] = nc.dram_tensor("in_" + name, a.shape, FP, kind="ExternalInput").ap()
    for name, shape in OUTPUTS:
        t_out[name] = nc.dram_tensor("out_" + name, shape, FP, kind="ExternalOutput").ap()
    encoder_step(nc, t_in, t_out)
    r = run_bass_kernel_spmd(nc, [arrays], core_ids=[0])
    return tuple(r.results[0]["out_" + name] for name, _ in OUTPUTS)
```
